# Optimizing a Trainium2 kernel written in Bass

```python
import math
import jax, jax.numpy as jnp
from jax import lax
import numpy as np

D_MODEL = 1024
BATCH = 1
SEQ = 512
DEPTH = 2

MEM_LEN = 256
N_EVEN = (DEPTH + 1) // 2
N_ODD = DEPTH // 2
MIX_WIDTH = D_MODEL
EPS = 1e-6
Q_BLOCK = 128

HGRN_DIM = 128
HGRN_WIDTH = MIX_WIDTH // 2
HGRN_HEADS = HGRN_WIDTH // HGRN_DIM
HGRN_CHUNK = 64

DIFF_WIDTH = MIX_WIDTH - HGRN_WIDTH
DIFF_HEADS = 4
DIFF_V_DIM = DIFF_WIDTH // DIFF_HEADS
DIFF_QK_DIM = DIFF_V_DIM // 2

FOX_WIDTH = MIX_WIDTH // 2
FOX_HEADS = 8
FOX_DIM = FOX_WIDTH // FOX_HEADS

CONV_CH = MIX_WIDTH - FOX_WIDTH
CONV_WIDTH = 31

XATTN_HEADS = 4
XATTN_DIM = D_MODEL // XATTN_HEADS

D_FF = 2816

EVEN_IN = 4 * HGRN_WIDTH + 3 * DIFF_WIDTH
EVEN_SPLITS = [HGRN_WIDTH, 2 * HGRN_WIDTH, 3 * HGRN_WIDTH, 4 * HGRN_WIDTH,
               4 * HGRN_WIDTH + DIFF_WIDTH, 4 * HGRN_WIDTH + 2 * DIFF_WIDTH]
ODD_IN = 3 * FOX_WIDTH + FOX_HEADS + 2 * CONV_CH
ODD_SPLITS = [FOX_WIDTH, 2 * FOX_WIDTH, 3 * FOX_WIDTH, 3 * FOX_WIDTH + FOX_HEADS,
              3 * FOX_WIDTH + FOX_HEADS + CONV_CH]

kernel_name = "hybrid_hgrn2_diffattn_fox_conformer_trunk"

def rms_norm(x, g):
    xf = x.astype(jnp.float32)
    y = xf * lax.rsqrt(jnp.mean(xf * xf, axis=-1, keepdims=True) + EPS)
    return (y * g.astype(jnp.float32)).astype(x.dtype)

def layer_norm(x, g, b):
    xf = x.astype(jnp.float32)
    mu = jnp.mean(xf, axis=-1, keepdims=True)
    var = jnp.mean(jnp.square(xf - mu), axis=-1, keepdims=True)
    y = (xf - mu) * lax.rsqrt(var + EPS) * g.astype(jnp.float32) + b.astype(jnp.float32)
    return y.astype(x.dtype)

def swiglu(x, w_gate, w_up, w_down):
    return (jax.nn.silu(x @ w_gate) * (x @ w_up)) @ w_down

def to_heads(t, n_heads):
    b, s, _ = t.shape
    return t.reshape(b, s, n_heads, -1).transpose(0, 2, 1, 3)

def from_heads(t):
    b, n, s, d = t.shape
    return t.transpose(0, 2, 1, 3).reshape(b, s, n * d)

def alibi_slopes(n):
    return jnp.asarray(2.0 ** (-8.0 * np.arange(1, n + 1) / n), jnp.float32)

def causal_block_attention(q, k, v, bias_fn):
    seq = q.shape[2]
    scale = q.shape[-1] ** -0.5
    outs = []
    for blk in range(seq // Q_BLOCK):
        q0, q1 = blk * Q_BLOCK, (blk + 1) * Q_BLOCK
        logits = jnp.einsum('bgtd,bgsd->bgts', q[:, :, q0:q1], k[:, :, :q1]).astype(jnp.float32) * scale
        logits = logits + bias_fn(q0, q1)
        t_pos = jnp.arange(q0, q1)[:, None]
        s_pos = jnp.arange(q1)[None, :]
        logits = jnp.where(s_pos <= t_pos, logits, -jnp.inf)
        p = jax.nn.softmax(logits, axis=-1).astype(v.dtype)
        outs.append(jnp.einsum('bgts,bgsv->bgtv', p, v[:, :, :q1]))
    return jnp.concatenate(outs, axis=2)

def hgrn2_mixer(q, f_logit, inp, gate, lb, norm_g):
    f32 = jnp.float32
    bsz, seq, _ = q.shape
    lbh = jnp.maximum(lb.astype(f32), 0.0).reshape(HGRN_HEADS, 1, HGRN_DIM)
    z = to_heads(f_logit.astype(f32), HGRN_HEADS)
    logf = jnp.logaddexp(jnp.log(lbh), jnp.log1p(-lbh) + jax.nn.log_sigmoid(z))
    k = -jnp.expm1(logf)
    qh = to_heads(q.astype(f32), HGRN_HEADS)
    vh = to_heads(inp.astype(f32), HGRN_HEADS)
    nc = seq // HGRN_CHUNK

    def chunks(t):
        return t.reshape(bsz, HGRN_HEADS, nc, HGRN_CHUNK, -1).transpose(2, 0, 1, 3, 4)

    causal = jnp.tril(jnp.ones((HGRN_CHUNK, HGRN_CHUNK), bool))[:, :, None]

    def step(state, xs):
        qc, kc, vc, lfc = xs
        b = jnp.cumsum(lfc, axis=-2)
        decay = jnp.exp(jnp.where(causal, b[..., :, None, :] - b[..., None, :, :], -jnp.inf))
        scores = jnp.einsum('bhtd,bhsd,bhtsd->bhts', qc, kc, decay)
        o = (jnp.einsum('bhts,bhsv->bhtv', scores, vc)
             + jnp.einsum('bhtd,bhdv->bhtv', qc * jnp.exp(b), state))
        b_end = b[..., -1:, :]
        state = (jnp.exp(b_end)[..., 0, :, None] * state
                 + jnp.einsum('bhsd,bhsv->bhdv', kc * jnp.exp(b_end - b), vc))
        return state, o

    s0 = jnp.zeros((bsz, HGRN_HEADS, HGRN_DIM, HGRN_DIM), f32)
    _, o = lax.scan(step, s0, (chunks(qh), chunks(k), chunks(vh), chunks(logf)))
    o = o.transpose(1, 0, 3, 2, 4).reshape(bsz, seq, HGRN_HEADS, HGRN_DIM)
    o = rms_norm(o, norm_g.reshape(HGRN_HEADS, HGRN_DIM))
    o = o.reshape(bsz, seq, HGRN_WIDTH) * jax.nn.silu(gate.astype(f32))
    return o.astype(q.dtype)

def diff_attention(q, k, v, lam_p, norm_g, layer_idx):
    f32 = jnp.float32
    bsz, seq, _ = q.shape

    def split_maps(t):
        return t.reshape(bsz, seq, 2 * DIFF_HEADS, DIFF_QK_DIM).transpose(0, 2, 1, 3)

    vh = jnp.repeat(to_heads(v, DIFF_HEADS), 2, axis=1)
    slopes = jnp.repeat(alibi_slopes(DIFF_HEADS), 2)

    def alibi(q0, q1):
        t_pos = jnp.arange(q0, q1, dtype=f32)[:, None]
        s_pos = jnp.arange(q1, dtype=f32)[None, :]
        return -slopes[None, :, None, None] * (t_pos - s_pos)

    o = causal_block_attention(split_maps(q), split_maps(k), vh, alibi)
    o = o.reshape(bsz, DIFF_HEADS, 2, seq, DIFF_V_DIM).astype(f32)
    lam_init = 0.8 - 0.6 * math.exp(-0.3 * layer_idx)
    lp = lam_p.astype(f32)
    lam = jnp.exp(jnp.sum(lp[0] * lp[1])) - jnp.exp(jnp.sum(lp[2] * lp[3])) + lam_init
    o = o[:, :, 0] - lam * o[:, :, 1]
    o = rms_norm(o.transpose(0, 2, 1, 3), norm_g.reshape(DIFF_HEADS, DIFF_V_DIM)) * (1.0 - lam_init)
    return o.reshape(bsz, seq, DIFF_WIDTH).astype(q.dtype)

def even_mixer(hn, w_in, w_out, lb, hgrn_g, lam_p, diff_g, layer_idx):
    proj = hn @ w_in
    a_q, a_f, a_i, a_g, b_q, b_k, b_v = jnp.split(proj, EVEN_SPLITS, axis=-1)
    ya = hgrn2_mixer(a_q, a_f, a_i, a_g, lb, hgrn_g)
    yb = diff_attention(b_q, b_k, b_v, lam_p, diff_g, layer_idx)
    return jnp.concatenate([ya, yb], axis=-1) @ w_out

def odd_mixer(hn, w_in, w_out, f_bias, conv_w, conv_b, ln_g, ln_b):
    f32 = jnp.float32
    proj = hn @ w_in
    c_q, c_k, c_v, c_f, d_a, d_g = jnp.split(proj, ODD_SPLITS, axis=-1)
    logf = jax.nn.log_sigmoid(c_f.astype(f32) + f_bias.astype(f32))
    cum_f = jnp.cumsum(logf, axis=1).transpose(0, 2, 1)

    def forget_bias(q0, q1):
        return cum_f[:, :, q0:q1, None] - cum_f[:, :, None, :q1]

    yc = from_heads(causal_block_attention(to_heads(c_q, FOX_HEADS), to_heads(c_k, FOX_HEADS),
                                           to_heads(c_v, FOX_HEADS), forget_bias))
    u = d_a * jax.nn.sigmoid(d_g)
    conv = lax.conv_general_dilated(u, conv_w[:, None, :].astype(u.dtype), window_strides=(1,),
                                    padding=[(CONV_WIDTH - 1, 0)],
                                    dimension_numbers=('NWC', 'WIO', 'NWC'),
                                    feature_group_count=CONV_CH) + conv_b.astype(u.dtype)
    yd = jax.nn.silu(layer_norm(conv, ln_g, ln_b))
    return jnp.concatenate([yc.astype(hn.dtype), yd.astype(hn.dtype)], axis=-1) @ w_out

def cross_attention(hn, mem, mem_g, w_q, w_kv, w_o):
    q = to_heads(hn @ w_q, XATTN_HEADS)
    k, v = jnp.split(rms_norm(mem, mem_g) @ w_kv, 2, axis=-1)
    kh, vh = to_heads(k, XATTN_HEADS), to_heads(v, XATTN_HEADS)
    logits = jnp.einsum('bhtd,bhsd->bhts', q, kh).astype(jnp.float32) * (XATTN_DIM ** -0.5)
    p = jax.nn.softmax(logits, axis=-1).astype(vh.dtype)
    return from_heads(jnp.einsum('bhts,bhsv->bhtv', p, vh)) @ w_o

def setup_inputs(seed: int = 0) -> dict:
    key = jax.random.key(seed)
    ks = jax.random.split(key, 32)
    f32 = jnp.float32

    def nrm(k, shape, scale):
        return scale * jax.random.normal(k, shape, f32)

    def gain(k, shape):
        return 1.0 + 0.02 * jax.random.normal(k, shape, f32)

    return {
        "x": nrm(ks[0], (BATCH, SEQ, D_MODEL), 1.0),
        "mem": nrm(ks[1], (BATCH, MEM_LEN, D_MODEL), 1.0),
        "ffn_norm_pre": gain(ks[2], (DEPTH, 2, D_MODEL)),
        "ffn_norm_post": gain(ks[3], (DEPTH, 2, D_MODEL)),
        "ffn_w_gate": nrm(ks[4], (DEPTH, 2, D_MODEL, D_FF), D_MODEL ** -0.5),
        "ffn_w_up": nrm(ks[5], (DEPTH, 2, D_MODEL, D_FF), D_MODEL ** -0.5),
        "ffn_w_down": nrm(ks[6], (DEPTH, 2, D_FF, D_MODEL), D_FF ** -0.5),
        "mix_norm_pre": gain(ks[7], (DEPTH, D_MODEL)),
        "mix_norm_post": gain(ks[8], (DEPTH, D_MODEL)),
        "even_w_in": nrm(ks[9], (N_EVEN, D_MODEL, EVEN_IN), D_MODEL ** -0.5),
        "even_w_out": nrm(ks[10], (N_EVEN, MIX_WIDTH, D_MODEL), MIX_WIDTH ** -0.5),
        "hgrn_lb_logits": nrm(ks[11], (N_EVEN, HGRN_WIDTH), 0.5),
        "hgrn_norm_g": gain(ks[12], (N_EVEN, HGRN_WIDTH)),
        "diff_lambda": nrm(ks[13], (N_EVEN, 4, DIFF_QK_DIM), 0.1),
        "diff_norm_g": gain(ks[14], (N_EVEN, DIFF_WIDTH)),
        "odd_w_in": nrm(ks[15], (N_ODD, D_MODEL, ODD_IN), D_MODEL ** -0.5),
        "odd_w_out": nrm(ks[16], (N_ODD, MIX_WIDTH, D_MODEL), MIX_WIDTH ** -0.5),
        "fox_f_bias": 2.0 + nrm(ks[17], (N_ODD, FOX_HEADS), 0.1),
        "conv_w": nrm(ks[18], (N_ODD, CONV_WIDTH, CONV_CH), CONV_WIDTH ** -0.5),
        "conv_b": nrm(ks[19], (N_ODD, CONV_CH), 0.02),
        "conv_ln_g": gain(ks[20], (N_ODD, CONV_CH)),
        "conv_ln_b": nrm(ks[21], (N_ODD, CONV_CH), 0.02),
        "xattn_norm_pre": gain(ks[22], (DEPTH, D_MODEL)),
        "xattn_norm_post": gain(ks[23], (DEPTH, D_MODEL)),
        "mem_norm_g": gain(ks[24], (DEPTH, D_MODEL)),
        "xattn_w_q": nrm(ks[25], (DEPTH, D_MODEL, D_MODEL), D_MODEL ** -0.5),
        "xattn_w_kv": nrm(ks[26], (DEPTH, D_MODEL, 2 * D_MODEL), D_MODEL ** -0.5),
        "xattn_w_o": nrm(ks[27], (DEPTH, D_MODEL, D_MODEL), D_MODEL ** -0.5),
    }

def reference(x, mem, ffn_norm_pre, ffn_norm_post, ffn_w_gate, ffn_w_up, ffn_w_down,
              mix_norm_pre, mix_norm_post,
              even_w_in, even_w_out, hgrn_lb_logits, hgrn_norm_g, diff_lambda, diff_norm_g,
              odd_w_in, odd_w_out, fox_f_bias, conv_w, conv_b, conv_ln_g, conv_ln_b,
              xattn_norm_pre, xattn_norm_post, mem_norm_g, xattn_w_q, xattn_w_kv, xattn_w_o):
    lb_all = jnp.cumsum(jax.nn.softmax(hgrn_lb_logits.astype(jnp.float32), axis=0), axis=0)
    lb_all = lb_all - lb_all[0]

    def half_ffn(h, l, j):
        y = swiglu(rms_norm(h, ffn_norm_pre[l, j]), ffn_w_gate[l, j], ffn_w_up[l, j], ffn_w_down[l, j])
        return h + 0.5 * rms_norm(y, ffn_norm_post[l, j])

    h = x
    for l in range(DEPTH):
        h = half_ffn(h, l, 0)
        hn = rms_norm(h, mix_norm_pre[l])
        if l % 2 == 0:
            e = l // 2
            y = even_mixer(hn, even_w_in[e], even_w_out[e], lb_all[e], hgrn_norm_g[e],
                           diff_lambda[e], diff_norm_g[e], l)
        else:
            o = l // 2
            y = odd_mixer(hn, odd_w_in[o], odd_w_out[o], fox_f_bias[o], conv_w[o], conv_b[o],
                          conv_ln_g[o], conv_ln_b[o])
        h = h + rms_norm(y, mix_norm_post[l])
        y = cross_attention(rms_norm(h, xattn_norm_pre[l]), mem, mem_norm_g[l],
                            xattn_w_q[l], xattn_w_kv[l], xattn_w_o[l])
        h = h + rms_norm(y, xattn_norm_post[l])
        h = half_ffn(h, l, 1)
    return h


_drawn_inputs = setup_inputs


def setup_inputs(seed=0):
    import zlib

    import numpy as np

    out = dict(_drawn_inputs(seed))
    spreads = {}
    factors = {'ffn_norm_post': 3.301,
     'mix_norm_post': 3.229,
     'hgrn_norm_g': 6.443,
     'diff_lambda': 5.752,
     'diff_norm_g': 4.855,
     'fox_f_bias': 64.0,
     'conv_b': 4.166,
     'conv_ln_g': 32.907,
     'conv_ln_b': 32.947,
     'xattn_norm_pre': 3.721,
     'xattn_norm_post': 3.747}
    for name, (base, spread) in spreads.items():
        noise = np.random.default_rng([zlib.crc32(name.encode()), seed]).standard_normal(out[name].shape)
        drawn = base * np.exp(spread * noise) if base else spread * noise
        out[name] = __import__('jax').numpy.asarray(drawn.astype(out[name].dtype))
    for name, factor in factors.items():
        out[name] = (out[name] * factor).astype(out[name].dtype)
    return out
```

```python
import math
from collections import Counter

import numpy as np
import concourse.bass as bass
from concourse import mybir

D = 1024
SEQ = 512
MEM = 256
FF = 2816
DEPTH = 2
assert (DEPTH + 1) // 2 == 1
P = 128
KT = D // P
TT = SEQ // P
MT = MEM // P
EPS = 1e-6
GC = 512
PK = 2
RAW_SLOTS = 4
SPLIT_SLOTS = 4
LOOKAHEAD = 3
HEAD = 128
FOX_HEADS = 8
CONV_W = 31
CONV_T = 4
FF_PASSES = ((0, 6), (6, 5))
NEG = -1e30

FFN_PRE, FFN_POST, MIX_PRE, MIX_POST, X_PRE, X_POST = 0, 32, 64, 80, 96, 112
MEM_G, HGRN_G, DIFF_G, CONV_B, LN_G, LN_B, CONV_TAPS = 128, 144, 148, 152, 156, 160, 164
N_VEC = CONV_TAPS + CONV_W * CONV_T


def stages():
    out = []

    def ffn(l, j):
        for n, (g0, ng) in enumerate(FF_PASSES):
            out.append(("gate_up", l, (j, n), ng, KT // PK))
            out.append(("down", l, (j, n), 2, ng))
    for l in range(DEPTH):
        ffn(l, 0)
        out.append(("even_in", l, None, 7, 4) if l % 2 == 0 else ("odd_in", l, None, 6, 4))
        out.append(("mix_out", l, None, 2, 4))
        out.append(("kv", l, None, 4, 4))
        out.append(("xq", l, None, 2, 4))
        out.append(("xo", l, None, 2, 4))
        ffn(l, 1)
    return out


EVEN_COLS = [("a_f", 512), ("a_q", 0), ("a_g", 1536), ("a_i", 1024), ("b_q", 2048), ("b_k", 2560), ("b_v", 3072)]
ODD_COLS = [("d_a", 1544), ("d_g", 2056), ("c_f", 1536), ("c_q", 0), ("c_k", 512), ("c_v", 1024)]
TOKEN_MAJOR = ("a_i", "b_v", "c_v")

DIFF_STEPS = [(h, b) for h in range(4) for b in range(TT)]
FOX_STEPS = [(h, b) for h in range(4) for b in range(TT)]
X_STEPS = [(h, b) for h in range(2) for b in range(TT)]
LEVELS = [64, 32, 16, 8, 4, 2, 1]
CROSS = [(1, 0), (2, 1), (3, 2), (2, 0), (3, 1), (3, 0)]


def build(nc, A, out):
    f32, f32r, bf16, i8 = mybir.dt.float32, mybir.dt.float32r, mybir.dt.bfloat16, mybir.dt.int8
    ALU, ACT, AX = mybir.AluOpType, mybir.ActivationFunctionType, mybir.AxisListType
    MUL, ADD, SUB = ALU.mult, ALU.add, ALU.subtract
    LAM_INIT = 0.8 - 0.6 * math.exp(-0.3 * 0)

    FLOAT = 4
    top = [(int(nc.sbuf_base) + 511) // 512 * 512]

    def place(name, shape, dt=f32, at=None, size=FLOAT):
        n = (int(np.prod(shape[1:])) * size + 31) // 32 * 32
        if at is None:
            at = top[0]
            top[0] += n
        assert at + n <= nc.sbuf_usable_end, (name, at + n - nc.sbuf_usable_end)
        return nc.alloc_sbuf_tensor_at(name, shape, dt, offset=at)

    NB = 4 * SEQ
    h = place("h", [P, KT, SEQ])
    y_at = top[0]
    y = place("y", [P, KT, SEQ])
    x_at = top[0]
    xhi = place("xhi", [P, KT, SEQ], f32r)
    xlo = place("xlo", [P, KT, SEQ], f32r)
    raw = place("raw", [P, RAW_SLOTS, PK, GC])
    whi = place("whi", [P, SPLIT_SLOTS, PK, GC], f32r)
    wlo = place("wlo", [P, SPLIT_SLOTS, PK, GC], f32r)
    memT = place("memT", [P, KT, MEM])
    ring = place("ring", [P, 4, SEQ])
    rsb = place("rsb", [P, SEQ])
    diag = place("diag", [P, TT, P])
    ident = place("ident", [P, P])
    ones = place("ones", [P, P])
    vec = place("vec", [P, N_VEC])
    neg_half = place("neg_half", [P, 16])
    var = place("var", [P, 16])
    rstd = place("rstd", [P, 16])
    rstd_in = place("rstd_in", [P, TT])
    negmax = place("negmax", [P, 2, 2])
    rowsum = place("rowsum", [P, 2, 2])
    recip = place("recip", [P, 2, 2])
    lam = place("lam", [P, 8])
    tile_decay = place("tile_decay", [P, 4, TT])
    fbias = place("fbias", [FOX_HEADS, 8])
    head_sel = place("head_sel", [FOX_HEADS, FOX_HEADS, P], f32r)
    ident_bf = place("ident_bf", [P, P], bf16, size=2)
    causal_neg = place("causal_neg", [P, P], bf16, size=2)
    level_mask = place("level_mask", [P, len(LEVELS) + 1, P], i8, size=1)
    w_at = top[0]
    at = lambda n: w_at + n * FLOAT
    mem_in = place("mem_in", [P, MT, D], f32, at(0))
    mem_sq = place("mem_sq", [P, D], f32, at(2048))
    rows = place("rows", [P, 3, P], f32, at(3072))
    lam_in = place("lam_in", [P, 4, 64], f32, at(3456))
    level_f = place("level_f", [P, P], f32, at(3712))
    head_sel_f = place("head_sel_f", [FOX_HEADS, FOX_HEADS, P], f32, at(3840))
    position = place("position", [4, SEQ], f32, at(4864))
    slope = place("slope", [4, 8], f32, at(5376))
    x_in = place("x_in", [P, TT, D], f32, y_at)
    mid_hi = place("mid_hi", [P, 12, SEQ], f32r, at(0))
    mid_lo = place("mid_lo", [P, 12, SEQ], f32r, at(6144))
    gate = place("gate", [P, 2, SEQ], f32, at(12288))
    up = place("up", [P, 2, SEQ], f32, at(13312))
    a_b = place("a_b", [P, 4, SEQ], f32, at(0))
    a_k = place("a_k", [P, 4, SEQ], f32, at(NB))
    a_q = place("a_q", [P, 4, SEQ], f32, at(2 * NB))
    a_g = place("a_g", [P, 4, SEQ], f32, at(3 * NB))
    a_v = place("a_v", [P, TT, SEQ], f32, at(4 * NB))
    b_q = place("b_q", [P, 4, SEQ], f32, at(5 * NB))
    b_k = place("b_k", [P, 4, SEQ], f32, at(6 * NB))
    b_v = place("b_v", [P, TT, SEQ], f32, at(7 * NB))
    alibi = place("alibi", [4, SEQ], f32r, at(8 * NB))
    soft = place("soft", [P, 4, SEQ], f32, y_at)
    logf = place("logf", [P, 4, SEQ], f32, y_at + NB * FLOAT)
    cross = place("cross", [P, 24, P], f32, y_at)
    lv = place("lv", [P, 2, 4 * SEQ], f32, x_at)
    scoresT = place("scoresT", [P, 16, P], f32, x_at + 2 * NB * FLOAT)
    kd2 = place("kd2", [P, 4, 2, P], f32, x_at + 3 * NB * FLOAT)
    kd3 = place("kd3", [P, 4, P], f32, x_at + (3 * NB + 1024) * FLOAT)
    probs = place("probs", [P, 2, 2, SEQ], f32, x_at)
    probsT = place("probsT", [P, 2 * TT, P], f32, x_at + NB * FLOAT)
    U0 = CONV_W - 1
    UN = CONV_T * (U0 + SEQ)
    u = place("u", [P, CONV_T, U0 + SEQ], f32, at(0))
    sg = place("sg", [P, CONV_T, SEQ], f32, at(UN))
    conv = place("conv", [P, CONV_T, SEQ], f32, at(UN + NB))
    c_q = place("c_q", [P, 4, SEQ], f32, at(UN + 2 * NB))
    c_k = place("c_k", [P, 4, SEQ], f32, at(UN + 3 * NB))
    c_v = place("c_v", [P, TT, SEQ], f32, at(UN + 4 * NB))
    c_z = place("c_z", [FOX_HEADS, 3, SEQ], f32, at(UN + 5 * NB))
    cum_hi = place("cum_hi", [FOX_HEADS, SEQ], f32r, at(UN + 5 * NB + 1536))
    cum_lo = place("cum_lo", [FOX_HEADS, SEQ], f32r, at(UN + 5 * NB + 2048))
    m_hi = place("m_hi", [P, KT, MEM], f32r, at(0))
    m_lo = place("m_lo", [P, KT, MEM], f32r, at(NB))
    x_k = place("x_k", [P, KT, MEM], f32, at(2 * NB))
    x_v = place("x_v", [P, MT, D], f32, at(3 * NB))
    x_q = place("x_q", [P, KT, SEQ], f32, at(4 * NB))

    PS = nc.alloc_psum_tensor("ps", [P, 8, 512], f32)
    flat = lambda t: t.rearrange("p a b -> p (a b)")
    blocks_of = lambda b0, b1: PS[:, b0:b1, :].rearrange("p a (b j) -> p (a b) j", j=P)

    def sem(name):
        return nc.alloc_semaphore(name)

    x_loaded, mem_loaded, rows_loaded, small_loaded, stored = map(sem, (
        "x_loaded", "mem_loaded", "rows_loaded", "small_loaded", "stored"))
    raw_full = [sem(f"raw_full{i}") for i in range(RAW_SLOTS)]
    hi_made, lo_made, pieces_used = map(sem, ("hi_made", "lo_made", "pieces_used"))
    bank_free = [sem("even_banks_free"), sem("odd_banks_free")]
    vector_step, scalar_step, pool_step = map(sem, ("vector_step", "scalar_step", "pool_step"))
    consts_ready, tables_ready, vec_ready, mem_squared, mem_scaled, memT_ready, lam_exp = map(sem, (
        "consts_ready", "tables_ready", "vec_ready", "mem_squared", "mem_scaled", "memT_ready", "lam_exp"))
    transposed = sem("transposed")
    h_ready, xhi_ready, xlo_ready, m_hi_ready, m_lo_ready = map(sem, (
        "h_ready", "xhi_ready", "xlo_ready", "m_hi_ready", "m_lo_ready"))
    h_squared, h_summed, ring_squared, ring_summed = map(sem, (
        "h_squared", "h_summed", "ring_squared", "ring_summed"))
    var_ready, rstd_ready, diag_ready, spread_ready, spread_used = map(sem, (
        "var_ready", "rstd_ready", "diag_ready", "spread_ready", "spread_used"))
    gate_scaled, up_scaled, gate_silu, product_ready, mid_hi_ready, mid_lo_ready = map(sem, (
        "gate_scaled", "up_scaled", "gate_silu", "product_ready", "mid_hi_ready", "mid_lo_ready"))
    y_ready, proj_ready, v_ready, y_mixed = map(sem, ("y_ready", "proj_ready", "v_ready", "y_mixed"))
    scores_ready, negmax_ready, exp_done, probs_ready = map(sem, (
        "scores_ready", "negmax_ready", "exp_done", "probs_ready"))
    probsT_ready, probsT_copied, o_ready, o_copied = map(sem, (
        "probsT_ready", "probsT_copied", "o_ready", "o_copied"))
    softplus_ready, level_diff, level_exp, level_ready, level_scores, level_merged = map(sem, (
        "softplus_ready", "level_diff", "level_exp", "level_ready", "level_scores", "level_merged"))
    decay_ready, cross_ready, cross_scores, cross_copied, cum_ready, cum_hi_ready, cum_lo_ready = map(sem, (
        "decay_ready", "cross_ready", "cross_scores", "cross_copied", "cum_ready", "cum_hi_ready", "cum_lo_ready"))
    sigmoid_ready, conv_ready, conv_summed, conv_centred, conv_scaled = map(sem, (
        "sigmoid_ready", "conv_ready", "conv_summed", "conv_centred", "conv_scaled"))
    y_silu = sem("y_silu")

    STAGES = stages()
    total_pieces = sum(ng * n for _, _, _, ng, n in STAGES) - 3 * (DEPTH // 2)

    def group_pieces(kind, g, n):
        return 1 if kind == "odd_in" and ODD_COLS[g][0] == "c_f" else n

    def straight_groups(ng):
        return 2 if ng % 2 == 0 else 1

    def column_name(kind, g):
        return {"even_in": EVEN_COLS, "odd_in": ODD_COLS}[kind][g][0] if kind in ("even_in", "odd_in") else ""

    def from_h(kind, arg):
        return kind in ("even_in", "odd_in", "xq") or (kind == "gate_up" and arg[1] == 0)

    def gain_of(kind, l, arg):
        return {"even_in": MIX_PRE, "odd_in": MIX_PRE, "xq": X_PRE}[kind] + l * KT if kind != "gate_up" else \
            FFN_PRE + (2 * l + arg[0]) * KT

    def ends_sublayer(kind, arg):
        return kind in ("mix_out", "xo") or (kind == "down" and arg[1] == 1)

    def post_gain(kind, l, arg):
        return {"mix_out": MIX_POST, "xo": X_POST}[kind] + l * KT if kind != "down" else \
            FFN_POST + (2 * l + arg[0]) * KT

    def diff_block(i):
        return i // TT, i % TT

    class Engine:

        def __init__(self, eng, chain):
            self.eng, self.chain = eng, chain
            self.made, self.seen, self.last = Counter(), Counter(), None
            self.piece = self.group = 0

        def run(self, ins, s=None, n=1):
            s = self.chain if s is None else s
            self.made[s.name] += n
            ins.then_inc(s, n)
            self.last = (s, self.made[s.name])

        def own(self):
            self.eng.wait_ge(*self.last)

        def await_(self, s, n=1):
            self.seen[s.name] += n
            self.eng.wait_ge(s, self.seen[s.name])

        def release_banks(self):
            self.eng.wait_ge(*self.last).then_inc(bank_free[self.group % 2], 1)

        def group_done(self):
            self.eng.wait_ge(pieces_used, self.piece + SPLIT_SLOTS)

    block_ctx = nc.Block()
    block = block_ctx.__enter__()

    @block.sync
    def _(sp):
        sp.dma_start(x_in[:], A["x"][0].rearrange("(t p) d -> p t d", p=P)).then_inc(x_loaded, 16)
        r = 0
        for name in ("ffn_norm_pre", "ffn_norm_post", "mix_norm_pre", "mix_norm_post",
                     "xattn_norm_pre", "xattn_norm_post"):
            src = A[name]
            src = src.rearrange("l j (k p) -> (l j k) p", p=P) if len(src.shape) == 3 else \
                src.rearrange("l (k p) -> (l k) p", p=P)
            sp.dma_start(rows[r:r + src.shape[0], 0, :], src).then_inc(rows_loaded, 16)
            r += src.shape[0]
        r = 0
        for name in ("mem_norm_g", "hgrn_norm_g", "diff_norm_g", "conv_b", "conv_ln_g", "conv_ln_b"):
            src = A[name].rearrange("l (k p) -> (l k) p", p=P)
            sp.dma_start(rows[r:r + src.shape[0], 1, :], src).then_inc(rows_loaded, 16)
            r += src.shape[0]
        sp.dma_start(rows[0:CONV_W * CONV_T, 2, :],
                     A["conv_w"][0].rearrange("w (c p) -> (w c) p", p=P)).then_inc(rows_loaded, 16)
        sp.dma_start(mem_in[:], A["mem"][0].rearrange("(t p) d -> p t d", p=P)).then_inc(mem_loaded, 16)
        sp.dma_start(lam_in[:], A["diff_lambda"].broadcast_to([P, 4, 64])).then_inc(small_loaded, 16)
        with nc.allow_non_contiguous_dma("eight biases, one to a partition"):
            sp.dma_start(fbias[:, 0:1], A["fox_f_bias"].rearrange("o h -> h o")).then_inc(small_loaded, 16)

        def load(base, g, halves):
            slot = base % RAW_SLOTS
            sp.wait_ge(lo_made, base + 1 + 4 * g)
            for dst, src in halves(slot):
                sp.dma_start(dst, src).then_inc(raw_full[slot], 16)

        def two_rows(w, k0, c0):
            def halves(slot):
                for i in range(2):
                    yield raw[:, slot, i, :], w[(k0 + i) * P:(k0 + i + 1) * P, c0:c0 + GC]
            return halves

        def gate_and_up(l, j, kp, c0):
            def halves(slot):
                for i, name in enumerate(("ffn_w_gate", "ffn_w_up")):
                    w = A[name][l, j].rearrange("(k p) n -> p k n", p=P)
                    yield raw[:, slot, :, i * 256:(i + 1) * 256], w[:, 2 * kp:2 * kp + 2, bass.ds(c0, 256)]
            return halves

        def forget_rows(w, c0):
            def halves(slot):
                dst = raw[:, slot].rearrange("p a (b n) -> p (a b) n", n=P)
                src = w.rearrange("(k p) n -> p k n", p=P)
                for i in range(2):
                    yield dst[:, 4 * i:4 * i + 4, :], src[:, 4 * i:4 * i + 4, c0:c0 + P]
            return halves

        piece = 0
        for kind, l, arg, ng, np_ in STAGES:
            if kind == "gate_up":
                j, n = arg
                first = straight_groups(ng)
                g0 = FF_PASSES[n][0]
                for g in range(first):
                    for kp in range(4):
                        load(piece + 4 * g + kp, 0, gate_and_up(l, j, kp, (g0 + g) * 256))
                with sp.Fori(0, (ng - first) // 2) as i:
                    for q in range(2):
                        for kp in range(4):
                            load(piece + 4 * (first + q) + kp, 2 * i,
                                 gate_and_up(l, j, kp, (g0 + first + q) * 256 + i * 512))
                piece += 4 * ng
                continue
            for g in range(ng):
                for kp in range(group_pieces(kind, g, np_)):
                    if kind == "down":
                        j, n = arg
                        src = two_rows(A["ffn_w_down"][l, j], 2 * FF_PASSES[n][0] + 2 * kp, g * GC)
                    elif kind == "even_in":
                        src = two_rows(A["even_w_in"][l // 2], 2 * kp, EVEN_COLS[g][1])
                    elif kind == "odd_in":
                        name, c0 = ODD_COLS[g]
                        w = A["odd_w_in"][l // 2]
                        src = forget_rows(w, c0) if name == "c_f" else two_rows(w, 2 * kp, c0)
                    else:
                        w = {"mix_out": A["even_w_out" if l % 2 == 0 else "odd_w_out"][l // 2],
                             "kv": A["xattn_w_kv"][l], "xq": A["xattn_w_q"][l], "xo": A["xattn_w_o"][l]}[kind]
                        src = two_rows(w, 2 * kp, g * GC)
                    load(piece, 0, src)
                    piece += 1
        assert piece == total_pieces
        for t in range(TT):
            sp.wait_ge(y_mixed, KT + 2 * (t + 1))
            sp.dma_start(out[0, t * P:(t + 1) * P, :], x_in[:, t, :]).then_inc(stored, 16)
        sp.wait_ge(stored, 16 * TT)

    @block.gpsimd
    def _(pool):
        E = Engine(pool, pool_step)
        g = nc.gpsimd

        def on_diagonal(t, pattern):
            E.run(g.memset(t, 0.0))
            E.own()
            E.run(g.affine_select(out=t, in_=t, compare_op=ALU.not_equal, fill=1.0, base=0,
                                  pattern=pattern, channel_multiplier=1))
        E.run(g.memset(ones[:], 1.0))
        E.run(g.memset(neg_half[:], -0.5))
        on_diagonal(ident[:], [[-1, P]])
        E.own()
        pool.wait_ge(*E.last).then_inc(consts_ready, 1)
        on_diagonal(head_sel_f[:], [[-1, FOX_HEADS], [0, P]])
        on_diagonal(ident_bf[:], [[-1, P]])
        E.run(g.iota(position[:], pattern=[[1, SEQ]], base=0, channel_multiplier=0,
                     allow_small_or_imprecise_dtypes=True))
        E.run(g.memset(slope[:], 0.0))
        for n in range(4):
            E.own()
            E.run(g.affine_select(out=slope[:], in_=slope[:], compare_op=ALU.not_equal, base=-n,
                                  fill=8.0 * 2.0 ** (-8.0 * (n + 1) / 4), pattern=[[0, 8]], channel_multiplier=1))
        E.run(g.memset(causal_neg[:], 0.0))
        E.own()
        E.run(g.affine_select(out=causal_neg[:], in_=causal_neg[:], compare_op=ALU.is_ge, fill=NEG, base=0,
                              pattern=[[-1, P]], channel_multiplier=1))
        for n, L in enumerate(LEVELS):
            m = level_f[:].rearrange("p (b r j) -> p b r j", r=2, j=L)
            nb = P // (2 * L)
            E.run(g.memset(level_f[:], 1.0))
            for base, ch, pat in ((0, 1, [[-2 * L, nb], [0, 2], [0, L]]),
                                  (L - 1, -1, [[2 * L, nb], [0, 2], [0, L]]),
                                  (-1, 0, [[0, nb], [1, 2], [0, L]])):
                E.own()
                E.run(g.affine_select(out=m, in_=m, compare_op=ALU.is_ge, fill=0.0, base=base,
                                      pattern=pat, channel_multiplier=ch))
            E.own()
            E.run(g.tensor_copy(level_mask[:, n, :], level_f[:]))
            E.own()
        E.run(g.tensor_copy(level_mask[:, len(LEVELS), :], ident[:]), tables_ready)

        def power(n):
            E.await_(var_ready)
            E.run(g.tensor_tensor(rstd[:, 0:n], var[:, 0:n], neg_half[:, 0:n], ALU.pow), rstd_ready)

        power(MT)
        products = 0
        for kind, l, arg, ng, np_ in STAGES:
            if from_h(kind, arg):
                power(TT)
            if kind == "gate_up":
                def multiply(n):
                    pool.wait_ge(gate_silu, n)
                    pool.wait_ge(up_scaled, n)
                    g.tensor_tensor(up[:], gate[:], up[:], MUL).then_inc(product_ready, 1)
                first = straight_groups(ng)
                for q in range(first):
                    multiply(products + q + 1)
                with pool.Fori(0, (ng - first) // 2) as i:
                    for q in range(2):
                        multiply(products + first + q + 1 + 2 * i)
                products += ng
            elif kind == "even_in":
                power(16)
                power(16)
            elif kind == "odd_in":
                power(TT)
            elif ends_sublayer(kind, arg):
                power(TT)

    @block.scalar
    def _(act):
        E = Engine(act, scalar_step)
        a = nc.scalar.activation

        def split(base, g=0):
            slot = base % RAW_SLOTS
            act.wait_ge(raw_full[slot], 32 * (base // RAW_SLOTS + 1) + 32 * g)
            act.wait_ge(pieces_used, base + 1 + 4 * g)
            a(flat(whi[:, slot]), flat(raw[:, slot]), ACT.Copy).then_inc(hi_made, 1)

        def split_next():
            if E.piece + LOOKAHEAD < total_pieces:
                split(E.piece + LOOKAHEAD)
            E.piece += 1

        def open_input(gain):
            for k in range(KT):
                E.await_(h_ready)
                E.run(a(xhi[:, k, :], h[:, k, :], ACT.Copy, scale=vec[:, gain + k:gain + k + 1]), xhi_ready)
            split(E.piece + LOOKAHEAD)
            for k in range(KT):
                E.run(a(y[:, k, :], h[:, k, :], ACT.Square), h_squared)

        def square_into_ring(src):
            n = E.made[ring_squared.name]
            if n >= 4:
                act.wait_ge(ring_summed, n - 3)
            E.run(a(ring[:, n % 4, :], src, ACT.Square), ring_squared)

        def input_from_y(ready=None):
            for k in range(KT):
                if ready is not None:
                    E.await_(ready)
                E.run(a(xhi[:, k, :], y[:, k, :], ACT.Copy), xhi_ready)

        def memory_input(l):
            for k in range(KT):
                E.run(a(m_hi[:, k, :], memT[:, k, :], ACT.Copy,
                        scale=vec[:, MEM_G + l * KT + k:MEM_G + l * KT + k + 1]), m_hi_ready)

        def attention(n_steps, nk_of, scale, n_blocks, o_copy):
            t0, o0 = E.seen[probsT_ready.name], E.seen[o_ready.name]
            for i in range(n_steps + 2):
                if i < n_steps:
                    E.await_(negmax_ready)
                    if i >= 2:
                        act.wait_ge(probsT_ready, t0 + i - 1)
                    nk = nk_of(i)
                    for m in range(2):
                        E.run(a(probs[:, i % 2, m, 0:nk], PS[:, 2 * (i % 2) + m, 0:nk], ACT.Exp,
                                bias=negmax[:, i % 2, m:m + 1], scale=scale,
                                accum_out=rowsum[:, i % 2, m:m + 1]), exp_done)
                if 1 <= i <= n_steps:
                    E.await_(probsT_ready)
                    if i >= 2:
                        act.wait_ge(o_ready, o0 + i - 1)
                    n = n_blocks(i - 1)
                    E.run(a(probsT[:, 0:n, :], blocks_of(4, 6)[:, 0:n, :], ACT.Copy), probsT_copied)
                if i >= 2:
                    E.await_(o_ready)
                    dst, src = o_copy(i - 2)
                    E.run(a(dst, src, ACT.Copy), o_copied)

        act.wait_ge(mem_loaded, 16)
        for t in range(MT):
            if t:
                E.own()
            E.run(a(mem_sq[:], mem_in[:, t, :], ACT.Square, accum_out=lam[:, 4 + t:5 + t]), mem_squared)
        E.await_(lam_exp)
        E.run(a(lam[:, 2:4], lam[:, 0:2], ACT.Exp), mem_squared)
        E.await_(vec_ready)
        for p in range(LOOKAHEAD):
            split(p)

        mids = 0
        for kind, l, arg, ng, np_ in STAGES:
            base_piece = E.piece
            early = from_h(kind, arg)
            if early and kind != "xq":
                open_input(gain_of(kind, l, arg))
            if kind == "mix_out":
                memory_input(l)
            if kind == "kv":
                open_input(gain_of("xq", l, None))
                early = True
            if kind == "xq":
                early = False

            if kind == "gate_up":
                def body(base, g, n, tile, skip_split=False):
                    for kp in range(4):
                        if not (skip_split and kp == 0):
                            split(base + kp + LOOKAHEAD, g)
                    act.wait_ge(gate_scaled, n)
                    a(gate[:], gate[:], ACT.Silu).then_inc(gate_silu, 1)
                    act.wait_ge(product_ready, n)
                    a(mid_hi[:, tile, :], up[:], ACT.Copy).then_inc(mid_hi_ready, 1)

                first = straight_groups(ng)
                for q in range(first):
                    body(base_piece + 4 * q, 0, mids + q + 1, slice(2 * q, 2 * q + 2), early and q == 0)
                with act.Fori(0, (ng - first) // 2) as i:
                    for q in range(2):
                        body(base_piece + 4 * (first + q), 2 * i, mids + first + q + 1 + 2 * i,
                             bass.ds(2 * (first + q) + 4 * i, 2))
                mids += ng
                E.made[mid_hi_ready.name] = mids
                E.last = (mid_hi_ready, mids)
                E.piece += 4 * ng
                E.group += ng
                continue

            for g in range(ng):
                for kp in range(group_pieces(kind, g, np_)):
                    if early and g == 0 and kp == 0:
                        E.piece += 1
                    else:
                        split_next()
                bank = 4 * (E.group % 2)
                name = column_name(kind, g)
                if kind in ("mix_out", "xo", "down"):
                    if ends_sublayer(kind, arg):
                        for c in range(4):
                            E.await_(y_ready)
                            square_into_ring(y[:, 4 * g + c, :])
                    else:
                        E.seen[y_ready.name] += 4
                elif name in TOKEN_MAJOR:
                    dst = {"a_i": a_v, "b_v": b_v, "c_v": c_v}[name]
                    E.group_done()
                    for t in range(TT):
                        E.run(a(dst[:, t, :], PS[:, bank + t, :], ACT.Copy, scale=rstd_in[:, t:t + 1]), v_ready)
                    E.release_banks()
                elif kind == "kv" and g >= 2:
                    E.group_done()
                    E.run(a(x_v[:, :, (g - 2) * GC:(g - 1) * GC], PS[:, bank:bank + MT, :], ACT.Copy), v_ready)
                    E.release_banks()
                else:
                    E.await_(proj_ready)
                    if name == "a_f":
                        E.run(a(a_k[:], a_b[:], ACT.Sigmoid, scale=-1.0))
                        E.run(a(soft[:], a_b[:], ACT.Abs))
                        E.own()
                        E.run(a(soft[:], soft[:], ACT.Exp, scale=-1.0))
                        E.own()
                        E.run(a(soft[:], soft[:], ACT.Ln, bias=ones[:, 0:1]), softplus_ready)
                    elif name == "a_g":
                        E.run(a(a_g[:], a_g[:], ACT.Silu))
                    elif name == "d_g":
                        E.run(a(sg[:], sg[:], ACT.Sigmoid), sigmoid_ready)
                    elif name == "c_f":
                        E.run(a(c_z[:, 1, :], c_z[:, 0, :], ACT.Abs))
                        E.own()
                        E.run(a(c_z[:, 1, :], c_z[:, 1, :], ACT.Exp, scale=-1.0))
                        E.own()
                        E.run(a(c_z[:, 1, :], c_z[:, 1, :], ACT.Ln, bias=ones[0:FOX_HEADS, 0:1]), softplus_ready)
                        E.await_(cum_ready)
                        E.run(a(cum_hi[:], c_z[:, 0, :], ACT.Copy), cum_hi_ready)
                E.group += 1

            if kind == "even_in":
                for n in range(len(LEVELS)):
                    E.await_(level_diff)
                    E.run(a(lv[:, n % 2, :], lv[:, n % 2, :], ACT.Exp), level_exp)
                act.wait_ge(level_scores, len(LEVELS))
                E.run(a(lv[:, 0, :], flat(a_b[:]), ACT.Exp), decay_ready)
                E.run(a(tile_decay[:], a_b[:].rearrange("p h (t j) -> p h t j", j=P)[:, :, :, P - 1], ACT.Exp),
                      decay_ready)
                E.await_(level_diff)
                E.run(a(lv[:, 1, :], lv[:, 1, :], ACT.Exp), decay_ready)
                E.await_(cross_scores)
                E.run(a(cross[:], blocks_of(0, 6), ACT.Copy), cross_copied)
                E.await_(o_ready)
                E.run(a(y[:, 0:4, :], PS[:, 0:4, :], ACT.Copy), o_copied)
                attention(16, lambda i: (i % TT + 1) * P, 0.125, lambda i: i % TT + 1,
                          lambda i: (y[:, 4 + i // TT, i % TT * P:(i % TT + 1) * P], PS[:, 6 + i % 2, 0:P]))
                E.own()
                for k in range(KT):
                    square_into_ring(y[:, k, :])
                input_from_y(y_mixed)
            if kind == "odd_in":
                attention(16, lambda i: (i % TT + 1) * P, 0.125, lambda i: 2 * (i % TT + 1),
                          lambda i: (y[:, i // TT, i % TT * P:(i % TT + 1) * P], PS[:, 6 + i % 2, 0:P]))
                for c in range(CONV_T):
                    E.await_(conv_centred)
                    square_into_ring(conv[:, c, :])
                for c in range(CONV_T):
                    E.await_(conv_scaled)
                    E.run(a(y[:, 4 + c, :], conv[:, c, :], ACT.Silu, scale=vec[:, LN_G + c:LN_G + c + 1],
                            bias=vec[:, LN_B + c:LN_B + c + 1]), y_silu)
                E.own()
                input_from_y()
            if kind == "xq":
                attention(8, lambda i: MEM, 0.0625, lambda i: 2 * MT,
                          lambda i: (y[:, 4 * (i // TT):4 * (i // TT) + 4, i % TT * P:(i % TT + 1) * P],
                                     PS[:, 6 + i % 2, :].rearrange("p (a j) -> p a j", j=P)))
                E.own()
                input_from_y()

    @block.vector
    def _(dve):
        E = Engine(dve, vector_step)
        v = nc.vector

        def split(base, g=0):
            slot = base % RAW_SLOTS
            dve.wait_ge(hi_made, base + 1 + 4 * g)
            v.tensor_tensor(flat(wlo[:, slot]), flat(raw[:, slot]), flat(whi[:, slot]).bitcast(f32),
                            SUB).then_inc(lo_made, 1)

        def split_next():
            if E.piece + LOOKAHEAD < total_pieces:
                split(E.piece + LOOKAHEAD)
            E.piece += 1

        def make_diag(cols):
            E.run(v.tensor_tensor(diag[:], ident[:].unsqueeze(1).broadcast_to([P, TT, P]),
                                  cols.unsqueeze(2).broadcast_to([P, TT, P]), MUL), diag_ready)

        def variance(src, n, cols):
            E.run(v.tensor_scalar(var[:, 0:cols], src, 1.0 / n, EPS, MUL, ADD), var_ready)

        def input_stats(bank):
            E.await_(h_summed)
            variance(PS[:, bank, 0:TT], D, TT)
            E.await_(rstd_ready)
            E.run(v.tensor_copy(rstd_in[:], rstd[:, 0:TT]))
            make_diag(rstd[:, 0:TT])

        def input_spread(bank):
            E.await_(spread_ready)
            E.run(v.tensor_copy(rsb[:], PS[:, bank + 1, :]), spread_used)
            E.own()

        def input_lo(k, gain=None):
            E.await_(xhi_ready)
            if gain is None:
                E.run(v.tensor_tensor(xlo[:, k, :], y[:, k, :], xhi[:, k, :].bitcast(f32), SUB), xlo_ready)
            else:
                E.run(v.scalar_tensor_tensor(out=xlo[:, k, :], in0=h[:, k, :], scalar=vec[:, gain + k:gain + k + 1],
                                             in1=xhi[:, k, :].bitcast(f32), op0=MUL, op1=SUB), xlo_ready)

        def memory_lo(l):
            for k in range(KT):
                E.await_(m_hi_ready)
                c = MEM_G + l * KT + k
                E.run(v.scalar_tensor_tensor(out=m_lo[:, k, :], in0=memT[:, k, :], scalar=vec[:, c:c + 1],
                                             in1=m_hi[:, k, :].bitcast(f32), op0=MUL, op1=SUB), m_lo_ready)

        def close_sublayer(kind, l, arg, bank, next_gain):
            E.await_(ring_summed, 8)
            variance(PS[:, bank, 0:TT], D, TT)
            E.await_(rstd_ready)
            make_diag(rstd[:, 0:TT])
            E.await_(spread_ready)
            gain = post_gain(kind, l, arg)
            for k in range(KT):
                s = spread_used if k == KT - 1 else None
                E.run(v.tensor_tensor(y[:, k, :], y[:, k, :], PS[:, (bank + 5) % 8, :], MUL), s)
                E.own()
                E.run(v.scalar_tensor_tensor(out=h[:, k, :], in0=y[:, k, :], scalar=vec[:, gain + k:gain + k + 1],
                                             in1=h[:, k, :], op0=MUL, op1=ADD), h_ready)
                if k >= 1 and next_gain is not None:
                    input_lo(k - 1, next_gain)
            if next_gain is not None:
                input_lo(KT - 1, next_gain)

        def attention(n_steps, nk_of, scale, differential, meanwhile=None):
            for i in range(n_steps + 1):
                if i < n_steps:
                    E.await_(scores_ready)
                    nk = nk_of(i)
                    E.run(v.tensor_reduce(out=negmax[:, i % 2, :], in_=PS[:, 2 * (i % 2):2 * (i % 2) + 2, 0:nk],
                                          axis=AX.X, op=ALU.max, negate=True))
                    E.own()
                    E.run(v.tensor_scalar(negmax[:, i % 2, :], negmax[:, i % 2, :], scale, None, MUL), negmax_ready)
                if meanwhile is not None:
                    meanwhile(2)
                if i >= 1:
                    j = (i - 1) % 2
                    nk = nk_of(i - 1)
                    E.await_(exp_done, 2)
                    E.run(v.reciprocal(recip[:, j, :], rowsum[:, j, :]))
                    E.own()
                    p0, p1 = probs[:, j, 0, 0:nk], probs[:, j, 1, 0:nk]
                    if differential:
                        E.run(v.tensor_scalar(p1, p1, recip[:, j, 1:2], lam[:, 6:7], MUL, MUL))
                        E.own()
                        E.run(v.scalar_tensor_tensor(out=p0, in0=p0, scalar=recip[:, j, 0:1], in1=p1,
                                                     op0=MUL, op1=ADD), probs_ready)
                    else:
                        E.run(v.tensor_scalar(p0, p0, recip[:, j, 0:1], None, MUL), probs_ready)
                        E.run(v.tensor_scalar(p1, p1, recip[:, j, 1:2], None, MUL), probs_ready)

        dve.wait_ge(small_loaded, 32)
        E.run(v.tensor_tensor(lam_in[:, 0:4:2, :], lam_in[:, 0:4:2, :], lam_in[:, 1:4:2, :], MUL))
        E.own()
        E.run(v.tensor_reduce(out=lam[:, 0:2], in_=lam_in[:, 0:4:2, :], axis=AX.X, op=ADD), lam_exp)
        for k in range(KT):
            E.await_(transposed)
            E.run(v.tensor_copy(h[:, k, :], PS[:, k, :]), h_ready)
        E.await_(transposed)
        E.run(v.tensor_copy(vec[:], PS[:, 0, 0:N_VEC]))
        E.own()
        E.run(v.tensor_scalar(vec[:, FFN_POST:FFN_POST + 32], vec[:, FFN_POST:FFN_POST + 32], 0.5, None, MUL))
        E.run(v.tensor_scalar(vec[:, DIFF_G:DIFF_G + 4], vec[:, DIFF_G:DIFF_G + 4], 1.0 - LAM_INIT, None, MUL),
              vec_ready)
        E.await_(mem_squared, 3)
        E.run(v.tensor_scalar(var[:, 0:MT], lam[:, 4:6], 1.0 / D, EPS, MUL, ADD), var_ready)
        E.run(v.tensor_tensor(lam[:, 7:8], lam[:, 3:4], lam[:, 2:3], SUB))
        E.own()
        E.run(v.tensor_scalar(lam[:, 6:7], lam[:, 7:8], -LAM_INIT, None, ADD))
        E.await_(rstd_ready)
        for t in range(MT):
            E.run(v.tensor_scalar(mem_in[:, t, :], mem_in[:, t, :], rstd[:, t:t + 1], None, MUL), mem_scaled)
        E.await_(transposed)
        E.run(v.tensor_copy(memT[:].rearrange("p a b -> p (a b)"), flat(PS[:, 4:8, :])), memT_ready)
        E.await_(tables_ready)
        E.run(v.tensor_copy(head_sel[:], head_sel_f[:]))
        E.run(v.tensor_scalar(alibi[:], position[:], slope[:, 0:1], None, MUL))
        E.own()
        dve.wait_ge(*E.last).then_inc(lo_made, RAW_SLOTS)

        def conv_steps():
            for c in range(CONV_T):
                for w in range(CONV_W):
                    tap = vec[:, CONV_TAPS + CONV_T * w + c:CONV_TAPS + CONV_T * w + c + 1]
                    if w == 0:
                        E.run(v.tensor_scalar(conv[:, c, :], u[:, c, 0:SEQ], tap,
                                              vec[:, CONV_B + c:CONV_B + c + 1], MUL, ADD))
                    else:
                        E.own()
                        E.run(v.scalar_tensor_tensor(out=conv[:, c, :], in0=u[:, c, w:w + SEQ], scalar=tap,
                                                     in1=conv[:, c, :], op0=MUL, op1=ADD),
                              conv_ready if w == CONV_W - 1 else None)
                    yield

        conv_left = conv_steps()

        def convolve(n):
            for _ in range(n):
                next(conv_left, None)

        for p in range(LOOKAHEAD):
            split(p)
        for k in range(KT):
            input_lo(k, FFN_PRE)

        mids = 0
        for n_stage, (kind, l, arg, ng, np_) in enumerate(STAGES):
            base_piece = E.piece
            stats = from_h(kind, arg)
            other = 4 * ((E.group + 1) % 2)
            if kind == "gate_up":
                def body(base, g, n, tile, with_stats=False, bank=0):
                    for kp in range(4):
                        split(base + kp + LOOKAHEAD, g)
                        if kp == 0 and with_stats:
                            input_stats(other)
                    if with_stats:
                        input_spread(other)
                    dve.wait_ge(pieces_used, base + 4 + SPLIT_SLOTS + 4 * g)
                    started = not isinstance(n, int) or n > 1
                    if started:
                        dve.wait_ge(product_ready, n - 1)
                    v.tensor_tensor(gate[:], PS[:, bank:bank + 2, :],
                                    rsb[:].unsqueeze(1).broadcast_to([P, 2, SEQ]), MUL).then_inc(gate_scaled, 1)
                    if started:
                        dve.wait_ge(mid_lo_ready, n - 1)
                    v.tensor_tensor(up[:], PS[:, bank + 2:bank + 4, :],
                                    rsb[:].unsqueeze(1).broadcast_to([P, 2, SEQ]), MUL).then_inc(up_scaled, 1)
                    dve.wait_ge(up_scaled, n).then_inc(bank_free[bank // 4], 1)
                    dve.wait_ge(mid_hi_ready, n)
                    v.tensor_tensor(mid_lo[:, tile, :], up[:], mid_hi[:, tile, :].bitcast(f32),
                                    SUB).then_inc(mid_lo_ready, 1)

                first = straight_groups(ng)
                for q in range(first):
                    body(base_piece + 4 * q, 0, mids + q + 1, slice(2 * q, 2 * q + 2), stats and q == 0,
                         4 * ((E.group + q) % 2))
                with dve.Fori(0, (ng - first) // 2) as i:
                    for q in range(2):
                        body(base_piece + 4 * (first + q), 2 * i, mids + first + q + 1 + 2 * i,
                             bass.ds(2 * (first + q) + 4 * i, 2), False, 4 * ((E.group + first + q) % 2))
                mids += ng
                E.last = (mid_lo_ready, mids)
                E.piece += 4 * ng
                E.group += ng
                continue

            if kind == "mix_out":
                memory_lo(l)
            first_bank = 4 * (E.group % 2)
            if kind == "odd_in":
                E.run(v.memset(u[:, :, 0:U0], 0.0))
            for g in range(ng):
                bank = 4 * (E.group % 2)
                name = column_name(kind, g)
                for kp in range(group_pieces(kind, g, np_)):
                    split_next()
                    if stats and g == 0 and kp == 0:
                        input_stats(other)
                    if kind == "odd_in" and g >= 3:
                        convolve(5)
                if stats and g == 0:
                    input_spread(other)
                if kind in ("down", "mix_out", "xo"):
                    E.group_done()
                    for c in range(4):
                        k = 4 * g + c
                        if kind == "down" and arg[1] == 1:
                            E.run(v.tensor_tensor(y[:, k, :], PS[:, bank + c, :], y[:, k, :], ADD), y_ready)
                        else:
                            E.run(v.tensor_copy(y[:, k, :], PS[:, bank + c, :]), y_ready)
                    E.release_banks()
                elif name in TOKEN_MAJOR or (kind == "kv" and g >= 2):
                    pass
                elif name == "c_f":
                    E.group_done()
                    E.run(v.tensor_tensor(c_z[:, 0, :], PS[0:FOX_HEADS, bank, :], rsb[0:FOX_HEADS, :], MUL))
                    E.release_banks()
                    E.run(v.tensor_scalar(c_z[:, 0, :], c_z[:, 0, :], fbias[:, 0:1], None, ADD), proj_ready)
                    E.await_(softplus_ready)
                    E.run(v.scalar_tensor_tensor(out=c_z[:, 0, :], in0=c_z[:, 0, :], scalar=0.0,
                                                 in1=c_z[:, 1, :], op0=ALU.min, op1=SUB))
                    E.own()
                    E.run(v.tensor_tensor_scan(c_z[:, 2, :], ones[0:FOX_HEADS, 0:1].broadcast_to([FOX_HEADS, SEQ]),
                                               c_z[:, 0, :], 0.0, MUL, ADD))
                    E.own()
                    E.run(v.tensor_scalar(c_z[:, 0, :], c_z[:, 2, :], -8.0, None, MUL), cum_ready)
                    E.await_(cum_hi_ready)
                    E.run(v.tensor_tensor(cum_lo[:], c_z[:, 0, :], cum_hi[:].bitcast(f32), SUB), cum_lo_ready)
                else:
                    E.group_done()
                    if kind == "kv":
                        E.run(v.tensor_copy(x_k[:, 4 * g:4 * g + 4, :], PS[:, bank:bank + 4, 0:MEM]), proj_ready)
                    else:
                        dst = {"a_f": a_b, "a_q": a_q, "a_g": a_g, "b_q": b_q, "b_k": b_k, "d_g": sg,
                               "c_q": c_q, "c_k": c_k}.get(name)
                        dst = dst[:] if dst is not None else u[:, :, U0:] if name == "d_a" else \
                            x_q[:, 4 * g:4 * g + 4, :]
                        E.run(v.tensor_tensor(dst, PS[:, bank:bank + 4, :],
                                              rsb[:].unsqueeze(1).broadcast_to([P, 4, SEQ]), MUL), proj_ready)
                    E.release_banks()
                    if name == "a_f":
                        E.await_(softplus_ready)
                        E.run(v.scalar_tensor_tensor(out=logf[:], in0=a_b[:], scalar=0.0, in1=soft[:],
                                                     op0=ALU.min, op1=SUB))
                        E.own()
                        for hd in range(4):
                            for t in range(TT):
                                tok = slice(t * P, (t + 1) * P)
                                E.run(v.tensor_tensor_scan(a_b[:, hd, tok], ones[:], logf[:, hd, tok], 0.0, MUL, ADD))
                    if name == "d_g":
                        E.await_(sigmoid_ready)
                        E.run(v.tensor_tensor(u[:, :, U0:], u[:, :, U0:], sg[:], MUL))
                        E.own()
                E.group += 1

            if kind == "even_in":
                E.group_done()
                E.run(v.memset(scoresT[:], 0.0))
                bflat = flat(a_b[:])

                def halves(t, L):
                    t = t.rearrange("p (b r j) -> p b r j", r=2, j=L)
                    return t[:, :, 0, :], t[:, :, 1, :]

                def level_sub(n):
                    L = LEVELS[n]
                    nb = 4 * SEQ // (2 * L)
                    left, right = halves(bflat, L)
                    ref = left[:, :, L - 1:L].broadcast_to([P, nb, L])
                    if n >= 2:
                        dve.wait_ge(level_scores, n - 1)
                    dl, dr = halves(lv[:, n % 2, :], L)
                    E.run(v.tensor_tensor(dl, ref, left, SUB))
                    E.run(v.tensor_tensor(dr, right, ref, SUB), level_diff)

                def level_mul(n):
                    L = LEVELS[n]
                    E.await_(level_exp)
                    dl, dr = halves(lv[:, n % 2, :], L)
                    kl, _ = halves(flat(a_k[:]), L)
                    _, qr = halves(flat(a_q[:]), L)
                    E.run(v.tensor_tensor(dl, dl, kl, MUL))
                    E.run(v.tensor_tensor(dr, dr, qr, MUL), level_ready)

                def level_merge(n):
                    E.await_(level_scores)
                    if n:
                        dve.wait_ge(level_merged, n)
                    E.run(v.copy_predicated(scoresT[:], level_mask[:, n, :].unsqueeze(1).broadcast_to([P, 16, P]),
                                            blocks_of(4 * (n % 2), 4 * (n % 2) + 4)), level_merged)

                n_levels = len(LEVELS)
                level_sub(0)
                for n in range(n_levels):
                    if n + 1 < n_levels:
                        level_sub(n + 1)
                    level_mul(n)
                    if n >= 1:
                        level_merge(n - 1)
                level_merge(n_levels - 1)
                level_merge(n_levels)
                b4 = a_b[:].rearrange("p h (t j) -> p (h t) j", j=P)
                E.run(v.tensor_tensor(lv[:, 1, :].rearrange("p (t j) -> p t j", j=P),
                                      b4[:, :, P - 1:P].broadcast_to([P, 16, P]), b4, SUB), level_diff)
                E.await_(decay_ready, 3)
                E.run(v.tensor_tensor(lv[:, 0, :], lv[:, 0, :], flat(a_q[:]), MUL))
                E.run(v.tensor_tensor(lv[:, 1, :], lv[:, 1, :], flat(a_k[:]), MUL))
                E.own()
                kd = lv[:, 1, :].rearrange("p (h t j) -> p h t j", t=TT, j=P)
                for J in range(2):
                    E.run(v.tensor_tensor(kd2[:, :, J, :], kd[:, :, J, :],
                                          tile_decay[:, :, J + 1:J + 2].broadcast_to([P, 4, P]), MUL))
                E.own()
                E.run(v.tensor_tensor(kd3[:], kd2[:, :, 0, :], tile_decay[:, :, 2:3].broadcast_to([P, 4, P]), MUL),
                      cross_ready)
                attention(16, lambda i: (i % TT + 1) * P, 0.125, True)
                for half in range(2):
                    E.await_(ring_summed, 4)
                    variance(PS[:, 0, 16 * half:16 * half + 16], HEAD, 16)
                    E.await_(rstd_ready)
                    for t in range(4):
                        k = 4 * half + t
                        make_diag(rstd[:, 4 * t:4 * t + 4])
                        E.await_(spread_ready)
                        E.run(v.tensor_tensor(y[:, k, :], y[:, k, :], PS[:, 1 + t, :], MUL))
                        E.own()
                        if half == 0:
                            E.run(v.scalar_tensor_tensor(out=y[:, k, :], in0=y[:, k, :],
                                                         scalar=vec[:, HGRN_G + t:HGRN_G + t + 1],
                                                         in1=a_g[:, t, :], op0=MUL, op1=MUL), y_mixed)
                        else:
                            E.run(v.tensor_scalar(y[:, k, :], y[:, k, :], vec[:, DIFF_G + t:DIFF_G + t + 1],
                                                  None, MUL), y_mixed)
                for k in range(KT):
                    input_lo(k)
            if kind == "odd_in":
                attention(16, lambda i: (i % TT + 1) * P, 0.125, False, convolve)
                convolve(CONV_T * CONV_W)
                E.await_(conv_summed)
                E.run(v.tensor_scalar(var[:, 0:TT], PS[:, 0, 0:TT], 1.0 / (CONV_T * P), None, MUL))
                E.own()
                make_diag(var[:, 0:TT])
                E.await_(spread_ready)
                for c in range(CONV_T):
                    E.run(v.tensor_tensor(conv[:, c, :], conv[:, c, :], PS[:, 1, :], SUB), conv_centred)
                E.await_(ring_summed, 4)
                variance(PS[:, 0, TT:2 * TT], CONV_T * P, TT)
                E.await_(rstd_ready)
                make_diag(rstd[:, 0:TT])
                E.await_(spread_ready)
                for c in range(CONV_T):
                    E.run(v.tensor_tensor(conv[:, c, :], conv[:, c, :], PS[:, 2, :], MUL), conv_scaled)
                for k in range(KT):
                    input_lo(k)
            if kind == "xq":
                attention(8, lambda i: MEM, 0.0625, False)
                for k in range(KT):
                    input_lo(k)
            if ends_sublayer(kind, arg):
                nxt = next(((k2, l2, a2) for k2, l2, a2, _, _ in STAGES[n_stage + 1:] if k2 != "kv"), None)
                close_sublayer(kind, l, arg, first_bank, gain_of(*nxt) if nxt else None)
        for t in range(TT):
            for i in range(2):
                E.await_(transposed)
                E.run(v.tensor_copy(x_in[:, t, i * 512:(i + 1) * 512], PS[:, 2 * t + i, :]), y_mixed)

    @block.tensor
    def _(pe):
        E = Engine(pe, None)
        mm = nc.tensor.matmul

        def three(out_ap, lh, ll, rh, rl, start, stop):
            mm(out_ap, lh, rl, start=start, stop=False)
            mm(out_ap, ll, rh, start=False, stop=False)
            return mm(out_ap, lh, rh, start=False, stop=stop)

        def spread(bank):
            E.await_(diag_ready)
            for t in range(TT):
                last = mm(PS[:, bank, t * P:(t + 1) * P], ones[:], diag[:, t, :], start=True, stop=True)
            E.run(last, spread_ready)

        def column_sums(bank, c0, tile, start, stop):
            for t in range(TT):
                last = mm(PS[:, bank, c0 + t:c0 + t + 1], tile[:, t * P:(t + 1) * P], ones[:, 0:1],
                          start=start and t == 0, stop=stop and t == TT - 1, skip_group_check=True)
            return last

        unread = [False, False]

        def wait_banks(group):
            if group >= 2:
                pe.wait_ge(bank_free[group % 2], group // 2)
            if unread[group % 2]:
                E.await_(spread_used)
                unread[group % 2] = False

        def attention(n_steps, qk, blocks, pv):
            e0, c0, o0 = E.seen[exp_done.name], E.seen[probsT_copied.name], E.seen[o_copied.name]

            def scores(i):
                if i >= 2:
                    pe.wait_ge(exp_done, e0 + 2 * (i - 1))
                E.run(qk(i), scores_ready)
            scores(0)
            for i in range(n_steps):
                if i + 1 < n_steps:
                    scores(i + 1)
                bl = blocks(i)
                E.await_(probs_ready, len({m for m, _ in bl}))
                if i >= 1:
                    pe.wait_ge(probsT_copied, c0 + i)
                for n, (m, kt) in enumerate(bl):
                    last = nc.tensor.transpose(blocks_of(4, 6)[:, n, :], probs[:, i % 2, m, kt * P:(kt + 1) * P],
                                               ident[:])
                E.run(last, probsT_ready)
                pe.wait_ge(probsT_copied, c0 + i + 1)
                if i >= 2:
                    pe.wait_ge(o_copied, o0 + i - 1)
                E.run(pv(i, PS[:, 6 + i % 2, :]), o_ready)
            E.seen[exp_done.name] = e0 + 2 * n_steps
            E.seen[probsT_copied.name] = c0 + n_steps
            E.seen[o_copied.name] = o0 + n_steps
            pe.wait_ge(exp_done, e0 + 2 * n_steps)
            pe.wait_ge(o_copied, o0 + n_steps)

        def weights(base, g=0):
            pe.wait_ge(lo_made, base + 1 + RAW_SLOTS + 4 * g)

        def feature_major(slot, kp, n_kp, bank, src_hi, src_lo, k_of, n=SEQ):
            for i in range(PK):
                k = k_of(kp, i)
                for c in range(4):
                    cols = slice(c * P, (c + 1) * P)
                    last = three(PS[:, bank + c, 0:n], whi[:, slot, i, cols], wlo[:, slot, i, cols],
                                 src_hi[:, k, :], src_lo[:, k, :], kp + i == 0, kp == n_kp - 1 and i == PK - 1)
            return last

        def token_major(slot, kp, n_kp, bank, src_hi, src_lo, tiles):
            for i in range(PK):
                k = 2 * kp + i
                for t in range(tiles):
                    toks = slice(t * P, (t + 1) * P)
                    last = three(PS[:, bank + t, :], src_hi[:, k, toks], src_lo[:, k, toks],
                                 whi[:, slot, i, :], wlo[:, slot, i, :], kp + i == 0,
                                 kp == n_kp - 1 and i == PK - 1)
            return last

        def forget_gates(slot, bank):
            w = [t[:, slot].rearrange("p a (b n) -> p (a b) n", n=P) for t in (whi, wlo)]
            for k in range(KT):
                last = three(PS[:, bank, :], w[0][:, k, :], w[1][:, k, :], xhi[:, k, :], xlo[:, k, :],
                             k == 0, k == KT - 1)
            return last

        T = nc.tensor.transpose
        pe.wait_ge(x_loaded, 16)
        pe.wait_ge(consts_ready, 1)
        for k in range(KT):
            for t in range(TT):
                last = T(PS[:, k, t * P:(t + 1) * P], x_in[:, t, k * P:(k + 1) * P], ident[:])
            E.run(last, transposed)
        pe.wait_ge(rows_loaded, 16 * 13)
        pe.wait_ge(h_ready, 1)
        n1 = CONV_TAPS - MEM_G
        n2 = CONV_W * CONV_T
        T(PS[:, 0, 0:P], rows[:, 0, :], ident[:])
        T(PS[:, 0, P:P + n1], rows[0:n1, 1, :], ident[0:n1, 0:n1])
        E.run(T(PS[:, 0, CONV_TAPS:CONV_TAPS + n2], rows[0:n2, 2, :], ident[0:n2, 0:n2]), transposed)
        pe.wait_ge(h_ready, KT)
        E.await_(mem_scaled, MT)
        memo = PS[:, 4:8, :].rearrange("p a (b j) -> p (a b) j", j=MEM)
        for k in range(KT):
            for t in range(MT):
                last = T(memo[:, k, t * P:(t + 1) * P], mem_in[:, t, k * P:(k + 1) * P], ident[:])
        E.run(last, transposed)
        pe.wait_ge(transposed, E.made[transposed.name]).then_inc(pieces_used, SPLIT_SLOTS)
        E.await_(memT_ready)

        mids = 0
        for kind, l, arg, ng, np_ in STAGES:
            stats = from_h(kind, arg)
            if kind != "kv" and (stats or kind in ("mix_out", "xo")):
                E.seen[xlo_ready.name] += KT
            x_ready = E.seen[xlo_ready.name] - KT
            if kind == "kv":
                E.seen[m_lo_ready.name] += KT

            if kind == "gate_up":
                def body(base, g, group, n, with_stats=False):
                    bank = 4 * (group % 2)
                    for kp in range(4):
                        weights(base + kp, g)
                        if kp == 0:
                            pe.wait_ge(bank_free[group % 2], group // 2 + n)
                        pe.wait_ge(xlo_ready, x_ready + 2 * kp + 2)
                        slot = (base + kp) % SPLIT_SLOTS
                        feature_major(slot, kp, 4, bank, xhi, xlo, lambda a_, b_: 2 * a_ + b_).then_inc(pieces_used, 1)
                        if with_stats and kp == 2:
                            input_sums(group)
                        if with_stats and kp == 3:
                            spread(4 * ((group + 1) % 2) + 1)
                            unread[(group + 1) % 2] = True

                def input_sums(group):
                    wait_banks(group + 1)
                    for k in range(KT):
                        E.await_(h_squared)
                        last = column_sums(4 * ((group + 1) % 2), 0, y[:, k, :], k == 0, k == KT - 1)
                    E.run(last, h_summed)

                first = straight_groups(ng)
                for q in range(first):
                    wait_banks(E.group + q)
                    body(E.piece + 4 * q, 0, E.group + q, 0, stats and q == 0)
                with pe.Fori(0, (ng - first) // 2) as i:
                    for q in range(2):
                        body(E.piece + 4 * (first + q), 2 * i, E.group + first + q, i)
                E.piece += 4 * ng
                E.group += ng
                continue

            if kind == "down":
                m0, mids = mids, mids + np_
            for g in range(ng):
                wait_banks(E.group)
                bank = 4 * (E.group % 2)
                other = 4 * ((E.group + 1) % 2)
                name = column_name(kind, g)
                n_kp = group_pieces(kind, g, np_)
                for kp in range(n_kp):
                    weights(E.piece)
                    slot = E.piece % SPLIT_SLOTS
                    if kind == "down":
                        pe.wait_ge(mid_lo_ready, m0 + kp + 1)
                        last = feature_major(slot, kp, n_kp, bank, mid_hi, mid_lo, lambda a_, b_: 2 * a_ + b_)
                    elif kind == "kv":
                        pe.wait_ge(m_lo_ready, E.seen[m_lo_ready.name])
                        last = feature_major(slot, kp, 4, bank, m_hi, m_lo, lambda a_, b_: 2 * a_ + b_, MEM) \
                            if g < 2 else token_major(slot, kp, 4, bank, m_hi, m_lo, MT)
                    else:
                        pe.wait_ge(xlo_ready, x_ready + (KT if name == "c_f" else 2 * kp + 2))
                        last = forget_gates(slot, bank) if name == "c_f" else \
                            token_major(slot, kp, 4, bank, xhi, xlo, TT) if name in TOKEN_MAJOR else \
                            feature_major(slot, kp, 4, bank, xhi, xlo, lambda a_, b_: 2 * a_ + b_)
                    last.then_inc(pieces_used, 1)
                    E.piece += 1
                    if stats and g == 0 and kp == 2:
                        wait_banks(E.group + 1)
                        for k in range(KT):
                            E.await_(h_squared)
                            last = column_sums(other, 0, y[:, k, :], k == 0, k == KT - 1)
                        E.run(last, h_summed)
                    if stats and g == 0 and kp == 3:
                        spread(other + 1)
                        unread[(E.group + 1) % 2] = True
                    if ends_sublayer(kind, arg) and g == 1 and kp == 2:
                        for c in range(4):
                            E.await_(ring_squared)
                            E.run(column_sums(other, 0, ring[:, E.made[ring_summed.name] % 4, :], c == 0, False),
                                  ring_summed)
                E.group += 1
            if ends_sublayer(kind, arg):
                for c in range(4):
                    E.await_(ring_squared)
                    E.run(column_sums(other, 0, ring[:, E.made[ring_summed.name] % 4, :], False, c == 3), ring_summed)
                spread(bank + 1)
                unread[bank // 4] = True

            if kind == "even_in":
                for q in range(2):
                    wait_banks(E.group + q)
                for n in range(len(LEVELS) + 1):
                    if n < len(LEVELS):
                        E.await_(level_ready)
                    if n >= 2:
                        pe.wait_ge(level_merged, n - 1)
                    for b in range(16):
                        tok = slice(b * P, (b + 1) * P)
                        lhs, rhs = (lv[:, n % 2, tok],) * 2 if n < len(LEVELS) else \
                            (flat(a_k[:])[:, tok], flat(a_q[:])[:, tok])
                        last = mm(blocks_of(4 * (n % 2), 4 * (n % 2) + 4)[:, b, :], lhs, rhs, start=True, stop=True)
                    E.run(last, level_scores)
                pe.wait_ge(level_merged, len(LEVELS) + 1)
                E.await_(cross_ready)
                kd = lv[:, 1, :].rearrange("p (h t j) -> p h t j", t=TT, j=P)
                for hd in range(4):
                    for n, (i, j) in enumerate(CROSS):
                        key = kd[:, hd, j, :] if i - j == 1 else kd2[:, hd, j, :] if i - j == 2 else kd3[:, hd, :]
                        last = mm(blocks_of(0, 6)[:, 6 * hd + n, :], key,
                                  lv[:, 0, hd * SEQ + i * P:hd * SEQ + (i + 1) * P], start=True, stop=True)
                E.run(last, cross_scores)
                E.await_(cross_copied)
                for hd in range(4):
                    for i in range(TT):
                        terms = [(cross[:, 6 * hd + n, :], j) for n, (ii, j) in enumerate(CROSS) if ii == i]
                        terms.append((scoresT[:, 4 * hd + i, :], i))
                        for n, (s, j) in enumerate(terms):
                            last = mm(PS[:, hd, i * P:(i + 1) * P], a_v[:, j, hd * P:(hd + 1) * P], s,
                                      start=n == 0, stop=n == len(terms) - 1)
                E.run(last, o_ready)
                E.await_(o_copied)

                def qk(i):
                    hd, qb = i // TT, i % TT
                    nk = (qb + 1) * P
                    for m in range(2):
                        o = PS[:, 2 * (i % 2) + m, :]
                        r = slice(64 * m, 64 * m + 64)
                        mm(o[:, 0:nk], b_q[r, hd, qb * P:nk], b_k[r, hd, 0:nk], start=True, stop=False)
                        mm(o[:, 0:nk], head_sel[0:4, hd, :], alibi[:, 0:nk], start=False, stop=False)
                        last = mm(o[:, qb * P:nk], ident_bf[:], causal_neg[:], start=False, stop=True)
                    return last

                def pv(i, o):
                    hd, qb = i // TT, i % TT
                    for kt in range(qb + 1):
                        last = mm(o[:, 0:P], b_v[:, kt, hd * P:(hd + 1) * P], probsT[:, kt, :],
                                  start=kt == 0, stop=kt == qb)
                    return last
                attention(16, qk, lambda i: [(0, kt) for kt in range(i % TT + 1)], pv)
                for half in range(2):
                    for t in range(4):
                        E.await_(ring_squared)
                        E.run(column_sums(0, 16 * half + 4 * t, ring[:, E.made[ring_summed.name] % 4, :], True, True),
                              ring_summed)
                    for t in range(4):
                        spread(1 + t)
            if kind == "odd_in":
                for q in range(2):
                    wait_banks(E.group + q)
                E.await_(cum_lo_ready)

                def qk(i):
                    pair, qb = i // TT, i % TT
                    nk = (qb + 1) * P
                    for m in range(2):
                        o = PS[:, 2 * (i % 2) + m, :]
                        r = slice(64 * m, 64 * m + 64)
                        sel = head_sel[:, 2 * pair + m, :]
                        mm(o[:, 0:nk], c_q[r, pair, qb * P:nk], c_k[r, pair, 0:nk], start=True, stop=False)
                        mm(o[:, 0:nk], sel, cum_lo[:, 0:nk], start=False, stop=False)
                        mm(o[:, 0:nk], sel, cum_hi[:, 0:nk], start=False, stop=False)
                        last = mm(o[:, qb * P:nk], ident_bf[:], causal_neg[:], start=False, stop=True)
                    return last

                def pv(i, o):
                    pair, qb = i // TT, i % TT
                    for m in range(2):
                        c = (2 * pair + m) * 64
                        for kt in range(qb + 1):
                            last = mm(o[64 * m:64 * m + 64, 0:P], c_v[:, kt, c:c + 64],
                                      probsT[:, m * (qb + 1) + kt, :], start=kt == 0, stop=kt == qb)
                    return last
                attention(16, qk, lambda i: [(m, kt) for m in range(2) for kt in range(i % TT + 1)], pv)
                E.await_(conv_ready, CONV_T)
                for c in range(CONV_T):
                    last = column_sums(0, 0, conv[:, c, :], c == 0, c == CONV_T - 1)
                E.run(last, conv_summed)
                spread(1)
                for c in range(CONV_T):
                    E.await_(ring_squared)
                    E.run(column_sums(0, TT, ring[:, E.made[ring_summed.name] % 4, :], c == 0, c == CONV_T - 1),
                          ring_summed)
                spread(2)
            if kind == "xq":
                for q in range(2):
                    wait_banks(E.group + q)

                def qk(i):
                    pair, qb = i // TT, i % TT
                    for m in range(2):
                        for kt in range(2):
                            ft = 2 * (2 * pair + m) + kt
                            last = mm(PS[:, 2 * (i % 2) + m, 0:MEM], x_q[:, ft, qb * P:(qb + 1) * P], x_k[:, ft, :],
                                      start=kt == 0, stop=kt == 1)
                    return last

                def pv(i, o):
                    pair = i // TT
                    for m in range(2):
                        for half in range(2):
                            n = 2 * m + half
                            c = (4 * pair + n) * P
                            for kt in range(MT):
                                last = mm(o[:, n * P:(n + 1) * P], x_v[:, kt, c:c + P], probsT[:, 2 * m + kt, :],
                                          start=kt == 0, stop=kt == MT - 1)
                    return last
                attention(8, qk, lambda i: [(m, kt) for m in range(2) for kt in range(MT)], pv)
        pe.wait_ge(h_ready, KT * (1 + 4 * DEPTH))
        for t in range(TT):
            for i in range(2):
                for k in range(4):
                    last = T(PS[:, 2 * t + i, k * P:(k + 1) * P], h[:, 4 * i + k, t * P:(t + 1) * P], ident[:])
                E.run(last, transposed)

    block_ctx.__exit__(None, None, None)


INPUTS = ["x", "mem", "ffn_norm_pre", "ffn_norm_post", "ffn_w_gate", "ffn_w_up", "ffn_w_down",
          "mix_norm_pre", "mix_norm_post", "even_w_in", "even_w_out", "hgrn_norm_g", "diff_lambda",
          "diff_norm_g", "odd_w_in", "odd_w_out", "fox_f_bias", "conv_w", "conv_b", "conv_ln_g", "conv_ln_b",
          "xattn_norm_pre", "xattn_norm_post", "mem_norm_g", "xattn_w_q", "xattn_w_kv", "xattn_w_o"]


def kernel(**inputs):
    import concourse.bacc as bacc
    from concourse.bass_utils import run_bass_kernel_spmd

    nc = bacc.Bacc("TRN2", target_bir_lowering=False, num_devices=1)
    arrays, tensors = {}, {}
    for name in INPUTS:
        a = np.ascontiguousarray(inputs[name])
        arrays[name + "_dram"] = a
        tensors[name] = nc.dram_tensor(name + "_dram", a.shape, mybir.dt.from_np(a.dtype), kind="ExternalInput").ap()
    out = nc.dram_tensor("out_dram", (1, SEQ, D), mybir.dt.float32, kind="ExternalOutput").ap()
    build(nc, tensors, out)
    r = run_bass_kernel_spmd(nc, [arrays], core_ids=[0])
    return r.results[0]["out_dram"]
```

```python
import math
from collections import Counter

import numpy as np
import concourse.bass as bass
from concourse import mybir

D = 1024
SEQ = 512
MEM = 256
FF = 2816
DEPTH = 2
assert (DEPTH + 1) // 2 == 1
P = 128
KT = D // P
TT = SEQ // P
MT = MEM // P
EPS = 1e-6
GC = 512
PK = 2
RAW_SLOTS = 4
SPLIT_SLOTS = 4
LOOKAHEAD = 3
HEAD = 128
FOX_HEADS = 8
CONV_W = 31
CONV_T = 4
FF_PASSES = ((0, 6), (6, 5))
NEG = -1e30

FFN_PRE, FFN_POST, MIX_PRE, MIX_POST, X_PRE, X_POST = 0, 32, 64, 80, 96, 112
MEM_G, HGRN_G, DIFF_G, CONV_B, LN_G, LN_B, CONV_TAPS = 128, 144, 148, 152, 156, 160, 164
N_VEC = CONV_TAPS + CONV_W * CONV_T


def stages():
    out = []

    def ffn(l, j):
        for n, (g0, ng) in enumerate(FF_PASSES):
            out.append(("gate_up", l, (j, n), ng, KT // PK))
            out.append(("down", l, (j, n), 2, ng))
    for l in range(DEPTH):
        ffn(l, 0)
        out.append(("even_in", l, None, 7, 4) if l % 2 == 0 else ("odd_in", l, None, 6, 4))
        out.append(("mix_out", l, None, 2, 4))
        out.append(("kv", l, None, 4, 4))
        out.append(("xq", l, None, 2, 4))
        out.append(("xo", l, None, 2, 4))
        ffn(l, 1)
    return out


EVEN_COLS = [("a_f", 512), ("a_q", 0), ("a_g", 1536), ("a_i", 1024), ("b_q", 2048), ("b_k", 2560), ("b_v", 3072)]
ODD_COLS = [("d_a", 1544), ("d_g", 2056), ("c_f", 1536), ("c_q", 0), ("c_k", 512), ("c_v", 1024)]
TOKEN_MAJOR = ("a_i", "b_v", "c_v")

DIFF_STEPS = [(h, b) for h in range(4) for b in range(TT)]
FOX_STEPS = [(h, b) for h in range(4) for b in range(TT)]
X_STEPS = [(h, b) for h in range(2) for b in range(TT)]
LEVELS = [64, 32, 16, 8, 4, 2, 1]
CROSS = [(1, 0), (2, 1), (3, 2), (2, 0), (3, 1), (3, 0)]


def build(nc, A, out):
    f32, f32r, bf16, i8 = mybir.dt.float32, mybir.dt.float32r, mybir.dt.bfloat16, mybir.dt.int8
    ALU, ACT, AX = mybir.AluOpType, mybir.ActivationFunctionType, mybir.AxisListType
    MUL, ADD, SUB = ALU.mult, ALU.add, ALU.subtract
    LAM_INIT = 0.8 - 0.6 * math.exp(-0.3 * 0)

    FLOAT = 4
    top = [(int(nc.sbuf_base) + 511) // 512 * 512]

    def place(name, shape, dt=f32, at=None, size=FLOAT):
        n = (int(np.prod(shape[1:])) * size + 31) // 32 * 32
        if at is None:
            at = top[0]
            top[0] += n
        assert at + n <= nc.sbuf_usable_end, (name, at + n - nc.sbuf_usable_end)
        return nc.alloc_sbuf_tensor_at(name, shape, dt, offset=at)

    NB = 4 * SEQ
    h = place("h", [P, KT, SEQ])
    y_at = top[0]
    y = place("y", [P, KT, SEQ])
    x_at = top[0]
    xhi = place("xhi", [P, KT, SEQ], f32r)
    xlo = place("xlo", [P, KT, SEQ], f32r)
    raw = place("raw", [P, RAW_SLOTS, PK, GC])
    whi = place("whi", [P, SPLIT_SLOTS, PK, GC], f32r)
    wlo = place("wlo", [P, SPLIT_SLOTS, PK, GC], f32r)
    memT = place("memT", [P, KT, MEM])
    ring_at = top[0]
    ring = place("ring", [P, 4, SEQ])
    rsb = place("rsb", [P, SEQ])
    diag = place("diag", [P, TT, P])
    ident = place("ident", [P, P])
    ones = place("ones", [P, P])
    vec = place("vec", [P, N_VEC])
    neg_half = place("neg_half", [P, 16])
    var = place("var", [P, 16])
    rstd = place("rstd", [P, 16])
    rstd_in = place("rstd_in", [P, TT])
    negmax = place("negmax", [P, 2, 2])
    rowsum = place("rowsum", [P, 2, 2])
    recip = place("recip", [P, 2, 2])
    lam = place("lam", [P, 8])
    tile_decay = place("tile_decay", [P, 4, TT])
    fbias = place("fbias", [FOX_HEADS, 8])
    head_sel = place("head_sel", [FOX_HEADS, FOX_HEADS, P], f32r)
    ident_bf = place("ident_bf", [P, P], bf16, size=2)
    causal_neg = place("causal_neg", [P, P], bf16, size=2)
    level_mask = place("level_mask", [P, len(LEVELS) + 1, P], i8, size=1)
    w_at = top[0]
    at = lambda n: w_at + n * FLOAT
    mem_in = place("mem_in", [P, MT, D], f32, at(0))
    mem_sq = place("mem_sq", [P, D], f32, at(2048))
    rows = place("rows", [P, 3, P], f32, at(3072))
    lam_in = place("lam_in", [P, 4, 64], f32, at(3456))
    level_f = place("level_f", [P, P], f32, at(3712))
    head_sel_f = place("head_sel_f", [FOX_HEADS, FOX_HEADS, P], f32, at(3840))
    position = place("position", [4, SEQ], f32, at(4864))
    slope = place("slope", [4, 8], f32, at(5376))
    x_in = place("x_in", [P, TT, D], f32, y_at)
    square_sum = place("square_sum", [P, SEQ], f32, at(7 * NB + SEQ))
    mid_hi = place("mid_hi", [P, 12, SEQ], f32r, at(0))
    mid_lo = place("mid_lo", [P, 12, SEQ], f32r, at(6144))
    gate = place("gate", [P, 2, SEQ], f32, at(12288))
    up = place("up", [P, 2, SEQ], f32, at(13312))
    a_b = place("a_b", [P, 4, SEQ], f32, at(0))
    a_k = place("a_k", [P, 4, SEQ], f32, at(NB))
    a_q = place("a_q", [P, 4, SEQ], f32, at(2 * NB))
    a_g = place("a_g", [P, 4, SEQ], f32, at(3 * NB))
    a_v = place("a_v", [P, TT, SEQ], f32, at(4 * NB))
    b_q = place("b_q", [P, 4, SEQ], f32, at(5 * NB))
    b_k = place("b_k", [P, 4, SEQ], f32, at(6 * NB))
    b_v = place("b_v", [P, TT, SEQ], f32, at(7 * NB))
    alibi = place("alibi", [4, SEQ], f32r, at(8 * NB))
    soft = place("soft", [P, 4, SEQ], f32, y_at)
    logf = place("logf", [P, 4, SEQ], f32, y_at + NB * FLOAT)
    cross = place("cross", [P, 24, P], f32, y_at)
    lv = place("lv", [P, 2, 4 * SEQ], f32, y_at)
    scoresT = place("scoresT", [P, 16, P], f32, ring_at)
    kd2 = place("kd2", [P, 4, 2, P], f32, x_at + 3 * NB * FLOAT)
    kd3 = place("kd3", [P, 4, P], f32, x_at + (3 * NB + 1024) * FLOAT)
    even_probs = place("even_probs", [P, 2, 2, SEQ], f32, at(0)), place("even_probsT", [P, 2 * TT, P], f32, at(NB))
    x_probs = place("probs", [P, 2, 2, SEQ], f32, x_at), place("probsT", [P, 2 * TT, P], f32, x_at + NB * FLOAT)
    U0 = CONV_W - 1
    UN = CONV_T * (U0 + SEQ)
    u = place("u", [P, CONV_T, U0 + SEQ], f32, at(0))
    sg = place("sg", [P, CONV_T, SEQ], f32, at(UN))
    conv = place("conv", [P, CONV_T, SEQ], f32, at(UN + NB))
    c_q = place("c_q", [P, 4, SEQ], f32, at(UN + 2 * NB))
    c_k = place("c_k", [P, 4, SEQ], f32, at(UN + 3 * NB))
    c_v = place("c_v", [P, TT, SEQ], f32, at(UN + 4 * NB))
    c_z = place("c_z", [FOX_HEADS, 3, SEQ], f32, at(UN + 5 * NB))
    cum_hi = place("cum_hi", [FOX_HEADS, SEQ], f32r, at(UN + 5 * NB + 1536))
    cum_lo = place("cum_lo", [FOX_HEADS, SEQ], f32r, at(UN + 5 * NB + 2048))
    m_hi = place("m_hi", [P, KT, MEM], f32r, at(0))
    m_lo = place("m_lo", [P, KT, MEM], f32r, at(NB))
    x_k = place("x_k", [P, KT, MEM], f32, at(2 * NB))
    x_v = place("x_v", [P, MT, D], f32, at(3 * NB))
    x_q = place("x_q", [P, KT, SEQ], f32, at(4 * NB))

    PS = nc.alloc_psum_tensor("ps", [P, 8, 512], f32)
    flat = lambda t: t.rearrange("p a b -> p (a b)")
    blocks_of = lambda b0, b1: PS[:, b0:b1, :].rearrange("p a (b j) -> p (a b) j", j=P)

    def sem(name):
        return nc.alloc_semaphore(name)

    x_loaded, mem_loaded, rows_loaded, small_loaded, stored = map(sem, (
        "x_loaded", "mem_loaded", "rows_loaded", "small_loaded", "stored"))
    raw_full = [sem(f"raw_full{i}") for i in range(RAW_SLOTS)]
    hi_made, lo_made, pieces_used = map(sem, ("hi_made", "lo_made", "pieces_used"))
    bank_free = [sem("even_banks_free"), sem("odd_banks_free")]
    vector_step, scalar_step, pool_step = map(sem, ("vector_step", "scalar_step", "pool_step"))
    consts_ready, tables_ready, vec_ready, mem_squared, mem_scaled, memT_ready, lam_exp = map(sem, (
        "consts_ready", "tables_ready", "vec_ready", "mem_squared", "mem_scaled", "memT_ready", "lam_exp"))
    transposed = sem("transposed")
    h_ready, xhi_ready, xlo_ready, m_hi_ready, m_lo_ready = map(sem, (
        "h_ready", "xhi_ready", "xlo_ready", "m_hi_ready", "m_lo_ready"))
    h_squared, h_added, h_summed, ring_squared, ring_summed = map(sem, (
        "h_squared", "h_added", "h_summed", "ring_squared", "ring_summed"))
    var_ready, rstd_ready, diag_ready, spread_ready, spread_used = map(sem, (
        "var_ready", "rstd_ready", "diag_ready", "spread_ready", "spread_used"))
    gate_scaled, up_scaled, gate_silu, product_ready, mid_hi_ready, mid_lo_ready = map(sem, (
        "gate_scaled", "up_scaled", "gate_silu", "product_ready", "mid_hi_ready", "mid_lo_ready"))
    y_tile_done, y_ready, proj_ready, v_ready, y_mixed = map(sem, ("y_tile_done", "y_ready", "proj_ready", "v_ready", "y_mixed"))
    scores_ready, negmax_ready, exp_done, probs_ready = map(sem, (
        "scores_ready", "negmax_ready", "exp_done", "probs_ready"))
    probsT_ready, probsT_copied, o_ready, o_copied = map(sem, (
        "probsT_ready", "probsT_copied", "o_ready", "o_copied"))
    head_scaled = sem("head_scaled")
    softplus_ready, level_diff, level_exp, level_ready, level_scores, level_merged = map(sem, (
        "softplus_ready", "level_diff", "level_exp", "level_ready", "level_scores", "level_merged"))
    decay_ready, cross_ready, cross_scores, cross_copied, cum_ready, cum_hi_ready, cum_lo_ready = map(sem, (
        "decay_ready", "cross_ready", "cross_scores", "cross_copied", "cum_ready", "cum_hi_ready", "cum_lo_ready"))
    sigmoid_ready, conv_ready, conv_summed, conv_centred, conv_scaled = map(sem, (
        "sigmoid_ready", "conv_ready", "conv_summed", "conv_centred", "conv_scaled"))
    y_silu = sem("y_silu")

    STAGES = stages()
    total_pieces = sum(ng * n for _, _, _, ng, n in STAGES) - 3 * (DEPTH // 2)

    SPREAD_AT = [2, 3, 4, 5, 8, 12]
    HI_AT = [n + 4 for n in SPREAD_AT]
    A_GROUPS = 4

    def b_pieces(n):
        return min(2 + 3 * n // 2, 12)

    def straight(kind, ng):
        return A_GROUPS if kind == "even_in" else ng

    def group_pieces(kind, g, n):
        return 1 if kind == "odd_in" and ODD_COLS[g][0] == "c_f" else n

    def straight_groups(ng):
        return 2 if ng % 2 == 0 else 1

    def column_name(kind, g):
        return {"even_in": EVEN_COLS, "odd_in": ODD_COLS}[kind][g][0] if kind in ("even_in", "odd_in") else ""

    def from_h(kind, arg):
        return kind in ("even_in", "odd_in", "xq") or (kind == "gate_up" and arg[1] == 0)

    def gain_of(kind, l, arg):
        return {"even_in": MIX_PRE, "odd_in": MIX_PRE, "xq": X_PRE}[kind] + l * KT if kind != "gate_up" else \
            FFN_PRE + (2 * l + arg[0]) * KT

    def ends_sublayer(kind, arg):
        return kind in ("mix_out", "xo") or (kind == "down" and arg[1] == 1)

    def post_gain(kind, l, arg):
        return {"mix_out": MIX_POST, "xo": X_POST}[kind] + l * KT if kind != "down" else \
            FFN_POST + (2 * l + arg[0]) * KT

    def diff_block(i):
        return i // TT, i % TT

    class Engine:

        def __init__(self, eng, chain):
            self.eng, self.chain = eng, chain
            self.made, self.seen, self.last = Counter(), Counter(), None
            self.piece = self.group = 0

        def run(self, ins, s=None, n=1):
            s = self.chain if s is None else s
            self.made[s.name] += n
            ins.then_inc(s, n)
            self.last = (s, self.made[s.name])

        def own(self):
            self.eng.wait_ge(*self.last)

        def await_(self, s, n=1):
            self.seen[s.name] += n
            self.eng.wait_ge(s, self.seen[s.name])

        def release_banks(self):
            self.eng.wait_ge(*self.last).then_inc(bank_free[self.group % 2], 1)

        def group_done(self):
            self.eng.wait_ge(pieces_used, self.piece + SPLIT_SLOTS)

    block_ctx = nc.Block()
    block = block_ctx.__enter__()

    @block.sync
    def _(sp):
        sp.dma_start(x_in[:], A["x"][0].rearrange("(t p) d -> p t d", p=P)).then_inc(x_loaded, 16)
        r = 0
        for name in ("ffn_norm_pre", "ffn_norm_post", "mix_norm_pre", "mix_norm_post",
                     "xattn_norm_pre", "xattn_norm_post"):
            src = A[name]
            src = src.rearrange("l j (k p) -> (l j k) p", p=P) if len(src.shape) == 3 else \
                src.rearrange("l (k p) -> (l k) p", p=P)
            sp.dma_start(rows[r:r + src.shape[0], 0, :], src).then_inc(rows_loaded, 16)
            r += src.shape[0]
        r = 0
        for name in ("mem_norm_g", "hgrn_norm_g", "diff_norm_g", "conv_b", "conv_ln_g", "conv_ln_b"):
            src = A[name].rearrange("l (k p) -> (l k) p", p=P)
            sp.dma_start(rows[r:r + src.shape[0], 1, :], src).then_inc(rows_loaded, 16)
            r += src.shape[0]
        sp.dma_start(rows[0:CONV_W * CONV_T, 2, :],
                     A["conv_w"][0].rearrange("w (c p) -> (w c) p", p=P)).then_inc(rows_loaded, 16)
        sp.dma_start(mem_in[:], A["mem"][0].rearrange("(t p) d -> p t d", p=P)).then_inc(mem_loaded, 16)
        sp.dma_start(lam_in[:], A["diff_lambda"].broadcast_to([P, 4, 64])).then_inc(small_loaded, 16)
        with nc.allow_non_contiguous_dma("eight biases, one to a partition"):
            sp.dma_start(fbias[:, 0:1], A["fox_f_bias"].rearrange("o h -> h o")).then_inc(small_loaded, 16)

        def load(base, g, halves):
            slot = base % RAW_SLOTS
            sp.wait_ge(lo_made, base + 1 + 4 * g)
            for dst, src in halves(slot):
                sp.dma_start(dst, src).then_inc(raw_full[slot], 16)

        def two_rows(w, k0, c0):
            def halves(slot):
                for i in range(2):
                    yield raw[:, slot, i, :], w[(k0 + i) * P:(k0 + i + 1) * P, c0:c0 + GC]
            return halves

        def gate_and_up(l, j, kp, c0):
            def halves(slot):
                for i, name in enumerate(("ffn_w_gate", "ffn_w_up")):
                    w = A[name][l, j].rearrange("(k p) n -> p k n", p=P)
                    yield raw[:, slot, :, i * 256:(i + 1) * 256], w[:, 2 * kp:2 * kp + 2, bass.ds(c0, 256)]
            return halves

        def forget_rows(w, c0):
            def halves(slot):
                dst = raw[:, slot].rearrange("p a (b n) -> p (a b) n", n=P)
                src = w.rearrange("(k p) n -> p k n", p=P)
                for i in range(2):
                    yield dst[:, 4 * i:4 * i + 4, :], src[:, 4 * i:4 * i + 4, c0:c0 + P]
            return halves

        piece = 0
        for kind, l, arg, ng, np_ in STAGES:
            if kind == "gate_up":
                j, n = arg
                first = straight_groups(ng)
                g0 = FF_PASSES[n][0]
                for g in range(first):
                    for kp in range(4):
                        load(piece + 4 * g + kp, 0, gate_and_up(l, j, kp, (g0 + g) * 256))
                with sp.Fori(0, (ng - first) // 2) as i:
                    for q in range(2):
                        for kp in range(4):
                            load(piece + 4 * (first + q) + kp, 2 * i,
                                 gate_and_up(l, j, kp, (g0 + first + q) * 256 + i * 512))
                piece += 4 * ng
                continue
            for g in range(ng):
                for kp in range(group_pieces(kind, g, np_)):
                    if kind == "down":
                        j, n = arg
                        src = two_rows(A["ffn_w_down"][l, j], 2 * FF_PASSES[n][0] + 2 * kp, g * GC)
                    elif kind == "even_in":
                        src = two_rows(A["even_w_in"][l // 2], 2 * kp, EVEN_COLS[g][1])
                    elif kind == "odd_in":
                        name, c0 = ODD_COLS[g]
                        w = A["odd_w_in"][l // 2]
                        src = forget_rows(w, c0) if name == "c_f" else two_rows(w, 2 * kp, c0)
                    else:
                        w = {"mix_out": A["even_w_out" if l % 2 == 0 else "odd_w_out"][l // 2],
                             "kv": A["xattn_w_kv"][l], "xq": A["xattn_w_q"][l], "xo": A["xattn_w_o"][l]}[kind]
                        src = two_rows(w, 2 * kp, g * GC)
                    load(piece, 0, src)
                    piece += 1
        assert piece == total_pieces
        for t in range(TT):
            sp.wait_ge(y_mixed, KT + 2 * (t + 1))
            sp.dma_start(out[0, t * P:(t + 1) * P, :], x_in[:, t, :]).then_inc(stored, 16)
        sp.wait_ge(stored, 16 * TT)

    @block.gpsimd
    def _(pool):
        E = Engine(pool, pool_step)
        g = nc.gpsimd

        def on_diagonal(t, pattern):
            E.run(g.memset(t, 0.0))
            E.own()
            E.run(g.affine_select(out=t, in_=t, compare_op=ALU.not_equal, fill=1.0, base=0,
                                  pattern=pattern, channel_multiplier=1))
        E.run(g.memset(ones[:], 1.0))
        E.run(g.memset(neg_half[:], -0.5))
        on_diagonal(ident[:], [[-1, P]])
        E.own()
        pool.wait_ge(*E.last).then_inc(consts_ready, 1)
        on_diagonal(head_sel_f[:], [[-1, FOX_HEADS], [0, P]])
        on_diagonal(ident_bf[:], [[-1, P]])
        E.run(g.iota(position[:], pattern=[[1, SEQ]], base=0, channel_multiplier=0,
                     allow_small_or_imprecise_dtypes=True))
        E.run(g.memset(slope[:], 0.0))
        for n in range(4):
            E.own()
            E.run(g.affine_select(out=slope[:], in_=slope[:], compare_op=ALU.not_equal, base=-n,
                                  fill=8.0 * 2.0 ** (-8.0 * (n + 1) / 4), pattern=[[0, 8]], channel_multiplier=1))
        E.run(g.memset(causal_neg[:], 0.0))
        E.own()
        E.run(g.affine_select(out=causal_neg[:], in_=causal_neg[:], compare_op=ALU.is_ge, fill=NEG, base=0,
                              pattern=[[-1, P]], channel_multiplier=1))
        for n, L in enumerate(LEVELS):
            m = level_f[:].rearrange("p (b r j) -> p b r j", r=2, j=L)
            nb = P // (2 * L)
            E.run(g.memset(level_f[:], 1.0))
            for base, ch, pat in ((0, 1, [[-2 * L, nb], [0, 2], [0, L]]),
                                  (L - 1, -1, [[2 * L, nb], [0, 2], [0, L]]),
                                  (-1, 0, [[0, nb], [1, 2], [0, L]])):
                E.own()
                E.run(g.affine_select(out=m, in_=m, compare_op=ALU.is_ge, fill=0.0, base=base,
                                      pattern=pat, channel_multiplier=ch))
            E.own()
            E.run(g.tensor_copy(level_mask[:, n, :], level_f[:]))
            E.own()
        E.run(g.tensor_copy(level_mask[:, len(LEVELS), :], ident[:]), tables_ready)

        def power(n):
            E.await_(var_ready)
            E.run(g.tensor_tensor(rstd[:, 0:n], var[:, 0:n], neg_half[:, 0:n], ALU.pow), rstd_ready)

        power(MT)
        def add_input_squares():
            E.await_(h_squared)
            for k in range(1, KT):
                E.await_(h_squared)
                if k > 1:
                    E.own()
                E.run(g.tensor_tensor(y[:, 0, :], y[:, 0, :], y[:, k, :], ADD), h_added)

        def add_result_squares():
            n = E.made[ring_summed.name]
            E.await_(ring_squared)
            for k in range(1, KT - 1):
                E.await_(ring_squared)
                first = ring[:, n % 4, :] if k == 1 else square_sum[:]
                if k > 1:
                    E.own()
                E.run(g.tensor_tensor(square_sum[:], first, ring[:, (n + k) % 4, :], ADD), ring_summed,
                      2 if k == 1 else 1)
            E.made[ring_summed.name] += 1
            E.seen[ring_squared.name] += 1

        products = 0
        for kind, l, arg, ng, np_ in STAGES:
            if from_h(kind, arg):
                add_input_squares()
                power(TT)
            if kind == "gate_up":
                def multiply(n):
                    pool.wait_ge(gate_silu, n)
                    pool.wait_ge(up_scaled, n)
                    g.tensor_tensor(up[:], gate[:], up[:], MUL).then_inc(product_ready, 1)
                first = straight_groups(ng)
                for q in range(first):
                    multiply(products + q + 1)
                with pool.Fori(0, (ng - first) // 2) as i:
                    for q in range(2):
                        multiply(products + first + q + 1 + 2 * i)
                products += ng
            elif kind == "even_in":
                power(16)
                power(TT)
                power(TT)
                power(2 * TT)
                E.made[ring_summed.name] += KT
                E.seen[ring_squared.name] += KT
            elif kind == "odd_in":
                power(TT)
                E.made[ring_summed.name] += CONV_T
                E.seen[ring_squared.name] += CONV_T
            elif ends_sublayer(kind, arg):
                add_result_squares()
                power(TT)

    @block.scalar
    def _(act):
        E = Engine(act, scalar_step)
        a = nc.scalar.activation

        def split(base, g=0):
            slot = base % RAW_SLOTS
            act.wait_ge(raw_full[slot], 32 * (base // RAW_SLOTS + 1) + 32 * g)
            act.wait_ge(pieces_used, base + 1 + 4 * g)
            a(flat(whi[:, slot]), flat(raw[:, slot]), ACT.Copy).then_inc(hi_made, 1)

        def split_next():
            if E.piece + LOOKAHEAD < total_pieces:
                split(E.piece + LOOKAHEAD)
            E.piece += 1

        def open_input(gain):
            for k in range(KT):
                E.await_(h_ready)
                E.run(a(xhi[:, k, :], h[:, k, :], ACT.Copy, scale=vec[:, gain + k:gain + k + 1]), xhi_ready)
                E.run(a(y[:, k, :], h[:, k, :], ACT.Square), h_squared)
            split(E.piece + LOOKAHEAD)

        def square_into_ring(src):
            n = E.made[ring_squared.name]
            if n >= 4:
                act.wait_ge(ring_summed, n - 3)
            E.run(a(ring[:, n % 4, :], src, ACT.Square), ring_squared)

        def input_hi(k, ready=None):
            if ready is not None:
                E.await_(ready)
            E.run(a(xhi[:, k, :], y[:, k, :], ACT.Copy), xhi_ready)

        def input_from_y():
            for k in range(KT):
                input_hi(k)

        def memory_input(l):
            for k in range(KT):
                E.run(a(m_hi[:, k, :], memT[:, k, :], ACT.Copy,
                        scale=vec[:, MEM_G + l * KT + k:MEM_G + l * KT + k + 1]), m_hi_ready)

        def attention(n_steps, nk_of, scale, n_blocks, o_copy, buffers=x_probs, meanwhile=None):
            probs, probsT = buffers
            t0, o0 = E.seen[probsT_ready.name], E.seen[o_ready.name]
            for i in range(n_steps + 2):
                if i < n_steps:
                    E.await_(negmax_ready)
                    if i >= 2:
                        act.wait_ge(probsT_ready, t0 + i - 1)
                    nk = nk_of(i)
                    for m in range(2):
                        E.run(a(probs[:, i % 2, m, 0:nk], PS[:, 2 * (i % 2) + m, 0:nk], ACT.Exp,
                                bias=negmax[:, i % 2, m:m + 1], scale=scale,
                                accum_out=rowsum[:, i % 2, m:m + 1]), exp_done)
                if 1 <= i <= n_steps:
                    E.await_(probsT_ready)
                    if i >= 2:
                        act.wait_ge(o_ready, o0 + i - 1)
                    n = n_blocks(i - 1)
                    E.run(a(probsT[:, 0:n, :], blocks_of(4, 6)[:, 0:n, :], ACT.Copy), probsT_copied)
                if i >= 2:
                    E.await_(o_ready)
                    dst, src = o_copy(i - 2)
                    E.run(a(dst, src, ACT.Copy), o_copied)
                if meanwhile is not None:
                    meanwhile(i)

        act.wait_ge(mem_loaded, 16)
        for t in range(MT):
            if t:
                E.own()
            E.run(a(mem_sq[:], mem_in[:, t, :], ACT.Square, accum_out=lam[:, 4 + t:5 + t]), mem_squared)
        E.await_(lam_exp)
        E.run(a(lam[:, 2:4], lam[:, 0:2], ACT.Exp), mem_squared)
        E.await_(vec_ready)
        for p in range(LOOKAHEAD):
            split(p)

        mids = 0
        for kind, l, arg, ng, np_ in STAGES:
            base_piece = E.piece
            early = from_h(kind, arg)
            if early and kind != "xq":
                open_input(gain_of(kind, l, arg))
            if kind == "mix_out":
                memory_input(l)
            if kind == "kv":
                open_input(gain_of("xq", l, None))
                early = True
            if kind == "xq":
                early = False

            if kind == "gate_up":
                def body(base, g, n, tile, skip_split=False):
                    for kp in range(4):
                        if not (skip_split and kp == 0):
                            split(base + kp + LOOKAHEAD, g)
                    act.wait_ge(gate_scaled, n)
                    a(gate[:], gate[:], ACT.Silu).then_inc(gate_silu, 1)
                    act.wait_ge(product_ready, n)
                    a(mid_hi[:, tile, :], up[:], ACT.Copy).then_inc(mid_hi_ready, 1)

                first = straight_groups(ng)
                for q in range(first):
                    body(base_piece + 4 * q, 0, mids + q + 1, slice(2 * q, 2 * q + 2), early and q == 0)
                with act.Fori(0, (ng - first) // 2) as i:
                    for q in range(2):
                        body(base_piece + 4 * (first + q), 2 * i, mids + first + q + 1 + 2 * i,
                             bass.ds(2 * (first + q) + 4 * i, 2))
                mids += ng
                E.made[mid_hi_ready.name] = mids
                E.last = (mid_hi_ready, mids)
                E.piece += 4 * ng
                E.group += ng
                continue

            for g in range(straight(kind, ng)):
                for kp in range(group_pieces(kind, g, np_)):
                    if early and g == 0 and kp == 0:
                        E.piece += 1
                    else:
                        split_next()
                bank = 4 * (E.group % 2)
                name = column_name(kind, g)
                if kind in ("mix_out", "xo", "down"):
                    if ends_sublayer(kind, arg):
                        for c in range(4):
                            E.await_(y_ready)
                            square_into_ring(y[:, 4 * g + c, :])
                    else:
                        E.seen[y_ready.name] += 4
                elif name in TOKEN_MAJOR:
                    dst = {"a_i": a_v, "b_v": b_v, "c_v": c_v}[name]
                    E.group_done()
                    for t in range(TT):
                        E.run(a(dst[:, t, :], PS[:, bank + t, :], ACT.Copy, scale=rstd_in[:, t:t + 1]), v_ready)
                    E.release_banks()
                elif kind == "kv" and g >= 2:
                    E.group_done()
                    E.run(a(x_v[:, :, (g - 2) * GC:(g - 1) * GC], PS[:, bank:bank + MT, :], ACT.Copy), v_ready)
                    E.release_banks()
                else:
                    E.await_(proj_ready)
                    if name == "a_f":
                        E.run(a(a_k[:], a_b[:], ACT.Sigmoid, scale=-1.0))
                        E.run(a(soft[:], a_b[:], ACT.Abs))
                        E.own()
                        E.run(a(soft[:], soft[:], ACT.Exp, scale=-1.0))
                        E.own()
                        E.run(a(soft[:], soft[:], ACT.Ln, bias=ones[:, 0:1]), softplus_ready)
                    elif name == "a_g":
                        E.run(a(a_g[:], a_g[:], ACT.Silu))
                    elif name == "d_g":
                        E.run(a(sg[:], sg[:], ACT.Sigmoid), sigmoid_ready)
                    elif name == "c_f":
                        E.run(a(c_z[:, 1, :], c_z[:, 0, :], ACT.Abs))
                        E.own()
                        E.run(a(c_z[:, 1, :], c_z[:, 1, :], ACT.Exp, scale=-1.0))
                        E.own()
                        E.run(a(c_z[:, 1, :], c_z[:, 1, :], ACT.Ln, bias=ones[0:FOX_HEADS, 0:1]), softplus_ready)
                        E.await_(cum_ready)
                        E.run(a(cum_hi[:], c_z[:, 0, :], ACT.Copy), cum_hi_ready)
                E.group += 1

            if kind == "even_in":
                base, done = E.piece, LOOKAHEAD
                b_bank = 4 * (E.group % 2)

                def split_to(done, n):
                    for p in range(done, n):
                        split(base + p)
                    return n
                for n in range(len(LEVELS) + 1):
                    if n < len(LEVELS):
                        E.await_(level_diff)
                        E.run(a(lv[:, n % 2, :], lv[:, n % 2, :], ACT.Exp), level_exp)
                    done = split_to(done, b_pieces(n) + LOOKAHEAD)
                done = split_to(done, 12 + LOOKAHEAD)
                E.piece += 12
                E.group_done()
                E.group += 2
                E.await_(proj_ready, 2)
                for t in range(TT):
                    E.run(a(b_v[:, t, :], PS[:, b_bank + t, :], ACT.Copy, scale=rstd_in[:, t:t + 1]), v_ready)
                E.release_banks()
                E.group += 1
                act.wait_ge(level_scores, 2 * len(LEVELS))
                E.run(a(lv[:, 0, :], flat(a_b[:]), ACT.Exp), decay_ready)
                E.run(a(tile_decay[:], a_b[:].rearrange("p h (t j) -> p h t j", j=P)[:, :, :, P - 1], ACT.Exp),
                      decay_ready)
                E.await_(level_diff)
                E.run(a(lv[:, 1, :], lv[:, 1, :], ACT.Exp), decay_ready)
                E.await_(cross_scores)
                E.run(a(cross[:], blocks_of(0, 6), ACT.Copy), cross_copied)
                E.await_(o_ready)
                E.run(a(y[:, 0:4, :], PS[:, 0:4, :], ACT.Copy), o_copied)
                E.own()
                for k in range(4):
                    square_into_ring(y[:, k, :])

                def meanwhile(i):
                    if i >= TT + 1 and (i - TT - 1) % TT == 0:
                        E.own()
                        square_into_ring(y[:, 4 + (i - TT - 1) // TT, :])
                    if i in HI_AT:
                        input_hi(HI_AT.index(i), y_mixed)
                attention(16, lambda i: (i % TT + 1) * P, 0.125, lambda i: i % TT + 1,
                          lambda i: (y[:, 4 + i // TT, i % TT * P:(i % TT + 1) * P], PS[:, 6 + i % 2, 0:P]),
                          even_probs, meanwhile)
                for k in range(len(HI_AT), KT):
                    input_hi(k, y_mixed)
            if kind == "odd_in":
                attention(16, lambda i: (i % TT + 1) * P, 0.125, lambda i: 2 * (i % TT + 1),
                          lambda i: (y[:, i // TT, i % TT * P:(i % TT + 1) * P], PS[:, 6 + i % 2, 0:P]))
                for c in range(CONV_T):
                    E.await_(conv_centred)
                    square_into_ring(conv[:, c, :])
                for c in range(CONV_T):
                    E.await_(conv_scaled)
                    E.run(a(y[:, 4 + c, :], conv[:, c, :], ACT.Silu, scale=vec[:, LN_G + c:LN_G + c + 1],
                            bias=vec[:, LN_B + c:LN_B + c + 1]), y_silu)
                E.own()
                input_from_y()
            if kind == "xq":
                attention(8, lambda i: MEM, 0.0625, lambda i: 2 * MT,
                          lambda i: (y[:, 4 * (i // TT):4 * (i // TT) + 4, i % TT * P:(i % TT + 1) * P],
                                     PS[:, 6 + i % 2, :].rearrange("p (a j) -> p a j", j=P)))
                E.own()
                input_from_y()

    @block.vector
    def _(dve):
        E = Engine(dve, vector_step)
        v = nc.vector

        def split(base, g=0):
            slot = base % RAW_SLOTS
            dve.wait_ge(hi_made, base + 1 + 4 * g)
            v.tensor_tensor(flat(wlo[:, slot]), flat(raw[:, slot]), flat(whi[:, slot]).bitcast(f32),
                            SUB).then_inc(lo_made, 1)

        def split_next():
            if E.piece + LOOKAHEAD < total_pieces:
                split(E.piece + LOOKAHEAD)
            E.piece += 1

        def make_diag(cols):
            E.run(v.tensor_tensor(diag[:], ident[:].unsqueeze(1).broadcast_to([P, TT, P]),
                                  cols.unsqueeze(2).broadcast_to([P, TT, P]), MUL), diag_ready)

        def variance(src, n, cols):
            E.run(v.tensor_scalar(var[:, 0:cols], src, 1.0 / n, EPS, MUL, ADD), var_ready)

        def input_stats(bank):
            E.await_(h_summed)
            variance(PS[:, bank, 0:TT], D, TT)
            E.await_(rstd_ready)
            E.run(v.tensor_copy(rstd_in[:], rstd[:, 0:TT]))
            make_diag(rstd[:, 0:TT])

        def input_spread(bank):
            E.await_(spread_ready)
            E.run(v.tensor_copy(rsb[:], PS[:, bank + 1, :]), spread_used)
            E.own()

        def input_lo(k, gain=None):
            E.await_(xhi_ready)
            if gain is None:
                E.run(v.tensor_tensor(xlo[:, k, :], y[:, k, :], xhi[:, k, :].bitcast(f32), SUB), xlo_ready)
            else:
                E.run(v.scalar_tensor_tensor(out=xlo[:, k, :], in0=h[:, k, :], scalar=vec[:, gain + k:gain + k + 1],
                                             in1=xhi[:, k, :].bitcast(f32), op0=MUL, op1=SUB), xlo_ready)

        def memory_lo(l):
            for k in range(KT):
                E.await_(m_hi_ready)
                c = MEM_G + l * KT + k
                E.run(v.scalar_tensor_tensor(out=m_lo[:, k, :], in0=memT[:, k, :], scalar=vec[:, c:c + 1],
                                             in1=m_hi[:, k, :].bitcast(f32), op0=MUL, op1=SUB), m_lo_ready)

        def close_sublayer(kind, l, arg, bank, next_gain):
            E.await_(ring_summed, 8)
            variance(PS[:, bank, 0:TT], D, TT)
            E.await_(rstd_ready)
            make_diag(rstd[:, 0:TT])
            E.await_(spread_ready)
            gain = post_gain(kind, l, arg)
            for k in range(KT):
                s = spread_used if k == KT - 1 else None
                E.run(v.tensor_tensor(y[:, k, :], y[:, k, :], PS[:, (bank + 5) % 8, :], MUL), s)
                E.own()
                E.run(v.scalar_tensor_tensor(out=h[:, k, :], in0=y[:, k, :], scalar=vec[:, gain + k:gain + k + 1],
                                             in1=h[:, k, :], op0=MUL, op1=ADD), h_ready)
                if k >= 1 and next_gain is not None:
                    input_lo(k - 1, next_gain)
            if next_gain is not None:
                input_lo(KT - 1, next_gain)

        def attention(n_steps, nk_of, scale, differential, buffers=x_probs, meanwhile=None):
            probs, _ = buffers
            for i in range(n_steps + 1):
                if i < n_steps:
                    E.await_(scores_ready)
                    nk = nk_of(i)
                    E.run(v.tensor_reduce(out=negmax[:, i % 2, :], in_=PS[:, 2 * (i % 2):2 * (i % 2) + 2, 0:nk],
                                          axis=AX.X, op=ALU.max, negate=True))
                    E.own()
                    E.run(v.tensor_scalar(negmax[:, i % 2, :], negmax[:, i % 2, :], scale, None, MUL), negmax_ready)
                if meanwhile is not None:
                    meanwhile(i)
                if i >= 1:
                    j = (i - 1) % 2
                    nk = nk_of(i - 1)
                    E.await_(exp_done, 2)
                    E.run(v.reciprocal(recip[:, j, :], rowsum[:, j, :]))
                    E.own()
                    p0, p1 = probs[:, j, 0, 0:nk], probs[:, j, 1, 0:nk]
                    if differential:
                        E.run(v.tensor_scalar(p1, p1, recip[:, j, 1:2], lam[:, 6:7], MUL, MUL))
                        E.own()
                        E.run(v.scalar_tensor_tensor(out=p0, in0=p0, scalar=recip[:, j, 0:1], in1=p1,
                                                     op0=MUL, op1=ADD), probs_ready)
                    else:
                        E.run(v.tensor_scalar(p0, p0, recip[:, j, 0:1], None, MUL), probs_ready)
                        E.run(v.tensor_scalar(p1, p1, recip[:, j, 1:2], None, MUL), probs_ready)

        dve.wait_ge(small_loaded, 32)
        E.run(v.tensor_tensor(lam_in[:, 0:4:2, :], lam_in[:, 0:4:2, :], lam_in[:, 1:4:2, :], MUL))
        E.own()
        E.run(v.tensor_reduce(out=lam[:, 0:2], in_=lam_in[:, 0:4:2, :], axis=AX.X, op=ADD), lam_exp)
        for k in range(KT):
            E.await_(transposed)
            E.run(v.tensor_copy(h[:, k, :], PS[:, k, :]), h_ready)
        E.await_(transposed)
        E.run(v.tensor_copy(vec[:], PS[:, 0, 0:N_VEC]))
        E.own()
        E.run(v.tensor_scalar(vec[:, FFN_POST:FFN_POST + 32], vec[:, FFN_POST:FFN_POST + 32], 0.5, None, MUL))
        E.run(v.tensor_scalar(vec[:, DIFF_G:DIFF_G + 4], vec[:, DIFF_G:DIFF_G + 4], 1.0 - LAM_INIT, None, MUL),
              vec_ready)
        E.await_(mem_squared, 3)
        E.run(v.tensor_scalar(var[:, 0:MT], lam[:, 4:6], 1.0 / D, EPS, MUL, ADD), var_ready)
        E.run(v.tensor_tensor(lam[:, 7:8], lam[:, 3:4], lam[:, 2:3], SUB))
        E.own()
        E.run(v.tensor_scalar(lam[:, 6:7], lam[:, 7:8], -LAM_INIT, None, ADD))
        E.await_(rstd_ready)
        for t in range(MT):
            E.run(v.tensor_scalar(mem_in[:, t, :], mem_in[:, t, :], rstd[:, t:t + 1], None, MUL), mem_scaled)
        E.await_(transposed)
        E.run(v.tensor_copy(memT[:].rearrange("p a b -> p (a b)"), flat(PS[:, 4:8, :])), memT_ready)
        E.await_(tables_ready)
        E.run(v.tensor_copy(head_sel[:], head_sel_f[:]))
        E.run(v.tensor_scalar(alibi[:], position[:], slope[:, 0:1], None, MUL))
        E.own()
        dve.wait_ge(*E.last).then_inc(lo_made, RAW_SLOTS)

        def conv_steps():
            for c in range(CONV_T):
                for w in range(CONV_W):
                    tap = vec[:, CONV_TAPS + CONV_T * w + c:CONV_TAPS + CONV_T * w + c + 1]
                    if w == 0:
                        E.run(v.tensor_scalar(conv[:, c, :], u[:, c, 0:SEQ], tap,
                                              vec[:, CONV_B + c:CONV_B + c + 1], MUL, ADD))
                    else:
                        E.own()
                        E.run(v.scalar_tensor_tensor(out=conv[:, c, :], in0=u[:, c, w:w + SEQ], scalar=tap,
                                                     in1=conv[:, c, :], op0=MUL, op1=ADD),
                              conv_ready if w == CONV_W - 1 else None)
                    yield

        conv_left = conv_steps()

        def convolve(n):
            for _ in range(n):
                next(conv_left, None)

        for p in range(LOOKAHEAD):
            split(p)
        for k in range(KT):
            input_lo(k, FFN_PRE)

        mids = 0
        for n_stage, (kind, l, arg, ng, np_) in enumerate(STAGES):
            base_piece = E.piece
            stats = from_h(kind, arg)
            other = 4 * ((E.group + 1) % 2)
            if kind == "gate_up":
                def body(base, g, n, tile, with_stats=False, bank=0):
                    for kp in range(4):
                        split(base + kp + LOOKAHEAD, g)
                        if kp == 0 and with_stats:
                            input_stats(other)
                    if with_stats:
                        input_spread(other)
                    dve.wait_ge(pieces_used, base + 4 + SPLIT_SLOTS + 4 * g)
                    started = not isinstance(n, int) or n > 1
                    if started:
                        dve.wait_ge(product_ready, n - 1)
                    v.tensor_tensor(gate[:], PS[:, bank:bank + 2, :],
                                    rsb[:].unsqueeze(1).broadcast_to([P, 2, SEQ]), MUL).then_inc(gate_scaled, 1)
                    if started:
                        dve.wait_ge(mid_lo_ready, n - 1)
                    v.tensor_tensor(up[:], PS[:, bank + 2:bank + 4, :],
                                    rsb[:].unsqueeze(1).broadcast_to([P, 2, SEQ]), MUL).then_inc(up_scaled, 1)
                    dve.wait_ge(up_scaled, n).then_inc(bank_free[bank // 4], 1)
                    dve.wait_ge(mid_hi_ready, n)
                    v.tensor_tensor(mid_lo[:, tile, :], up[:], mid_hi[:, tile, :].bitcast(f32),
                                    SUB).then_inc(mid_lo_ready, 1)

                first = straight_groups(ng)
                for q in range(first):
                    body(base_piece + 4 * q, 0, mids + q + 1, slice(2 * q, 2 * q + 2), stats and q == 0,
                         4 * ((E.group + q) % 2))
                with dve.Fori(0, (ng - first) // 2) as i:
                    for q in range(2):
                        body(base_piece + 4 * (first + q), 2 * i, mids + first + q + 1 + 2 * i,
                             bass.ds(2 * (first + q) + 4 * i, 2), False, 4 * ((E.group + first + q) % 2))
                mids += ng
                E.last = (mid_lo_ready, mids)
                E.piece += 4 * ng
                E.group += ng
                continue

            if kind == "mix_out":
                memory_lo(l)
            first_bank = 4 * (E.group % 2)
            if kind == "odd_in":
                E.run(v.memset(u[:, :, 0:U0], 0.0))
            for g in range(straight(kind, ng)):
                bank = 4 * (E.group % 2)
                name = column_name(kind, g)
                for kp in range(group_pieces(kind, g, np_)):
                    split_next()
                    if stats and g == 0 and kp == 0:
                        input_stats(other)
                    if kind == "odd_in" and g >= 3:
                        convolve(5)
                if stats and g == 0:
                    input_spread(other)
                if kind in ("down", "mix_out", "xo"):
                    by_tile = ends_sublayer(kind, arg) and g == 1
                    if not by_tile:
                        E.group_done()
                    for c in range(4):
                        k = 4 * g + c
                        if by_tile and c < 3:
                            E.await_(y_tile_done)
                        elif by_tile:
                            E.group_done()
                        if kind == "down" and arg[1] == 1:
                            E.run(v.tensor_tensor(y[:, k, :], PS[:, bank + c, :], y[:, k, :], ADD), y_ready)
                        else:
                            E.run(v.tensor_copy(y[:, k, :], PS[:, bank + c, :]), y_ready)
                    E.release_banks()
                elif name in TOKEN_MAJOR or (kind == "kv" and g >= 2):
                    pass
                elif name == "c_f":
                    E.group_done()
                    E.run(v.tensor_tensor(c_z[:, 0, :], PS[0:FOX_HEADS, bank, :], rsb[0:FOX_HEADS, :], MUL))
                    E.release_banks()
                    E.run(v.tensor_scalar(c_z[:, 0, :], c_z[:, 0, :], fbias[:, 0:1], None, ADD), proj_ready)
                    E.await_(softplus_ready)
                    E.run(v.scalar_tensor_tensor(out=c_z[:, 0, :], in0=c_z[:, 0, :], scalar=0.0,
                                                 in1=c_z[:, 1, :], op0=ALU.min, op1=SUB))
                    E.own()
                    E.run(v.tensor_tensor_scan(c_z[:, 2, :], ones[0:FOX_HEADS, 0:1].broadcast_to([FOX_HEADS, SEQ]),
                                               c_z[:, 0, :], 0.0, MUL, ADD))
                    E.own()
                    E.run(v.tensor_scalar(c_z[:, 0, :], c_z[:, 2, :], -8.0, None, MUL), cum_ready)
                    E.await_(cum_hi_ready)
                    E.run(v.tensor_tensor(cum_lo[:], c_z[:, 0, :], cum_hi[:].bitcast(f32), SUB), cum_lo_ready)
                else:
                    E.group_done()
                    if kind == "kv":
                        E.run(v.tensor_copy(x_k[:, 4 * g:4 * g + 4, :], PS[:, bank:bank + 4, 0:MEM]), proj_ready)
                    else:
                        dst = {"a_f": a_b, "a_q": a_q, "a_g": a_g, "b_q": b_q, "b_k": b_k, "d_g": sg,
                               "c_q": c_q, "c_k": c_k}.get(name)
                        dst = dst[:] if dst is not None else u[:, :, U0:] if name == "d_a" else \
                            x_q[:, 4 * g:4 * g + 4, :]
                        E.run(v.tensor_tensor(dst, PS[:, bank:bank + 4, :],
                                              rsb[:].unsqueeze(1).broadcast_to([P, 4, SEQ]), MUL), proj_ready)
                    E.release_banks()
                    if name == "a_f":
                        E.await_(softplus_ready)
                        E.run(v.scalar_tensor_tensor(out=logf[:], in0=a_b[:], scalar=0.0, in1=soft[:],
                                                     op0=ALU.min, op1=SUB))
                        E.own()
                        for hd in range(4):
                            for t in range(TT):
                                tok = slice(t * P, (t + 1) * P)
                                E.run(v.tensor_tensor_scan(a_b[:, hd, tok], ones[:], logf[:, hd, tok], 0.0, MUL, ADD))
                    if name == "d_g":
                        E.await_(sigmoid_ready)
                        E.run(v.tensor_tensor(u[:, :, U0:], u[:, :, U0:], sg[:], MUL))
                        E.own()
                E.group += 1

            if kind == "even_in":
                E.run(v.memset(scoresT[:], 0.0))
                base, done = E.piece, LOOKAHEAD
                b_bank = 4 * (E.group % 2)
                level_bank = 4 - b_bank

                def split_to(done, n):
                    for p in range(done, n):
                        split(base + p)
                    return n

                def b_group(dst, bank):
                    E.piece += 4
                    E.group_done()
                    E.run(v.tensor_tensor(dst[:], PS[:, bank:bank + 4, :],
                                          rsb[:].unsqueeze(1).broadcast_to([P, 4, SEQ]), MUL), proj_ready)
                    E.release_banks()
                    E.group += 1
                bflat = flat(a_b[:])

                def halves(t, L):
                    t = t.rearrange("p (b r j) -> p b r j", r=2, j=L)
                    return t[:, :, 0, :], t[:, :, 1, :]

                def level_sub(n):
                    L = LEVELS[n]
                    nb = 4 * SEQ // (2 * L)
                    left, right = halves(bflat, L)
                    ref = left[:, :, L - 1:L].broadcast_to([P, nb, L])
                    if n >= 2:
                        dve.wait_ge(level_scores, 2 * (n - 1))
                    dl, dr = halves(lv[:, n % 2, :], L)
                    E.run(v.tensor_tensor(dl, ref, left, SUB))
                    E.run(v.tensor_tensor(dr, right, ref, SUB), level_diff)

                def level_mul(n):
                    L = LEVELS[n]
                    E.await_(level_exp)
                    dl, dr = halves(lv[:, n % 2, :], L)
                    kl, _ = halves(flat(a_k[:]), L)
                    _, qr = halves(flat(a_q[:]), L)
                    E.run(v.tensor_tensor(dl, dl, kl, MUL))
                    E.run(v.tensor_tensor(dr, dr, qr, MUL), level_ready)

                def level_merge(n):
                    for half in range(2):
                        E.await_(level_scores)
                        if n:
                            dve.wait_ge(level_merged, 2 * n - 1 + half)
                        bank = level_bank + 2 * half
                        E.run(v.copy_predicated(scoresT[:, 8 * half:8 * half + 8, :],
                                                level_mask[:, n, :].unsqueeze(1).broadcast_to([P, 8, P]),
                                                blocks_of(bank, bank + 2)), level_merged)

                n_levels = len(LEVELS)
                level_sub(0)
                for n in range(n_levels + 1):
                    if n + 1 < n_levels:
                        level_sub(n + 1)
                    if n < n_levels:
                        level_mul(n)
                    if n >= 1:
                        level_merge(n - 1)
                    done = split_to(done, b_pieces(n) + LOOKAHEAD)
                    for m, dst in ((4, b_q), (8, b_k)):
                        if b_pieces(n) >= m > b_pieces(n - 1):
                            b_group(dst, b_bank)
                level_merge(n_levels)
                done = split_to(done, 12 + LOOKAHEAD)
                E.piece += 4
                E.group_done()
                E.group += 1
                b4 = a_b[:].rearrange("p h (t j) -> p (h t) j", j=P)
                E.run(v.tensor_tensor(lv[:, 1, :].rearrange("p (t j) -> p t j", j=P),
                                      b4[:, :, P - 1:P].broadcast_to([P, 16, P]), b4, SUB), level_diff)
                E.await_(decay_ready, 3)
                E.run(v.tensor_tensor(lv[:, 0, :], lv[:, 0, :], flat(a_q[:]), MUL))
                E.run(v.tensor_tensor(lv[:, 1, :], lv[:, 1, :], flat(a_k[:]), MUL))
                E.own()
                kd = lv[:, 1, :].rearrange("p (h t j) -> p h t j", t=TT, j=P)
                for J in range(2):
                    E.run(v.tensor_tensor(kd2[:, :, J, :], kd[:, :, J, :],
                                          tile_decay[:, :, J + 1:J + 2].broadcast_to([P, 4, P]), MUL))
                E.own()
                E.run(v.tensor_tensor(kd3[:], kd2[:, :, 0, :], tile_decay[:, :, 2:3].broadcast_to([P, 4, P]), MUL),
                      cross_ready)
                def scale_head(k, bank):
                    E.await_(spread_ready)
                    E.run(v.tensor_tensor(y[:, k, :], y[:, k, :], PS[:, bank, :], MUL), head_scaled)
                    E.own()
                    if k < 4:
                        E.run(v.scalar_tensor_tensor(out=y[:, k, :], in0=y[:, k, :],
                                                     scalar=vec[:, HGRN_G + k:HGRN_G + k + 1],
                                                     in1=a_g[:, k, :], op0=MUL, op1=MUL), y_mixed)
                    else:
                        E.run(v.tensor_scalar(y[:, k, :], y[:, k, :], vec[:, DIFF_G + k - 4:DIFF_G + k - 3],
                                              None, MUL), y_mixed)

                def meanwhile(i):
                    if i == 2:
                        E.await_(ring_summed, 4)
                        variance(PS[:, 5, 0:16], HEAD, 16)
                    if i in (8, 12):
                        E.await_(ring_summed)
                        variance(PS[:, 5, 0:TT], HEAD, TT)
                    if i - 2 in SPREAD_AT:
                        scale_head(SPREAD_AT.index(i - 2), 5)
                    if i - 1 in SPREAD_AT:
                        k = SPREAD_AT.index(i - 1)
                        if k == 0 or k >= 4:
                            E.await_(rstd_ready)
                        c = 4 * k if k < 4 else 0
                        make_diag(rstd[:, c:c + 4])
                    if i - 2 in HI_AT:
                        input_lo(HI_AT.index(i - 2))
                attention(16, lambda i: (i % TT + 1) * P, 0.125, True, even_probs, meanwhile)
                for k in range(sum(n + 2 <= 16 for n in HI_AT), len(HI_AT)):
                    input_lo(k)
                other = 4 * ((E.group + 1) % 2)
                E.await_(ring_summed, 2)
                variance(PS[:, other, 0:2 * TT], HEAD, 2 * TT)
                E.await_(rstd_ready)
                for n in range(2):
                    make_diag(rstd[:, TT * n:TT * n + TT])
                    scale_head(6 + n, other + 1 + n)
                for n in range(2):
                    input_lo(6 + n)
            if kind == "odd_in":
                attention(16, lambda i: (i % TT + 1) * P, 0.125, False, x_probs, lambda i: convolve(2))
                convolve(CONV_T * CONV_W)
                E.await_(conv_summed)
                E.run(v.tensor_scalar(var[:, 0:TT], PS[:, 0, 0:TT], 1.0 / (CONV_T * P), None, MUL))
                E.own()
                make_diag(var[:, 0:TT])
                E.await_(spread_ready)
                for c in range(CONV_T):
                    E.run(v.tensor_tensor(conv[:, c, :], conv[:, c, :], PS[:, 1, :], SUB), conv_centred)
                E.await_(ring_summed, 4)
                variance(PS[:, 0, TT:2 * TT], CONV_T * P, TT)
                E.await_(rstd_ready)
                make_diag(rstd[:, 0:TT])
                E.await_(spread_ready)
                for c in range(CONV_T):
                    E.run(v.tensor_tensor(conv[:, c, :], conv[:, c, :], PS[:, 2, :], MUL), conv_scaled)
                for k in range(KT):
                    input_lo(k)
            if kind == "xq":
                attention(8, lambda i: MEM, 0.0625, False)
                for k in range(KT):
                    input_lo(k)
            if ends_sublayer(kind, arg):
                nxt = next(((k2, l2, a2) for k2, l2, a2, _, _ in STAGES[n_stage + 1:] if k2 != "kv"), None)
                close_sublayer(kind, l, arg, first_bank, gain_of(*nxt) if nxt else None)
        for t in range(TT):
            for i in range(2):
                E.await_(transposed)
                E.run(v.tensor_copy(x_in[:, t, i * 512:(i + 1) * 512], PS[:, 2 * t + i, :]), y_mixed)

    @block.tensor
    def _(pe):
        E = Engine(pe, None)
        mm = nc.tensor.matmul

        def three(out_ap, lh, ll, rh, rl, start, stop):
            mm(out_ap, lh, rl, start=start, stop=False)
            mm(out_ap, ll, rh, start=False, stop=False)
            return mm(out_ap, lh, rh, start=False, stop=stop)

        def spread(bank):
            E.await_(diag_ready)
            for t in range(TT):
                last = mm(PS[:, bank, t * P:(t + 1) * P], ones[:], diag[:, t, :], start=True, stop=True)
            E.run(last, spread_ready)

        def column_sums(bank, c0, tile, start, stop):
            for t in range(TT):
                last = mm(PS[:, bank, c0 + t:c0 + t + 1], tile[:, t * P:(t + 1) * P], ones[:, 0:1],
                          start=start and t == 0, stop=stop and t == TT - 1, skip_group_check=True)
            return last

        def square_sums(bank, c0):
            E.await_(ring_squared)
            E.run(column_sums(bank, c0, ring[:, E.made[ring_summed.name] % 4, :], True, True), ring_summed)

        unread = [False, False]

        def wait_banks(group):
            if group >= 2:
                pe.wait_ge(bank_free[group % 2], group // 2)
            if unread[group % 2]:
                E.await_(spread_used)
                unread[group % 2] = False

        def attention(n_steps, qk, blocks, pv, buffers=x_probs, meanwhile=None):
            probs, _ = buffers
            e0, c0, o0 = E.seen[exp_done.name], E.seen[probsT_copied.name], E.seen[o_copied.name]

            def scores(i):
                if i >= 2:
                    pe.wait_ge(exp_done, e0 + 2 * (i - 1))
                E.run(qk(i), scores_ready)
            scores(0)
            scores(1)
            for i in range(n_steps):
                bl = blocks(i)
                E.await_(probs_ready, len({m for m, _ in bl}))
                if i >= 1:
                    pe.wait_ge(probsT_copied, c0 + i)
                for n, (m, kt) in enumerate(bl):
                    last = nc.tensor.transpose(blocks_of(4, 6)[:, n, :], probs[:, i % 2, m, kt * P:(kt + 1) * P],
                                               ident[:])
                E.run(last, probsT_ready)
                if i + 2 < n_steps:
                    scores(i + 2)
                if meanwhile is not None:
                    meanwhile(i)
                pe.wait_ge(probsT_copied, c0 + i + 1)
                if i >= 2:
                    pe.wait_ge(o_copied, o0 + i - 1)
                E.run(pv(i, PS[:, 6 + i % 2, :]), o_ready)
            E.seen[exp_done.name] = e0 + 2 * n_steps
            E.seen[probsT_copied.name] = c0 + n_steps
            E.seen[o_copied.name] = o0 + n_steps
            pe.wait_ge(exp_done, e0 + 2 * n_steps)
            pe.wait_ge(o_copied, o0 + n_steps)

        def weights(base, g=0):
            pe.wait_ge(lo_made, base + 1 + RAW_SLOTS + 4 * g)

        def feature_major(slot, kp, n_kp, bank, src_hi, src_lo, k_of, n=SEQ):
            for i in range(PK):
                k = k_of(kp, i)
                for c in range(4):
                    cols = slice(c * P, (c + 1) * P)
                    last = three(PS[:, bank + c, 0:n], whi[:, slot, i, cols], wlo[:, slot, i, cols],
                                 src_hi[:, k, :], src_lo[:, k, :], kp + i == 0, kp == n_kp - 1 and i == PK - 1)
            return last

        def last_piece(slot, kp, bank, src_hi, src_lo, k_of):
            for c in range(4):
                cols = slice(c * P, (c + 1) * P)
                for i in range(PK):
                    k = k_of(kp, i)
                    last = three(PS[:, bank + c, :], whi[:, slot, i, cols], wlo[:, slot, i, cols],
                                 src_hi[:, k, :], src_lo[:, k, :], False, i == PK - 1)
                if c < 3:
                    E.run(last, y_tile_done)
            return last

        def token_major(slot, kp, n_kp, bank, src_hi, src_lo, tiles):
            for i in range(PK):
                k = 2 * kp + i
                for t in range(tiles):
                    toks = slice(t * P, (t + 1) * P)
                    last = three(PS[:, bank + t, :], src_hi[:, k, toks], src_lo[:, k, toks],
                                 whi[:, slot, i, :], wlo[:, slot, i, :], kp + i == 0,
                                 kp == n_kp - 1 and i == PK - 1)
            return last

        def forget_gates(slot, bank):
            w = [t[:, slot].rearrange("p a (b n) -> p (a b) n", n=P) for t in (whi, wlo)]
            for k in range(KT):
                last = three(PS[:, bank, :], w[0][:, k, :], w[1][:, k, :], xhi[:, k, :], xlo[:, k, :],
                             k == 0, k == KT - 1)
            return last

        T = nc.tensor.transpose
        pe.wait_ge(x_loaded, 16)
        pe.wait_ge(consts_ready, 1)
        for k in range(KT):
            for t in range(TT):
                last = T(PS[:, k, t * P:(t + 1) * P], x_in[:, t, k * P:(k + 1) * P], ident[:])
            E.run(last, transposed)
        pe.wait_ge(rows_loaded, 16 * 13)
        pe.wait_ge(h_ready, 1)
        n1 = CONV_TAPS - MEM_G
        n2 = CONV_W * CONV_T
        T(PS[:, 0, 0:P], rows[:, 0, :], ident[:])
        T(PS[:, 0, P:P + n1], rows[0:n1, 1, :], ident[0:n1, 0:n1])
        E.run(T(PS[:, 0, CONV_TAPS:CONV_TAPS + n2], rows[0:n2, 2, :], ident[0:n2, 0:n2]), transposed)
        pe.wait_ge(h_ready, KT)
        E.await_(mem_scaled, MT)
        memo = PS[:, 4:8, :].rearrange("p a (b j) -> p (a b) j", j=MEM)
        for k in range(KT):
            for t in range(MT):
                last = T(memo[:, k, t * P:(t + 1) * P], mem_in[:, t, k * P:(k + 1) * P], ident[:])
        E.run(last, transposed)
        pe.wait_ge(transposed, E.made[transposed.name]).then_inc(pieces_used, SPLIT_SLOTS)
        E.await_(memT_ready)

        mids = 0
        for kind, l, arg, ng, np_ in STAGES:
            stats = from_h(kind, arg)
            if kind != "kv" and (stats or kind in ("mix_out", "xo")):
                E.seen[xlo_ready.name] += KT
            x_ready = E.seen[xlo_ready.name] - KT
            if kind == "kv":
                E.seen[m_lo_ready.name] += KT

            if kind == "gate_up":
                def body(base, g, group, n, with_stats=False):
                    bank = 4 * (group % 2)
                    for kp in range(4):
                        weights(base + kp, g)
                        if kp == 0:
                            pe.wait_ge(bank_free[group % 2], group // 2 + n)
                        pe.wait_ge(xlo_ready, x_ready + 2 * kp + 2)
                        slot = (base + kp) % SPLIT_SLOTS
                        feature_major(slot, kp, 4, bank, xhi, xlo, lambda a_, b_: 2 * a_ + b_).then_inc(pieces_used, 1)
                        if with_stats and kp == 2:
                            input_sums(group)
                        if with_stats and kp == 3:
                            spread(4 * ((group + 1) % 2) + 1)
                            unread[(group + 1) % 2] = True

                def input_sums(group):
                    wait_banks(group + 1)
                    E.await_(h_added, KT - 1)
                    E.run(column_sums(4 * ((group + 1) % 2), 0, y[:, 0, :], True, True), h_summed)

                first = straight_groups(ng)
                for q in range(first):
                    wait_banks(E.group + q)
                    body(E.piece + 4 * q, 0, E.group + q, 0, stats and q == 0)
                with pe.Fori(0, (ng - first) // 2) as i:
                    for q in range(2):
                        body(E.piece + 4 * (first + q), 2 * i, E.group + first + q, i)
                E.piece += 4 * ng
                E.group += ng
                continue

            if kind == "down":
                m0, mids = mids, mids + np_
            for g in range(straight(kind, ng)):
                wait_banks(E.group)
                if kind == "mix_out" and l % 2 == 0 and g == 1:
                    pe.wait_ge(head_scaled, KT)
                bank = 4 * (E.group % 2)
                other = 4 * ((E.group + 1) % 2)
                name = column_name(kind, g)
                n_kp = group_pieces(kind, g, np_)
                for kp in range(n_kp):
                    weights(E.piece)
                    slot = E.piece % SPLIT_SLOTS
                    by_tile = ends_sublayer(kind, arg) and g == 1 and kp == n_kp - 1
                    if kind == "down":
                        pe.wait_ge(mid_lo_ready, m0 + kp + 1)
                        last = last_piece(slot, kp, bank, mid_hi, mid_lo, lambda a_, b_: 2 * a_ + b_) if by_tile else \
                            feature_major(slot, kp, n_kp, bank, mid_hi, mid_lo, lambda a_, b_: 2 * a_ + b_)
                    elif kind == "kv":
                        pe.wait_ge(m_lo_ready, E.seen[m_lo_ready.name])
                        last = feature_major(slot, kp, 4, bank, m_hi, m_lo, lambda a_, b_: 2 * a_ + b_, MEM) \
                            if g < 2 else token_major(slot, kp, 4, bank, m_hi, m_lo, MT)
                    else:
                        pe.wait_ge(xlo_ready, x_ready + (KT if name == "c_f" else 2 * kp + 2))
                        last = last_piece(slot, kp, bank, xhi, xlo, lambda a_, b_: 2 * a_ + b_) if by_tile else \
                            forget_gates(slot, bank) if name == "c_f" else \
                            token_major(slot, kp, 4, bank, xhi, xlo, TT) if name in TOKEN_MAJOR else \
                            feature_major(slot, kp, 4, bank, xhi, xlo, lambda a_, b_: 2 * a_ + b_)
                    last.then_inc(pieces_used, 1)
                    E.piece += 1
                    if kind == "mix_out" and l % 2 == 0 and g == 0 and kp == 0:
                        for n in range(2):
                            square_sums(other, 4 * n)
                    if kind == "mix_out" and l % 2 == 0 and g == 0 and kp == 1:
                        for n in range(2):
                            spread(other + 1 + n)
                    if stats and g == 0 and kp == 2:
                        wait_banks(E.group + 1)
                        E.await_(h_added, KT - 1)
                        E.run(column_sums(other, 0, y[:, 0, :], True, True), h_summed)
                    if stats and g == 0 and kp == 3:
                        spread(other + 1)
                        unread[(E.group + 1) % 2] = True
                E.group += 1
            if ends_sublayer(kind, arg):
                E.made[ring_summed.name] += KT - 1
                pe.wait_ge(ring_summed, E.made[ring_summed.name])
                column_sums(other, 0, square_sum[:], True, False)
                E.await_(ring_squared, KT)
                E.run(column_sums(other, 0, ring[:, E.made[ring_summed.name] % 4, :], False, True), ring_summed)
                spread(bank + 1)
                unread[bank // 4] = True

            if kind == "even_in":
                base = E.piece
                b_bank = 4 * (E.group % 2)
                level_bank = 4 - b_bank
                wait_banks(E.group)

                def b_piece(p):
                    g, kp = divmod(p, 4)
                    if g and kp == 0:
                        wait_banks(E.group + g + 1)
                    weights(base + p)
                    slot = (base + p) % SPLIT_SLOTS
                    last = token_major(slot, kp, 4, b_bank, xhi, xlo, TT) if g == 2 else \
                        feature_major(slot, kp, 4, b_bank, xhi, xlo, lambda a_, b_: 2 * a_ + b_)
                    last.then_inc(pieces_used, 1)
                done = 0
                for n in range(len(LEVELS) + 1):
                    while done < b_pieces(n):
                        b_piece(done)
                        done += 1
                    if n == 0:
                        wait_banks(E.group + 1)
                    if n < len(LEVELS):
                        E.await_(level_ready)
                    for half in range(2):
                        if n >= 1:
                            pe.wait_ge(level_merged, 2 * n - 1 + half)
                        for b in range(8 * half, 8 * half + 8):
                            tok = slice(b * P, (b + 1) * P)
                            lhs, rhs = (lv[:, n % 2, tok],) * 2 if n < len(LEVELS) else \
                                (flat(a_k[:])[:, tok], flat(a_q[:])[:, tok])
                            last = mm(blocks_of(level_bank, level_bank + 4)[:, b, :], lhs, rhs, start=True, stop=True)
                        E.run(last, level_scores)
                while done < 12:
                    b_piece(done)
                    done += 1
                E.piece += 12
                E.group += 3
                for q in range(2):
                    wait_banks(E.group + q)
                pe.wait_ge(level_merged, 2 * (len(LEVELS) + 1))
                E.await_(cross_ready)
                kd = lv[:, 1, :].rearrange("p (h t j) -> p h t j", t=TT, j=P)
                for hd in range(4):
                    for n, (i, j) in enumerate(CROSS):
                        key = kd[:, hd, j, :] if i - j == 1 else kd2[:, hd, j, :] if i - j == 2 else kd3[:, hd, :]
                        last = mm(blocks_of(0, 6)[:, 6 * hd + n, :], key,
                                  lv[:, 0, hd * SEQ + i * P:hd * SEQ + (i + 1) * P], start=True, stop=True)
                E.run(last, cross_scores)
                E.await_(cross_copied)
                for hd in range(4):
                    for i in range(TT):
                        terms = [(cross[:, 6 * hd + n, :], j) for n, (ii, j) in enumerate(CROSS) if ii == i]
                        terms.append((scoresT[:, 4 * hd + i, :], i))
                        for n, (s, j) in enumerate(terms):
                            last = mm(PS[:, hd, i * P:(i + 1) * P], a_v[:, j, hd * P:(hd + 1) * P], s,
                                      start=n == 0, stop=n == len(terms) - 1)
                E.run(last, o_ready)
                E.await_(o_copied)

                def qk(i):
                    hd, qb = i // TT, i % TT
                    nk = (qb + 1) * P
                    for m in range(2):
                        o = PS[:, 2 * (i % 2) + m, :]
                        r = slice(64 * m, 64 * m + 64)
                        mm(o[:, 0:nk], b_q[r, hd, qb * P:nk], b_k[r, hd, 0:nk], start=True, stop=False)
                        mm(o[:, 0:nk], head_sel[0:4, hd, :], alibi[:, 0:nk], start=False, stop=False)
                        last = mm(o[:, qb * P:nk], ident_bf[:], causal_neg[:], start=False, stop=True)
                    return last

                def pv(i, o):
                    hd, qb = i // TT, i % TT
                    for kt in range(qb + 1):
                        last = mm(o[:, 0:P], b_v[:, kt, hd * P:(hd + 1) * P], even_probs[1][:, kt, :],
                                  start=kt == 0, stop=kt == qb)
                    return last

                def meanwhile(i):
                    if i == 0:
                        for t in range(4):
                            square_sums(5, 4 * t)
                    if i in (6, 10):
                        pe.wait_ge(head_scaled, 4 if i == 6 else 5)
                        square_sums(5, 0)
                    if i in SPREAD_AT:
                        k = SPREAD_AT.index(i)
                        if k:
                            pe.wait_ge(head_scaled, k)
                        spread(5)
                attention(16, qk, lambda i: [(0, kt) for kt in range(i % TT + 1)], pv, even_probs, meanwhile)
            if kind == "odd_in":
                for q in range(2):
                    wait_banks(E.group + q)
                E.await_(cum_lo_ready)

                def qk(i):
                    pair, qb = i // TT, i % TT
                    nk = (qb + 1) * P
                    for m in range(2):
                        o = PS[:, 2 * (i % 2) + m, :]
                        r = slice(64 * m, 64 * m + 64)
                        sel = head_sel[:, 2 * pair + m, :]
                        mm(o[:, 0:nk], c_q[r, pair, qb * P:nk], c_k[r, pair, 0:nk], start=True, stop=False)
                        mm(o[:, 0:nk], sel, cum_lo[:, 0:nk], start=False, stop=False)
                        mm(o[:, 0:nk], sel, cum_hi[:, 0:nk], start=False, stop=False)
                        last = mm(o[:, qb * P:nk], ident_bf[:], causal_neg[:], start=False, stop=True)
                    return last

                def pv(i, o):
                    pair, qb = i // TT, i % TT
                    for m in range(2):
                        c = (2 * pair + m) * 64
                        for kt in range(qb + 1):
                            last = mm(o[64 * m:64 * m + 64, 0:P], c_v[:, kt, c:c + 64],
                                      x_probs[1][:, m * (qb + 1) + kt, :], start=kt == 0, stop=kt == qb)
                    return last
                attention(16, qk, lambda i: [(m, kt) for m in range(2) for kt in range(i % TT + 1)], pv)
                E.await_(conv_ready, CONV_T)
                for c in range(CONV_T):
                    last = column_sums(0, 0, conv[:, c, :], c == 0, c == CONV_T - 1)
                E.run(last, conv_summed)
                spread(1)
                for c in range(CONV_T):
                    E.await_(ring_squared)
                    E.run(column_sums(0, TT, ring[:, E.made[ring_summed.name] % 4, :], c == 0, c == CONV_T - 1),
                          ring_summed)
                spread(2)
            if kind == "xq":
                for q in range(2):
                    wait_banks(E.group + q)

                def qk(i):
                    pair, qb = i // TT, i % TT
                    for m in range(2):
                        for kt in range(2):
                            ft = 2 * (2 * pair + m) + kt
                            last = mm(PS[:, 2 * (i % 2) + m, 0:MEM], x_q[:, ft, qb * P:(qb + 1) * P], x_k[:, ft, :],
                                      start=kt == 0, stop=kt == 1)
                    return last

                def pv(i, o):
                    pair = i // TT
                    for m in range(2):
                        for half in range(2):
                            n = 2 * m + half
                            c = (4 * pair + n) * P
                            for kt in range(MT):
                                last = mm(o[:, n * P:(n + 1) * P], x_v[:, kt, c:c + P], x_probs[1][:, 2 * m + kt, :],
                                          start=kt == 0, stop=kt == MT - 1)
                    return last
                attention(8, qk, lambda i: [(m, kt) for m in range(2) for kt in range(MT)], pv)
        pe.wait_ge(h_ready, KT * (1 + 4 * DEPTH))
        for t in range(TT):
            for i in range(2):
                for k in range(4):
                    last = T(PS[:, 2 * t + i, k * P:(k + 1) * P], h[:, 4 * i + k, t * P:(t + 1) * P], ident[:])
                E.run(last, transposed)

    block_ctx.__exit__(None, None, None)


INPUTS = ["x", "mem", "ffn_norm_pre", "ffn_norm_post", "ffn_w_gate", "ffn_w_up", "ffn_w_down",
          "mix_norm_pre", "mix_norm_post", "even_w_in", "even_w_out", "hgrn_norm_g", "diff_lambda",
          "diff_norm_g", "odd_w_in", "odd_w_out", "fox_f_bias", "conv_w", "conv_b", "conv_ln_g", "conv_ln_b",
          "xattn_norm_pre", "xattn_norm_post", "mem_norm_g", "xattn_w_q", "xattn_w_kv", "xattn_w_o"]


def kernel(**inputs):
    import concourse.bacc as bacc
    from concourse.bass_utils import run_bass_kernel_spmd

    nc = bacc.Bacc("TRN2", target_bir_lowering=False, num_devices=1)
    arrays, tensors = {}, {}
    for name in INPUTS:
        a = np.ascontiguousarray(inputs[name])
        arrays[name + "_dram"] = a
        tensors[name] = nc.dram_tensor(name + "_dram", a.shape, mybir.dt.from_np(a.dtype), kind="ExternalInput").ap()
    out = nc.dram_tensor("out_dram", (1, SEQ, D), mybir.dt.float32, kind="ExternalOutput").ap()
    build(nc, tensors, out)
    r = run_bass_kernel_spmd(nc, [arrays], core_ids=[0])
    return r.results[0]["out_dram"]
```

```python
import math
from collections import Counter

import numpy as np
import concourse.bass as bass
from concourse import mybir

D = 1024
SEQ = 512
MEM = 256
FF = 2816
DEPTH = 2
assert (DEPTH + 1) // 2 == 1
P = 128
KT = D // P
TT = SEQ // P
MT = MEM // P
EPS = 1e-6
KV_GROUPS = 2 * D // 256
GC = 512
PK = 2
RAW_SLOTS = 4
SPLIT_SLOTS = 4
LOOKAHEAD = 3
HEAD = 128
FOX_HEADS = 8
CONV_W = 31
CONV_T = 4
FF_PASSES = ((0, 6), (6, 5))
NEG = -1e30

FFN_PRE, FFN_POST, MIX_PRE, MIX_POST, X_PRE, X_POST = 0, 32, 64, 80, 96, 112
MEM_G, HGRN_G, DIFF_G, CONV_B, LN_G, LN_B, CONV_TAPS = 128, 144, 148, 152, 156, 160, 164
N_VEC = CONV_TAPS + CONV_W * CONV_T


def stages():
    out = []

    def ffn(l, j):
        for n, (g0, ng) in enumerate(FF_PASSES):
            out.append(("gate_up", l, (j, n), ng, KT // PK))
            out.append(("down", l, (j, n), 2, ng))
    for l in range(DEPTH):
        ffn(l, 0)
        out.append(("even_in", l, None, 7, 4) if l % 2 == 0 else ("odd_in", l, None, 6, 4))
        out.append(("kv", l, None, KV_GROUPS, 2))
        out.append(("mix_out", l, None, 2, 4))
        out.append(("xq", l, None, 2, 4))
        out.append(("xo", l, None, 2, 4))
        ffn(l, 1)
    return out


EVEN_COLS = [("a_f", 512), ("a_q", 0), ("a_g", 1536), ("a_i", 1024), ("b_q", 2048), ("b_k", 2560), ("b_v", 3072)]
ODD_COLS = [("d_a", 1544), ("d_g", 2056), ("c_f", 1536), ("c_q", 0), ("c_k", 512), ("c_v", 1024)]
TOKEN_MAJOR = ("a_i", "b_v", "c_v")

LEVELS = [64, 32, 16, 8, 4, 2, 1]
CROSS = [(1, 0), (2, 1), (3, 2), (2, 0), (3, 1), (3, 0)]


def build(nc, A, out):
    f32, f32r, bf16, i8 = mybir.dt.float32, mybir.dt.float32r, mybir.dt.bfloat16, mybir.dt.int8
    ALU, ACT, AX = mybir.AluOpType, mybir.ActivationFunctionType, mybir.AxisListType
    MUL, ADD, SUB = ALU.mult, ALU.add, ALU.subtract
    LAM_INIT = 0.8 - 0.6 * math.exp(-0.3 * 0)

    FLOAT = 4
    top = [(int(nc.sbuf_base) + 511) // 512 * 512]

    def place(name, shape, dt=f32, at=None, size=FLOAT):
        n = (int(np.prod(shape[1:])) * size + 31) // 32 * 32
        if at is None:
            at = top[0]
            top[0] += n
        assert at + n <= nc.sbuf_usable_end, (name, at + n - nc.sbuf_usable_end)
        return nc.alloc_sbuf_tensor_at(name, shape, dt, offset=at)

    NB = 4 * SEQ
    h = place("h", [P, KT, SEQ])
    y_at = top[0]
    y = place("y", [P, KT, SEQ])
    x_at = top[0]
    xhi = place("xhi", [P, KT, SEQ], f32r)
    xlo = place("xlo", [P, KT, SEQ], f32r)
    raw = place("raw", [P, RAW_SLOTS, PK, GC])
    whi = place("whi", [P, SPLIT_SLOTS, PK, GC], f32r)
    wlo = place("wlo", [P, SPLIT_SLOTS, PK, GC], f32r)
    memT = place("memT", [P, KT, MEM])
    ring_at = top[0]
    ring = place("ring", [P, 4, SEQ])
    rsb = place("rsb", [P, SEQ])
    diag = place("diag", [P, TT, P])
    ident = place("ident", [P, P])
    ones = place("ones", [P, P])
    vec = place("vec", [P, N_VEC])
    neg_half = place("neg_half", [P, 16])
    var = place("var", [P, 16])
    rstd = place("rstd", [P, 16])
    rstd_in = place("rstd_in", [P, TT])
    negmax = place("negmax", [P, 2, 2])
    rowsum = place("rowsum", [P, 2, 2])
    recip = place("recip", [P, 2, 2])
    lam = place("lam", [P, 8])
    tile_decay = place("tile_decay", [P, 4, TT])
    fbias = place("fbias", [FOX_HEADS, 8])
    head_sel = place("head_sel", [FOX_HEADS, FOX_HEADS, P], f32r)
    ident_bf = place("ident_bf", [P, P], bf16, size=2)
    causal_neg = place("causal_neg", [P, P], bf16, size=2)
    level_mask = place("level_mask", [P, len(LEVELS) + 1, P], i8, size=1)
    w_at = top[0]
    at = lambda n: w_at + n * FLOAT
    mem_in = place("mem_in", [P, MT, D], f32, at(0))
    mem_sq = place("mem_sq", [P, D], f32, at(2048))
    rows = place("rows", [P, 3, P], f32, at(3072))
    lam_in = place("lam_in", [P, 4, 64], f32, at(3456))
    level_f = place("level_f", [P, P], f32, at(7 * NB))
    head_sel_f = place("head_sel_f", [FOX_HEADS, FOX_HEADS, P], f32, at(7 * NB + 128))
    position = place("position", [4, SEQ], f32, at(7 * NB + 1152))
    slope = place("slope", [4, 8], f32, at(7 * NB + 1664))
    x_in = place("x_in", [P, TT, D], f32, y_at)
    square_sum = place("square_sum", [P, SEQ], f32, at(11520))
    out_rows = place("out_rows", [P, TT, D], f32, at(0))
    mid_hi = place("mid_hi", [P, 12, SEQ], f32r, at(0))
    mid_lo = place("mid_lo", [P, 12, SEQ], f32r, at(6144))
    gate = place("gate", [P, 2, SEQ], f32, at(12288))
    up = place("up", [P, 2, SEQ], f32, at(13312))
    a_b = place("a_b", [P, 4, SEQ], f32, at(0))
    a_k = place("a_k", [P, 4, SEQ], f32, at(NB))
    a_q = place("a_q", [P, 4, SEQ], f32, at(2 * NB))
    a_g = place("a_g", [P, 4, SEQ], f32, at(3 * NB))
    a_v = place("a_v", [P, TT, SEQ], f32, at(4 * NB))
    b_q = place("b_q", [P, 4, SEQ], f32, at(5 * NB))
    b_k = place("b_k", [P, 4, SEQ], f32, at(6 * NB))
    b_v = place("b_v", [P, TT, SEQ], f32, at(7 * NB))
    alibi = place("alibi", [4, SEQ], f32r, at(8 * NB))
    soft = place("soft", [P, 4, SEQ], f32, y_at)
    logf = place("logf", [P, 4, SEQ], f32, y_at + NB * FLOAT)
    cross = place("cross", [P, 24, P], f32, y_at)
    lv = place("lv", [P, 2, 4 * SEQ], f32, y_at)
    scoresT = place("scoresT", [P, 16, P], f32, ring_at)
    kd2 = place("kd2", [P, 4, 2, P], f32, x_at + 2 * NB * FLOAT)
    kd3 = place("kd3", [P, 4, P], f32, x_at + (2 * NB + 1024) * FLOAT)
    even_probs = place("even_probs", [P, 2, 2, SEQ], f32, at(0)), place("even_probsT", [P, 2 * TT, P], f32, at(NB))
    fox_probs = place("fox_probs", [P, 2, 2, SEQ], f32, x_at), place("fox_probsT", [P, 2 * TT, P], f32, x_at + NB * FLOAT)
    U0 = CONV_W - 1
    UN = CONV_T * (U0 + SEQ)
    u = place("u", [P, CONV_T, U0 + SEQ], f32, at(0))
    sg = place("sg", [P, CONV_T, SEQ], f32, at(UN))
    conv = place("conv", [P, CONV_T, SEQ], f32, at(UN + NB))
    c_q = place("c_q", [P, 4, SEQ], f32, at(UN + 2 * NB))
    c_k = place("c_k", [P, 4, SEQ], f32, at(UN + 3 * NB))
    c_v = place("c_v", [P, TT, SEQ], f32, at(UN + 4 * NB))
    c_z = place("c_z", [FOX_HEADS, 3, SEQ], f32, at(UN + 5 * NB))
    cum_hi = place("cum_hi", [FOX_HEADS, SEQ], f32r, at(UN + 5 * NB + 1536))
    cum_lo = place("cum_lo", [FOX_HEADS, SEQ], f32r, at(UN + 5 * NB + 2048))
    m_hi = [place(f"m_hi{n}", [P, KT, MEM], f32r, x_at + c * NB * FLOAT) for n, c in enumerate((1, 2))]
    m_lo = place("m_lo", [P, KT, MEM], f32r, x_at + 3 * NB * FLOAT)
    x_k = [place(f"x_k{n}", [P, KT, MEM], f32, at(c)) for n, c in enumerate((2 * NB, UN + 5 * NB + 2560))]
    x_v = [place(f"x_v{n}", [P, MT, D], f32, at(c)) for n, c in enumerate((4 * NB, UN))]
    x_q = [place(f"x_q{n}", [P, KT, SEQ], f32, at(c)) for n, c in enumerate((5 * NB, UN + NB))]

    x_probs = [even_probs, (place("x_probs1", [P, 2, 2, SEQ], f32, at(9216)),
                            place("x_probsT1", [P, 2 * TT, P], f32, at(11264)))]

    PS = nc.alloc_psum_tensor("ps", [P, 8, 512], f32)
    flat = lambda t: t.rearrange("p a b -> p (a b)")
    blocks_of = lambda b0, b1: PS[:, b0:b1, :].rearrange("p a (b j) -> p (a b) j", j=P)

    def sem(name):
        return nc.alloc_semaphore(name)

    x_loaded, mem_loaded, rows_loaded, small_loaded, stored = map(sem, (
        "x_loaded", "mem_loaded", "rows_loaded", "small_loaded", "stored"))
    raw_full = [sem(f"raw_full{i}") for i in range(RAW_SLOTS)]
    hi_made, lo_made, pieces_used = map(sem, ("hi_made", "lo_made", "pieces_used"))
    bank_free = [sem("even_banks_free"), sem("odd_banks_free")]
    vector_step, scalar_step, pool_step = map(sem, ("vector_step", "scalar_step", "pool_step"))
    consts_ready, tables_ready, vec_ready, mem_squared, mem_scaled, memT_ready, lam_exp = map(sem, (
        "consts_ready", "tables_ready", "vec_ready", "mem_squared", "mem_scaled", "memT_ready", "lam_exp"))
    transposed = sem("transposed")
    h_ready, xhi_ready, xlo_ready, m_hi_ready, m_lo_ready = map(sem, (
        "h_ready", "xhi_ready", "xlo_ready", "m_hi_ready", "m_lo_ready"))
    h_squared, h_added, h_summed, ring_squared, ring_summed = map(sem, (
        "h_squared", "h_added", "h_summed", "ring_squared", "ring_summed"))
    var_ready, rstd_ready, diag_ready, spread_ready, spread_used = map(sem, (
        "var_ready", "rstd_ready", "diag_ready", "spread_ready", "spread_used"))
    gate_scaled, up_scaled, gate_silu, product_ready, mid_hi_ready, mid_lo_ready = map(sem, (
        "gate_scaled", "up_scaled", "gate_silu", "product_ready", "mid_hi_ready", "mid_lo_ready"))
    y_tile_done, y_ready, proj_ready, v_ready, y_mixed = map(sem, ("y_tile_done", "y_ready", "proj_ready", "v_ready", "y_mixed"))
    scores_ready, negmax_ready, exp_done, probs_ready = map(sem, (
        "scores_ready", "negmax_ready", "exp_done", "probs_ready"))
    probsT_ready, probsT_copied, o_ready, o_copied = map(sem, (
        "probsT_ready", "probsT_copied", "o_ready", "o_copied"))
    head_scaled, kv_copied = sem("head_scaled"), sem("kv_copied")
    softplus_ready, level_diff, level_exp, level_ready, level_scores, level_merged = map(sem, (
        "softplus_ready", "level_diff", "level_exp", "level_ready", "level_scores", "level_merged"))
    decay_ready, cross_ready, cross_scores, cross_copied, cum_ready, cum_hi_ready, cum_lo_ready = map(sem, (
        "decay_ready", "cross_ready", "cross_scores", "cross_copied", "cum_ready", "cum_hi_ready", "cum_lo_ready"))
    sigmoid_ready, conv_ready, conv_added, conv_summed, conv_centred, conv_scaled = map(sem, (
        "sigmoid_ready", "conv_ready", "conv_added", "conv_summed", "conv_centred", "conv_scaled"))
    y_silu = sem("y_silu")
    out_copied, odd_out_copied = sem("out_copied"), sem("odd_out_copied")

    STAGES = stages()
    total_pieces = sum(ng * n for _, _, _, ng, n in STAGES) - 3 * (DEPTH // 2)

    SPREAD_AT = [2, 3, 4, 5, 8, 12]
    POWER_AT = [2, 8, 12]
    HI_AT = [n + 4 for n in SPREAD_AT[:4]]
    ADDED = 6
    KV_PIECES = 2 * KV_GROUPS
    A_GROUPS = 4

    def b_pieces(n):
        return min(2 + n, 12)

    def straight(kind, ng):
        return A_GROUPS if kind == "even_in" else ng

    def group_pieces(kind, g, n):
        return 1 if kind == "odd_in" and ODD_COLS[g][0] == "c_f" else n

    def straight_groups(ng):
        return 2 if ng % 2 == 0 else 1

    def column_name(kind, g):
        return {"even_in": EVEN_COLS, "odd_in": ODD_COLS}[kind][g][0] if kind in ("even_in", "odd_in") else ""

    def from_h(kind, arg):
        return kind in ("even_in", "odd_in", "xq") or (kind == "gate_up" and arg[1] == 0)

    def gain_of(kind, l, arg):
        return {"even_in": MIX_PRE, "odd_in": MIX_PRE, "xq": X_PRE}[kind] + l * KT if kind != "gate_up" else \
            FFN_PRE + (2 * l + arg[0]) * KT

    def ends_sublayer(kind, arg):
        return kind in ("mix_out", "xo") or (kind == "down" and arg[1] == 1)

    def post_gain(kind, l, arg):
        return {"mix_out": MIX_POST, "xo": X_POST}[kind] + l * KT if kind != "down" else \
            FFN_POST + (2 * l + arg[0]) * KT

    class Engine:

        def __init__(self, eng, chain):
            self.eng, self.chain = eng, chain
            self.made, self.seen, self.last = Counter(), Counter(), None
            self.piece = self.group = 0

        def run(self, ins, s=None, n=1):
            s = self.chain if s is None else s
            self.made[s.name] += n
            ins.then_inc(s, n)
            self.last = (s, self.made[s.name])

        def own(self):
            self.eng.wait_ge(*self.last)

        def await_(self, s, n=1):
            self.seen[s.name] += n
            self.eng.wait_ge(s, self.seen[s.name])

        def release_banks(self):
            self.eng.wait_ge(*self.last).then_inc(bank_free[self.group % 2], 1)

        def group_done(self):
            self.eng.wait_ge(pieces_used, self.piece + SPLIT_SLOTS)

    block_ctx = nc.Block()
    block = block_ctx.__enter__()

    @block.sync
    def _(sp):
        sp.dma_start(x_in[:], A["x"][0].rearrange("(t p) d -> p t d", p=P)).then_inc(x_loaded, 16)
        r = 0
        for name in ("ffn_norm_pre", "ffn_norm_post", "mix_norm_pre", "mix_norm_post",
                     "xattn_norm_pre", "xattn_norm_post"):
            src = A[name]
            src = src.rearrange("l j (k p) -> (l j k) p", p=P) if len(src.shape) == 3 else \
                src.rearrange("l (k p) -> (l k) p", p=P)
            sp.dma_start(rows[r:r + src.shape[0], 0, :], src).then_inc(rows_loaded, 16)
            r += src.shape[0]
        r = 0
        for name in ("mem_norm_g", "hgrn_norm_g", "diff_norm_g", "conv_b", "conv_ln_g", "conv_ln_b"):
            src = A[name].rearrange("l (k p) -> (l k) p", p=P)
            sp.dma_start(rows[r:r + src.shape[0], 1, :], src).then_inc(rows_loaded, 16)
            r += src.shape[0]
        sp.dma_start(rows[0:CONV_W * CONV_T, 2, :],
                     A["conv_w"][0].rearrange("w (c p) -> (w c) p", p=P)).then_inc(rows_loaded, 16)
        sp.dma_start(mem_in[:], A["mem"][0].rearrange("(t p) d -> p t d", p=P)).then_inc(mem_loaded, 16)
        sp.dma_start(lam_in[:], A["diff_lambda"].broadcast_to([P, 4, 64])).then_inc(small_loaded, 16)
        with nc.allow_non_contiguous_dma("eight biases, one to a partition"):
            sp.dma_start(fbias[:, 0:1], A["fox_f_bias"].rearrange("o h -> h o")).then_inc(small_loaded, 16)

        def load(base, g, halves):
            slot = base % RAW_SLOTS
            sp.wait_ge(lo_made, base + 1 + 4 * g)
            for dst, src in halves(slot):
                sp.dma_start(dst, src).then_inc(raw_full[slot], 16)

        def two_rows(w, k0, c0):
            def halves(slot):
                for i in range(2):
                    yield raw[:, slot, i, :], w[(k0 + i) * P:(k0 + i + 1) * P, c0:c0 + GC]
            return halves

        def gate_and_up(l, j, kp, c0):
            def halves(slot):
                for i, name in enumerate(("ffn_w_gate", "ffn_w_up")):
                    w = A[name][l, j].rearrange("(k p) n -> p k n", p=P)
                    yield raw[:, slot, :, i * 256:(i + 1) * 256], w[:, 2 * kp:2 * kp + 2, bass.ds(c0, 256)]
            return halves

        def four_rows(w, k0, c0):
            def halves(slot):
                dst = raw[:, slot].rearrange("p a (b n) -> p (a b) n", n=256)
                src = w.rearrange("(k p) n -> p k n", p=P)
                for i in range(0, 4, 2):
                    yield dst[:, i:i + 2, :], src[:, k0 + i:k0 + i + 2, c0:c0 + 256]
            return halves

        def forget_rows(w, c0):
            def halves(slot):
                dst = raw[:, slot].rearrange("p a (b n) -> p (a b) n", n=P)
                src = w.rearrange("(k p) n -> p k n", p=P)
                for i in range(2):
                    yield dst[:, 4 * i:4 * i + 4, :], src[:, 4 * i:4 * i + 4, c0:c0 + P]
            return halves

        piece = 0
        for kind, l, arg, ng, np_ in STAGES:
            if kind == "gate_up":
                j, n = arg
                first = straight_groups(ng)
                g0 = FF_PASSES[n][0]
                for g in range(first):
                    for kp in range(4):
                        load(piece + 4 * g + kp, 0, gate_and_up(l, j, kp, (g0 + g) * 256))
                with sp.Fori(0, (ng - first) // 2) as i:
                    for q in range(2):
                        for kp in range(4):
                            load(piece + 4 * (first + q) + kp, 2 * i,
                                 gate_and_up(l, j, kp, (g0 + first + q) * 256 + i * 512))
                piece += 4 * ng
                continue
            for g in range(ng):
                for kp in range(group_pieces(kind, g, np_)):
                    if kind == "down":
                        j, n = arg
                        src = two_rows(A["ffn_w_down"][l, j], 2 * FF_PASSES[n][0] + 2 * kp, g * GC)
                    elif kind == "kv":
                        src = four_rows(A["xattn_w_kv"][l], 4 * kp, g * 256)
                    elif kind == "even_in":
                        src = two_rows(A["even_w_in"][l // 2], 2 * kp, EVEN_COLS[g][1])
                    elif kind == "odd_in":
                        name, c0 = ODD_COLS[g]
                        w = A["odd_w_in"][l // 2]
                        src = forget_rows(w, c0) if name == "c_f" else two_rows(w, 2 * kp, c0)
                    else:
                        w = {"mix_out": A["even_w_out" if l % 2 == 0 else "odd_w_out"][l // 2],
                             "xq": A["xattn_w_q"][l], "xo": A["xattn_w_o"][l]}[kind]
                        src = two_rows(w, 2 * kp, g * GC)
                    load(piece, 0, src)
                    piece += 1
        assert piece == total_pieces
        for i in range(2):
            for t in range(TT):
                if i and t % 2:
                    sp.wait_ge(odd_out_copied, t // 2 + 1)
                else:
                    sp.wait_ge(out_copied, t + 1 if i == 0 else TT + t // 2 + 1)
                sp.dma_start(out[0, t * P:(t + 1) * P, i * SEQ:(i + 1) * SEQ],
                             out_rows[:, t, i * SEQ:(i + 1) * SEQ]).then_inc(stored, 16)
        sp.wait_ge(stored, 16 * 2 * TT)

    @block.gpsimd
    def _(pool):
        E = Engine(pool, pool_step)
        g = nc.gpsimd

        def on_diagonal(t, pattern):
            E.run(g.memset(t, 0.0))
            E.own()
            E.run(g.affine_select(out=t, in_=t, compare_op=ALU.not_equal, fill=1.0, base=0,
                                  pattern=pattern, channel_multiplier=1))
        E.run(g.memset(ones[:], 1.0))
        E.run(g.memset(neg_half[:], -0.5))
        on_diagonal(ident[:], [[-1, P]])
        E.own()
        pool.wait_ge(*E.last).then_inc(consts_ready, 1)
        def power(n):
            E.await_(var_ready)
            E.run(g.tensor_tensor(rstd[:, 0:n], var[:, 0:n], neg_half[:, 0:n], ALU.pow), rstd_ready)

        def make_tables():
            on_diagonal(head_sel_f[:], [[-1, FOX_HEADS], [0, P]])
            on_diagonal(ident_bf[:], [[-1, P]])
            E.run(g.iota(position[:], pattern=[[1, SEQ]], base=0, channel_multiplier=0,
                         allow_small_or_imprecise_dtypes=True))
            E.run(g.memset(slope[:], 0.0))
            for n in range(4):
                E.own()
                E.run(g.affine_select(out=slope[:], in_=slope[:], compare_op=ALU.not_equal, base=-n,
                                      fill=8.0 * 2.0 ** (-8.0 * (n + 1) / 4), pattern=[[0, 8]], channel_multiplier=1))
            E.run(g.memset(causal_neg[:], 0.0))
            E.own()
            E.run(g.affine_select(out=causal_neg[:], in_=causal_neg[:], compare_op=ALU.is_ge, fill=NEG, base=0,
                                  pattern=[[-1, P]], channel_multiplier=1))
            for n, L in enumerate(LEVELS):
                m = level_f[:].rearrange("p (b r j) -> p b r j", r=2, j=L)
                nb = P // (2 * L)
                E.run(g.memset(level_f[:], 1.0))
                for base, ch, pat in ((0, 1, [[-2 * L, nb], [0, 2], [0, L]]),
                                      (L - 1, -1, [[2 * L, nb], [0, 2], [0, L]]),
                                      (-1, 0, [[0, nb], [1, 2], [0, L]])):
                    E.own()
                    E.run(g.affine_select(out=m, in_=m, compare_op=ALU.is_ge, fill=0.0, base=base,
                                          pattern=pat, channel_multiplier=ch))
                E.own()
                E.run(g.tensor_copy(level_mask[:, n, :], level_f[:]))
                E.own()
            E.run(g.tensor_copy(level_mask[:, len(LEVELS), :], ident[:]), tables_ready)

        def split(base):
            slot = base % RAW_SLOTS
            pool.wait_ge(hi_made, base + 1)
            pool.wait_ge(lo_made, base + RAW_SLOTS)
            g.tensor_tensor(flat(wlo[:, slot]), flat(raw[:, slot]), flat(whi[:, slot]).bitcast(f32),
                            SUB).then_inc(lo_made, 1)

        power(MT)
        def add_input_squares():
            E.await_(h_squared)
            for k in range(1, KT):
                E.await_(h_squared)
                if k > 1:
                    E.own()
                E.run(g.tensor_tensor(y[:, 0, :], y[:, 0, :], y[:, k, :], ADD), h_added)

        def add_result_squares():
            n = E.made[ring_summed.name]
            E.await_(ring_squared)
            for k in range(1, ADDED):
                E.await_(ring_squared)
                first = ring[:, n % 4, :] if k == 1 else square_sum[:]
                if k > 1:
                    E.own()
                E.run(g.tensor_tensor(square_sum[:], first, ring[:, (n + k) % 4, :], ADD), ring_summed,
                      2 if k == 1 else 1)
            E.made[ring_summed.name] += KT - ADDED
            E.seen[ring_squared.name] += KT - ADDED

        products = 0
        for kind, l, arg, ng, np_ in STAGES:
            base_piece = E.piece
            E.piece += sum(group_pieces(kind, g_, np_) for g_ in range(ng))
            if from_h(kind, arg):
                add_input_squares()
                power(TT)
            if kind == "gate_up":
                def multiply(n):
                    pool.wait_ge(gate_silu, n)
                    pool.wait_ge(up_scaled, n)
                    g.tensor_tensor(up[:], gate[:], up[:], MUL).then_inc(product_ready, 1)
                first = straight_groups(ng)
                for q in range(first):
                    multiply(products + q + 1)
                with pool.Fori(0, (ng - first) // 2) as i:
                    for q in range(2):
                        multiply(products + first + q + 1 + 2 * i)
                products += ng
            elif kind == "down" and (l, arg) == (0, (0, 0)):
                make_tables()
            elif kind == "even_in":
                for i in range(1, KV_PIECES + 1):
                    split(E.piece + LOOKAHEAD - 1 + i)
                    if i in POWER_AT:
                        power(16 if i == POWER_AT[0] else TT)
                power(2 * TT)
                E.made[ring_summed.name] += KT
                E.seen[ring_squared.name] += KT
            elif kind == "odd_in":
                for i in range(1, KV_PIECES + 1):
                    split(E.piece + LOOKAHEAD - 1 + i)
                E.await_(conv_ready)
                for c in range(1, CONV_T):
                    E.await_(conv_ready)
                    if c > 1:
                        E.own()
                    E.run(g.tensor_tensor(ring[:, 0, :], conv[:, 0, :] if c == 1 else ring[:, 0, :], conv[:, c, :],
                                          ADD), conv_added)
                power(TT)
                E.made[ring_summed.name] += CONV_T
                E.seen[ring_squared.name] += CONV_T
            elif ends_sublayer(kind, arg):
                add_result_squares()
                power(TT)

    @block.scalar
    def _(act):
        E = Engine(act, scalar_step)
        a = nc.scalar.activation

        def split(base, g=0):
            slot = base % RAW_SLOTS
            act.wait_ge(raw_full[slot], 32 * (base // RAW_SLOTS + 1) + 32 * g)
            act.wait_ge(pieces_used, base + 1 + 4 * g)
            a(flat(whi[:, slot]), flat(raw[:, slot]), ACT.Copy).then_inc(hi_made, 1)

        def split_next():
            if E.piece + LOOKAHEAD < total_pieces:
                split(E.piece + LOOKAHEAD)
            E.piece += 1

        def open_input(gain):
            for k0 in range(0, KT, 2):
                for k in (k0, k0 + 1):
                    E.await_(h_ready)
                    E.run(a(xhi[:, k, :], h[:, k, :], ACT.Copy, scale=vec[:, gain + k:gain + k + 1]), xhi_ready)
                for k in (k0, k0 + 1):
                    E.run(a(y[:, k, :], h[:, k, :], ACT.Square), h_squared)
            split(E.piece + LOOKAHEAD)

        def square_into_ring(src):
            n = E.made[ring_squared.name]
            if n >= 4:
                act.wait_ge(ring_summed, n - 3)
            E.run(a(ring[:, n % 4, :], src, ACT.Square), ring_squared)

        def input_hi(k, ready=None):
            if ready is not None:
                E.await_(ready)
            E.run(a(xhi[:, k, :], y[:, k, :], ACT.Copy), xhi_ready)

        def memory_input(l):
            for k in range(KT):
                E.run(a(m_hi[l % 2][:, k, :], memT[:, k, :], ACT.Copy,
                        scale=vec[:, MEM_G + l * KT + k:MEM_G + l * KT + k + 1]), m_hi_ready)

        def attention(n_steps, nk_of, scale, n_blocks, o_copy, buffers=fox_probs, meanwhile=None, kv_layer=None):
            probs, probsT = buffers
            t0, o0 = E.seen[probsT_ready.name], E.seen[o_ready.name]
            base = E.piece
            for i in range(n_steps + 2):
                if i < n_steps:
                    E.await_(negmax_ready)
                    if i >= 2:
                        act.wait_ge(probsT_ready, t0 + i - 1)
                    nk = nk_of(i)
                    for m in range(2):
                        E.run(a(probs[:, i % 2, m, 0:nk], PS[:, 2 * (i % 2) + m, 0:nk], ACT.Exp,
                                bias=negmax[:, i % 2, m:m + 1], scale=scale,
                                accum_out=rowsum[:, i % 2, m:m + 1]), exp_done)
                if kv_layer is not None and 1 <= i <= KV_PIECES:
                    split(base + i + LOOKAHEAD - 1)
                if i >= 2:
                    E.await_(o_ready)
                    dst, src = o_copy(i - 2)
                    E.run(a(dst, src, ACT.Copy), o_copied)
                if 1 <= i <= n_steps:
                    E.await_(probsT_ready)
                    if i >= 2:
                        act.wait_ge(o_ready, o0 + i - 1)
                    n = n_blocks(i - 1)
                    E.run(a(probsT[:, 0:n, :], blocks_of(4, 6)[:, 0:n, :], ACT.Copy), probsT_copied)
                if kv_layer is not None:
                    if 2 <= i <= KV_PIECES and i % 2 == 0:
                        g = i // 2 - 1
                        act.wait_ge(pieces_used, base + i + SPLIT_SLOTS)
                        k = x_k[kv_layer % 2][:, 2 * g:2 * g + 2, :] if g < 4 else \
                            x_v[kv_layer % 2][:, :, (g - 4) * 256:(g - 3) * 256]
                        E.run(a(k, PS[:, 7, :].rearrange("p (a n) -> p a n", n=256), ACT.Copy), kv_copied)
                if meanwhile is not None:
                    meanwhile(i)
            if kv_layer is not None:
                E.piece += KV_PIECES

        act.wait_ge(mem_loaded, 16)
        for t in range(MT):
            if t:
                E.own()
            E.run(a(mem_sq[:], mem_in[:, t, :], ACT.Square, accum_out=lam[:, 4 + t:5 + t]), mem_squared)
        E.await_(lam_exp)
        E.run(a(lam[:, 2:4], lam[:, 0:2], ACT.Exp), mem_squared)
        for p in range(LOOKAHEAD):
            split(p)
        E.await_(vec_ready)

        mids = 0
        for kind, l, arg, ng, np_ in STAGES:
            base_piece = E.piece
            early = from_h(kind, arg)
            if kind == "kv":
                continue
            if early:
                open_input(gain_of(kind, l, arg))

            if kind == "gate_up":
                def body(base, g, n, tile, skip_split=False):
                    for kp in range(4):
                        if not (skip_split and kp == 0):
                            split(base + kp + LOOKAHEAD, g)
                    act.wait_ge(gate_scaled, n)
                    a(gate[:], gate[:], ACT.Silu).then_inc(gate_silu, 1)
                    act.wait_ge(product_ready, n)
                    a(mid_hi[:, tile, :], up[:], ACT.Copy).then_inc(mid_hi_ready, 1)

                first = straight_groups(ng)
                for q in range(first):
                    body(base_piece + 4 * q, 0, mids + q + 1, slice(2 * q, 2 * q + 2), early and q == 0)
                with act.Fori(0, (ng - first) // 2) as i:
                    for q in range(2):
                        body(base_piece + 4 * (first + q), 2 * i, mids + first + q + 1 + 2 * i,
                             bass.ds(2 * (first + q) + 4 * i, 2))
                mids += ng
                E.made[mid_hi_ready.name] = mids
                E.last = (mid_hi_ready, mids)
                E.piece += 4 * ng
                E.group += ng
                continue

            for g in range(straight(kind, ng)):
                for kp in range(group_pieces(kind, g, np_)):
                    if early and g == 0 and kp == 0:
                        E.piece += 1
                    else:
                        split_next()
                bank = 4 * (E.group % 2)
                name = column_name(kind, g)
                if kind in ("mix_out", "xo", "down"):
                    if ends_sublayer(kind, arg):
                        for c in range(4):
                            E.await_(y_ready)
                            square_into_ring(y[:, 4 * g + c, :])
                    else:
                        E.seen[y_ready.name] += 4
                elif name in TOKEN_MAJOR:
                    dst = {"a_i": a_v, "b_v": b_v, "c_v": c_v}[name]
                    E.group_done()
                    for t in range(TT):
                        E.run(a(dst[:, t, :], PS[:, bank + t, :], ACT.Copy, scale=rstd_in[:, t:t + 1]), v_ready)
                    E.release_banks()
                else:
                    E.await_(proj_ready)
                    if name == "a_f":
                        E.run(a(a_k[:], a_b[:], ACT.Sigmoid, scale=-1.0))
                        E.run(a(soft[:], a_b[:], ACT.Abs))
                        E.own()
                        E.run(a(soft[:], soft[:], ACT.Exp, scale=-1.0))
                        E.own()
                        E.run(a(soft[:], soft[:], ACT.Ln, bias=ones[:, 0:1]), softplus_ready)
                    elif name == "a_g":
                        E.run(a(a_g[:], a_g[:], ACT.Silu))
                    elif name == "d_g":
                        E.run(a(sg[:], sg[:], ACT.Sigmoid), sigmoid_ready)
                    elif name == "c_f":
                        E.run(a(c_z[:, 1, :], c_z[:, 0, :], ACT.Abs))
                        E.own()
                        E.run(a(c_z[:, 1, :], c_z[:, 1, :], ACT.Exp, scale=-1.0))
                        E.own()
                        E.run(a(c_z[:, 1, :], c_z[:, 1, :], ACT.Ln, bias=ones[0:FOX_HEADS, 0:1]), softplus_ready)
                        E.await_(cum_ready)
                        E.run(a(cum_hi[:], c_z[:, 0, :], ACT.Copy), cum_hi_ready)
                E.group += 1

            if kind == "even_in":
                base, done = E.piece, LOOKAHEAD
                b_bank = 4 * (E.group % 2)

                def split_to(done, n):
                    for p in range(done, n):
                        split(base + p)
                    return n
                for n in range(len(LEVELS) + 1):
                    if n < len(LEVELS):
                        E.await_(level_diff)
                        E.run(a(lv[:, n % 2, :], lv[:, n % 2, :], ACT.Exp), level_exp)
                    done = split_to(done, b_pieces(n) + LOOKAHEAD)
                act.wait_ge(level_scores, 2 * len(LEVELS))
                E.run(a(lv[:, 0, :], flat(a_b[:]), ACT.Exp), decay_ready)
                E.run(a(tile_decay[:], a_b[:].rearrange("p h (t j) -> p h t j", j=P)[:, :, :, P - 1], ACT.Exp),
                      decay_ready)
                E.await_(level_diff)
                E.run(a(lv[:, 1, :], lv[:, 1, :], ACT.Exp), decay_ready)
                done = split_to(done, 12 + LOOKAHEAD)
                E.piece += 12
                E.group_done()
                E.group += 2
                E.await_(proj_ready, 2)
                for t in range(TT):
                    E.run(a(b_v[:, t, :], PS[:, b_bank + t, :], ACT.Copy, scale=rstd_in[:, t:t + 1]), v_ready)
                E.release_banks()
                E.group += 1
                memory_input(l)
                E.await_(cross_scores)
                E.run(a(cross[:], blocks_of(2, 8), ACT.Copy), cross_copied)
                E.await_(o_ready)
                E.run(a(y[:, 0:4, :], PS[:, 4:8, :], ACT.Copy), o_copied)
                E.own()
                for k in range(4):
                    square_into_ring(y[:, k, :])

                def meanwhile(i):
                    if i >= TT + 1 and (i - TT - 1) % TT == 0:
                        E.own()
                        square_into_ring(y[:, 4 + (i - TT - 1) // TT, :])
                    if i in HI_AT:
                        input_hi(HI_AT.index(i), y_mixed)
                attention(16, lambda i: (i % TT + 1) * P, 0.125, lambda i: i % TT + 1,
                          lambda i: (y[:, 4 + i // TT, i % TT * P:(i % TT + 1) * P], PS[:, 6, 0:P]),
                          even_probs, meanwhile, l)
                E.group_done()
                for k in range(len(HI_AT), KT):
                    input_hi(k, y_mixed)
            if kind == "odd_in":
                E.group_done()
                memory_input(l)
                attention(16, lambda i: (i % TT + 1) * P, 0.125, lambda i: 2 * (i % TT + 1),
                          lambda i: (y[:, i // TT, i % TT * P:(i % TT + 1) * P], PS[:, 6, 0:P]),
                          kv_layer=l)
                E.group_done()
                E.own()
                for k in range(4):
                    input_hi(k)
                for c in range(CONV_T):
                    E.await_(conv_centred)
                    square_into_ring(conv[:, c, :])
                for c in range(CONV_T):
                    E.await_(conv_scaled)
                    E.run(a(y[:, 4 + c, :], conv[:, c, :], ACT.Silu, scale=vec[:, LN_G + c:LN_G + c + 1],
                            bias=vec[:, LN_B + c:LN_B + c + 1]), y_silu)
                    E.own()
                    input_hi(4 + c)
            if kind == "xq":
                attention(8, lambda i: MEM, 0.0625, lambda i: 2 * MT,
                          lambda i: (y[:, 4 * (i // TT):4 * (i // TT) + 4, i % TT * P:(i % TT + 1) * P],
                                     PS[:, 6 + i % 2, :].rearrange("p (a j) -> p a j", j=P)),
                          x_probs[l % 2], lambda i: input_hi(i - TT - 2) if i >= TT + 2 else None)
                E.own()
                for k in range(4, KT):
                    input_hi(k)
        act.wait_ge(transposed, KT + 2 + 1)
        for t in range(TT):
            E.run(a(out_rows[:, t, 0:SEQ], PS[:, 2 * t, :], ACT.Copy), out_copied)
        for t in range(0, TT, 2):
            act.wait_ge(transposed, KT + 2 + 1 + t + 1)
            E.run(a(out_rows[:, t, SEQ:], PS[:, 2 * t + 1, :], ACT.Copy), out_copied)

    @block.vector
    def _(dve):
        E = Engine(dve, vector_step)
        v = nc.vector

        def split(base, g=0):
            slot = base % RAW_SLOTS
            dve.wait_ge(hi_made, base + 1 + 4 * g)
            v.tensor_tensor(flat(wlo[:, slot]), flat(raw[:, slot]), flat(whi[:, slot]).bitcast(f32),
                            SUB).then_inc(lo_made, 1)

        def split_next():
            if E.piece + LOOKAHEAD < total_pieces:
                split(E.piece + LOOKAHEAD)
            E.piece += 1

        def make_diag(cols):
            for t in range(TT):
                E.run(v.tensor_scalar(diag[:, t, :], ident[:], cols[:, t:t + 1], None, MUL), diag_ready)

        def variance(src, n, cols):
            E.run(v.tensor_scalar(var[:, 0:cols], src, 1.0 / n, EPS, MUL, ADD), var_ready)

        def input_stats(bank):
            E.await_(h_summed)
            variance(PS[:, bank, 0:TT], D, TT)
            E.await_(rstd_ready)
            E.run(v.tensor_copy(rstd_in[:], rstd[:, 0:TT]))
            make_diag(rstd[:, 0:TT])

        def input_spread(bank):
            E.await_(spread_ready)
            E.run(v.tensor_copy(rsb[:], PS[:, bank + 1, :]), spread_used)
            E.own()

        def input_lo(k, gain=None):
            E.await_(xhi_ready)
            if gain is None:
                E.run(v.tensor_tensor(xlo[:, k, :], y[:, k, :], xhi[:, k, :].bitcast(f32), SUB), xlo_ready)
            else:
                E.run(v.scalar_tensor_tensor(out=xlo[:, k, :], in0=h[:, k, :], scalar=vec[:, gain + k:gain + k + 1],
                                             in1=xhi[:, k, :].bitcast(f32), op0=MUL, op1=SUB), xlo_ready)

        def memory_lo(l):
            for k in range(KT):
                E.await_(m_hi_ready)
                c = MEM_G + l * KT + k
                E.run(v.scalar_tensor_tensor(out=m_lo[:, k, :], in0=memT[:, k, :], scalar=vec[:, c:c + 1],
                                             in1=m_hi[l % 2][:, k, :].bitcast(f32), op0=MUL, op1=SUB), m_lo_ready)

        def close_sublayer(kind, l, arg, bank, next_gain):
            E.await_(ring_summed, 8)
            variance(PS[:, bank, 0:TT], D, TT)
            E.await_(rstd_ready)
            make_diag(rstd[:, 0:TT])
            E.await_(spread_ready)
            gain = post_gain(kind, l, arg)
            for k0 in range(0, KT, 2):
                scaled = []
                for k in (k0, k0 + 1):
                    E.run(v.tensor_tensor(y[:, k, :], y[:, k, :], PS[:, (bank + 5) % 8, :], MUL),
                          spread_used if k == KT - 1 else None)
                    scaled.append(E.last)
                for k, done in zip((k0, k0 + 1), scaled):
                    dve.wait_ge(*done)
                    E.run(v.scalar_tensor_tensor(out=h[:, k, :], in0=y[:, k, :], scalar=vec[:, gain + k:gain + k + 1],
                                                 in1=h[:, k, :], op0=MUL, op1=ADD), h_ready)
                if next_gain is not None:
                    input_lo(k0, next_gain)
                    input_lo(k0 + 1, next_gain)

        def attention(n_steps, nk_of, scale, differential, buffers=fox_probs, meanwhile=None, with_kv=False):
            probs, _ = buffers
            for i in range(n_steps + 1):
                if i < n_steps:
                    E.await_(scores_ready)
                    nk = nk_of(i)
                    E.run(v.tensor_reduce(out=negmax[:, i % 2, :], in_=PS[:, 2 * (i % 2):2 * (i % 2) + 2, 0:nk],
                                          axis=AX.X, op=ALU.max, negate=True))
                    E.own()
                    E.run(v.tensor_scalar(negmax[:, i % 2, :], negmax[:, i % 2, :], scale, None, MUL), negmax_ready)
                if meanwhile is not None and differential:
                    meanwhile(i)
                if i >= 1:
                    j = (i - 1) % 2
                    nk = nk_of(i - 1)
                    E.await_(exp_done, 2)
                    E.run(v.reciprocal(recip[:, j, :], rowsum[:, j, :]))
                    E.own()
                    p0, p1 = probs[:, j, 0, 0:nk], probs[:, j, 1, 0:nk]
                    if differential:
                        E.run(v.tensor_scalar(p1, p1, recip[:, j, 1:2], lam[:, 6:7], MUL, MUL))
                        E.own()
                        E.run(v.scalar_tensor_tensor(out=p0, in0=p0, scalar=recip[:, j, 0:1], in1=p1,
                                                     op0=MUL, op1=ADD), probs_ready)
                    else:
                        E.run(v.tensor_scalar(p0, p0, recip[:, j, 0:1], None, MUL), probs_ready)
                        E.run(v.tensor_scalar(p1, p1, recip[:, j, 1:2], None, MUL), probs_ready)
                if meanwhile is not None and not differential:
                    meanwhile(i)
            if with_kv:
                E.piece += KV_PIECES
                dve.wait_ge(lo_made, E.piece + LOOKAHEAD + RAW_SLOTS)

        dve.wait_ge(small_loaded, 32).then_inc(lo_made, RAW_SLOTS)
        E.run(v.tensor_tensor(lam_in[:, 0:4:2, :], lam_in[:, 0:4:2, :], lam_in[:, 1:4:2, :], MUL))
        E.own()
        E.run(v.tensor_reduce(out=lam[:, 0:2], in_=lam_in[:, 0:4:2, :], axis=AX.X, op=ADD), lam_exp)
        for k in range(KT):
            E.await_(transposed)
            E.run(v.tensor_copy(h[:, k, :], PS[:, k, :]), h_ready)
        E.await_(transposed)
        E.run(v.tensor_copy(vec[:], PS[:, 0, 0:N_VEC]))
        E.own()
        E.run(v.tensor_scalar(vec[:, FFN_POST:FFN_POST + 32], vec[:, FFN_POST:FFN_POST + 32], 0.5, None, MUL))
        E.run(v.tensor_scalar(vec[:, DIFF_G:DIFF_G + 4], vec[:, DIFF_G:DIFF_G + 4], 1.0 - LAM_INIT, None, MUL),
              vec_ready)
        E.await_(mem_squared, 3)
        E.run(v.tensor_scalar(var[:, 0:MT], lam[:, 4:6], 1.0 / D, EPS, MUL, ADD), var_ready)
        E.run(v.tensor_tensor(lam[:, 7:8], lam[:, 3:4], lam[:, 2:3], SUB))
        E.own()
        E.run(v.tensor_scalar(lam[:, 6:7], lam[:, 7:8], -LAM_INIT, None, ADD))
        E.await_(rstd_ready)
        for t in range(MT):
            E.run(v.tensor_scalar(mem_in[:, t, :], mem_in[:, t, :], rstd[:, t:t + 1], None, MUL), mem_scaled)
        E.await_(transposed)
        E.run(v.tensor_copy(memT[:].rearrange("p a b -> p (a b)"), flat(PS[:, 4:8, :])), memT_ready)

        def conv_steps():
            last = [None] * CONV_T
            for pair in range(0, CONV_T, 2):
                for w, c in ((w, pair + n) for w in range(CONV_W) for n in range(2)):
                    tap = vec[:, CONV_TAPS + CONV_T * w + c:CONV_TAPS + CONV_T * w + c + 1]
                    if w == 0:
                        E.run(v.tensor_scalar(conv[:, c, :], u[:, c, 0:SEQ], tap,
                                              vec[:, CONV_B + c:CONV_B + c + 1], MUL, ADD))
                    else:
                        dve.wait_ge(*last[c])
                        E.run(v.scalar_tensor_tensor(out=conv[:, c, :], in0=u[:, c, w:w + SEQ], scalar=tap,
                                                     in1=conv[:, c, :], op0=MUL, op1=ADD),
                              conv_ready if w == CONV_W - 1 else None)
                    last[c] = E.last
                    yield

        conv_left = conv_steps()

        def convolve(n):
            for _ in range(n):
                next(conv_left, None)

        for p in range(LOOKAHEAD):
            split(p)
        for k in range(KT):
            input_lo(k, FFN_PRE)

        mids = 0
        for n_stage, (kind, l, arg, ng, np_) in enumerate(STAGES):
            base_piece = E.piece
            stats = from_h(kind, arg)
            other = 4 * ((E.group + 1) % 2)
            if kind == "gate_up":
                def body(base, g, n, tile, with_stats=False, bank=0):
                    for kp in range(4):
                        split(base + kp + LOOKAHEAD, g)
                        if kp == 0 and with_stats:
                            input_stats(other)
                    if with_stats:
                        input_spread(other)
                    dve.wait_ge(pieces_used, base + 4 + SPLIT_SLOTS + 4 * g)
                    started = not isinstance(n, int) or n > 1
                    if started:
                        dve.wait_ge(product_ready, n - 1)
                    v.tensor_tensor(gate[:], PS[:, bank:bank + 2, :],
                                    rsb[:].unsqueeze(1).broadcast_to([P, 2, SEQ]), MUL).then_inc(gate_scaled, 1)
                    if started:
                        dve.wait_ge(mid_lo_ready, n - 1)
                    v.tensor_tensor(up[:], PS[:, bank + 2:bank + 4, :],
                                    rsb[:].unsqueeze(1).broadcast_to([P, 2, SEQ]), MUL).then_inc(up_scaled, 1)
                    dve.wait_ge(up_scaled, n).then_inc(bank_free[bank // 4], 1)
                    dve.wait_ge(mid_hi_ready, n)
                    v.tensor_tensor(mid_lo[:, tile, :], up[:], mid_hi[:, tile, :].bitcast(f32),
                                    SUB).then_inc(mid_lo_ready, 1)

                first = straight_groups(ng)
                for q in range(first):
                    body(base_piece + 4 * q, 0, mids + q + 1, slice(2 * q, 2 * q + 2), stats and q == 0,
                         4 * ((E.group + q) % 2))
                with dve.Fori(0, (ng - first) // 2) as i:
                    for q in range(2):
                        body(base_piece + 4 * (first + q), 2 * i, mids + first + q + 1 + 2 * i,
                             bass.ds(2 * (first + q) + 4 * i, 2), False, 4 * ((E.group + first + q) % 2))
                mids += ng
                E.last = (mid_lo_ready, mids)
                E.piece += 4 * ng
                E.group += ng
                continue

            if kind == "kv":
                continue
            first_bank = 4 * (E.group % 2)
            if kind == "odd_in":
                E.run(v.memset(u[:, :, 0:U0], 0.0))
            if kind == "even_in":
                E.await_(tables_ready)
                E.run(v.tensor_copy(head_sel[:], head_sel_f[:]))
                E.run(v.tensor_scalar(alibi[:], position[:], slope[:, 0:1], None, MUL))
                E.own()
            for g in range(straight(kind, ng)):
                bank = 4 * (E.group % 2)
                name = column_name(kind, g)
                for kp in range(group_pieces(kind, g, np_)):
                    split_next()
                    if stats and g == 0 and kp == 0:
                        input_stats(other)
                    if kind == "odd_in" and g >= 3:
                        convolve(5 if g < 5 else 2)
                if stats and g == 0:
                    input_spread(other)
                if kind in ("down", "mix_out", "xo"):
                    by_tile = ends_sublayer(kind, arg) and g == 1
                    if not by_tile:
                        E.group_done()
                    for c in range(4):
                        k = 4 * g + c
                        if by_tile and c < 3:
                            E.await_(y_tile_done)
                        elif by_tile:
                            E.group_done()
                        if kind == "down" and arg[1] == 1:
                            E.run(v.tensor_tensor(y[:, k, :], PS[:, bank + c, :], y[:, k, :], ADD), y_ready)
                        else:
                            E.run(v.tensor_copy(y[:, k, :], PS[:, bank + c, :]), y_ready)
                    E.release_banks()
                elif name in TOKEN_MAJOR:
                    pass
                elif name == "c_f":
                    E.group_done()
                    E.run(v.tensor_tensor(c_z[:, 0, :], PS[0:FOX_HEADS, bank, :], rsb[0:FOX_HEADS, :], MUL))
                    E.release_banks()
                    E.run(v.tensor_scalar(c_z[:, 0, :], c_z[:, 0, :], fbias[:, 0:1], None, ADD), proj_ready)
                    E.await_(softplus_ready)
                    E.run(v.scalar_tensor_tensor(out=c_z[:, 0, :], in0=c_z[:, 0, :], scalar=0.0,
                                                 in1=c_z[:, 1, :], op0=ALU.min, op1=SUB))
                    E.own()
                    E.run(v.tensor_tensor_scan(c_z[:, 2, :], ones[0:FOX_HEADS, 0:1].broadcast_to([FOX_HEADS, SEQ]),
                                               c_z[:, 0, :], 0.0, MUL, ADD))
                    E.own()
                    E.run(v.tensor_scalar(c_z[:, 0, :], c_z[:, 2, :], -8.0, None, MUL), cum_ready)
                    E.await_(cum_hi_ready)
                    E.run(v.tensor_tensor(cum_lo[:], c_z[:, 0, :], cum_hi[:].bitcast(f32), SUB), cum_lo_ready)
                else:
                    E.group_done()
                    dst = {"a_f": a_b, "a_q": a_q, "a_g": a_g, "d_g": sg, "c_q": c_q, "c_k": c_k}.get(name)
                    dst = dst[:] if dst is not None else u[:, :, U0:] if name == "d_a" else \
                        x_q[l % 2][:, 4 * g:4 * g + 4, :]
                    E.run(v.tensor_tensor(dst, PS[:, bank:bank + 4, :],
                                          rsb[:].unsqueeze(1).broadcast_to([P, 4, SEQ]), MUL), proj_ready)
                    E.release_banks()
                    if name == "a_f":
                        E.await_(softplus_ready)
                        E.run(v.scalar_tensor_tensor(out=logf[:], in0=a_b[:], scalar=0.0, in1=soft[:],
                                                     op0=ALU.min, op1=SUB))
                        E.own()
                        for hd in range(4):
                            for t in range(TT):
                                tok = slice(t * P, (t + 1) * P)
                                E.run(v.tensor_tensor_scan(a_b[:, hd, tok], ones[:], logf[:, hd, tok], 0.0, MUL, ADD))
                    if name == "d_g":
                        E.await_(sigmoid_ready)
                        E.run(v.tensor_tensor(u[:, :, U0:], u[:, :, U0:], sg[:], MUL))
                        E.own()
                E.group += 1

            if kind == "even_in":
                E.run(v.memset(scoresT[:], 0.0))
                base, done = E.piece, LOOKAHEAD
                b_bank = 4 * (E.group % 2)
                level_bank = 4 - b_bank

                def split_to(done, n):
                    for p in range(done, n):
                        split(base + p)
                    return n

                def b_group(dst, bank):
                    E.piece += 4
                    E.group_done()
                    E.run(v.tensor_tensor(dst[:], PS[:, bank:bank + 4, :],
                                          rsb[:].unsqueeze(1).broadcast_to([P, 4, SEQ]), MUL), proj_ready)
                    E.release_banks()
                    E.group += 1
                bflat = flat(a_b[:])

                def halves(t, L):
                    t = t.rearrange("p (b r j) -> p b r j", r=2, j=L)
                    return t[:, :, 0, :], t[:, :, 1, :]

                def level_sub(n):
                    L = LEVELS[n]
                    nb = 4 * SEQ // (2 * L)
                    left, right = halves(bflat, L)
                    ref = left[:, :, L - 1:L].broadcast_to([P, nb, L])
                    if n >= 2:
                        dve.wait_ge(level_scores, 2 * (n - 1))
                    dl, dr = halves(lv[:, n % 2, :], L)
                    E.run(v.tensor_tensor(dl, ref, left, SUB))
                    E.run(v.tensor_tensor(dr, right, ref, SUB), level_diff)

                def level_mul(n):
                    L = LEVELS[n]
                    E.await_(level_exp)
                    dl, dr = halves(lv[:, n % 2, :], L)
                    kl, _ = halves(flat(a_k[:]), L)
                    _, qr = halves(flat(a_q[:]), L)
                    E.run(v.tensor_tensor(dl, dl, kl, MUL))
                    E.run(v.tensor_tensor(dr, dr, qr, MUL), level_ready)

                def level_merge(n):
                    for half in range(2):
                        E.await_(level_scores)
                        if n:
                            dve.wait_ge(level_merged, 2 * n - 1 + half)
                        bank = level_bank + 2 * half
                        E.run(v.copy_predicated(scoresT[:, 8 * half:8 * half + 8, :],
                                                level_mask[:, n, :].unsqueeze(1).broadcast_to([P, 8, P]),
                                                blocks_of(bank, bank + 2)), level_merged)

                n_levels = len(LEVELS)
                level_sub(0)
                for n in range(n_levels + 1):
                    if n + 1 < n_levels:
                        level_sub(n + 1)
                    if n < n_levels:
                        level_mul(n)
                    if n >= 1:
                        level_merge(n - 1)
                    done = split_to(done, b_pieces(n) + LOOKAHEAD)
                    for m, dst in ((4, b_q), (8, b_k)):
                        if b_pieces(n) >= m > b_pieces(n - 1):
                            b_group(dst, b_bank)
                b4 = a_b[:].rearrange("p h (t j) -> p (h t) j", j=P)
                E.run(v.tensor_tensor(lv[:, 1, :].rearrange("p (t j) -> p t j", j=P),
                                      b4[:, :, P - 1:P].broadcast_to([P, 16, P]), b4, SUB), level_diff)
                level_merge(n_levels)
                done = split_to(done, 12 + LOOKAHEAD)
                E.await_(decay_ready, 3)
                E.run(v.tensor_tensor(lv[:, 0, :], lv[:, 0, :], flat(a_q[:]), MUL))
                E.run(v.tensor_tensor(lv[:, 1, :], lv[:, 1, :], flat(a_k[:]), MUL))
                E.own()
                kd = lv[:, 1, :].rearrange("p (h t j) -> p h t j", t=TT, j=P)
                E.piece += 4
                E.group_done()
                E.group += 1
                for J in range(2):
                    E.run(v.tensor_tensor(kd2[:, :, J, :], kd[:, :, J, :],
                                          tile_decay[:, :, J + 1:J + 2].broadcast_to([P, 4, P]), MUL))
                E.own()
                E.run(v.tensor_tensor(kd3[:], kd2[:, :, 0, :], tile_decay[:, :, 2:3].broadcast_to([P, 4, P]), MUL),
                      cross_ready)
                def scale_head(k, bank):
                    E.await_(spread_ready)
                    E.run(v.tensor_tensor(y[:, k, :], y[:, k, :], PS[:, bank, :], MUL), head_scaled)
                    E.own()
                    if k < 4:
                        E.run(v.scalar_tensor_tensor(out=y[:, k, :], in0=y[:, k, :],
                                                     scalar=vec[:, HGRN_G + k:HGRN_G + k + 1],
                                                     in1=a_g[:, k, :], op0=MUL, op1=MUL), y_mixed)
                    else:
                        E.run(v.tensor_scalar(y[:, k, :], y[:, k, :], vec[:, DIFF_G + k - 4:DIFF_G + k - 3],
                                              None, MUL), y_mixed)

                def meanwhile(i):
                    if i == 2:
                        E.await_(ring_summed, 4)
                        variance(PS[:, 5, 0:16], HEAD, 16)
                    if i in (8, 12):
                        E.await_(ring_summed)
                        variance(PS[:, 5, 0:TT], HEAD, TT)
                    if i - 2 in SPREAD_AT:
                        scale_head(SPREAD_AT.index(i - 2), 5)
                    if i - 1 in SPREAD_AT:
                        k = SPREAD_AT.index(i - 1)
                        if k == 0 or k >= 4:
                            E.await_(rstd_ready)
                        c = 4 * k if k < 4 else 0
                        make_diag(rstd[:, c:c + 4])
                    if i - 2 in HI_AT:
                        input_lo(HI_AT.index(i - 2))
                memory_lo(l)
                attention(16, lambda i: (i % TT + 1) * P, 0.125, True, even_probs, meanwhile, True)
                E.group_done()
                for k in range(len(HI_AT), 6):
                    input_lo(k)
                other = 4 * ((E.group + 1) % 2)
                E.await_(ring_summed, 2)
                variance(PS[:, other, 0:2 * TT], HEAD, 2 * TT)
                E.await_(rstd_ready)
                for n in range(2):
                    make_diag(rstd[:, TT * n:TT * n + TT])
                    scale_head(6 + n, other + 1 + n)
                for n in range(2):
                    input_lo(6 + n)
            if kind == "odd_in":
                E.group_done()
                memory_lo(l)
                attention(16, lambda i: (i % TT + 1) * P, 0.125, False, fox_probs, lambda i: convolve(5), True)
                E.group_done()
                for k in range(4):
                    input_lo(k)
                convolve(CONV_T * CONV_W)
                other = 4 * ((E.group + 1) % 2)
                E.await_(conv_summed)
                E.run(v.tensor_scalar(var[:, 0:TT], PS[:, other, 0:TT], 1.0 / (CONV_T * P), None, MUL))
                E.own()
                make_diag(var[:, 0:TT])
                E.await_(spread_ready)
                for c in range(CONV_T):
                    E.run(v.tensor_tensor(conv[:, c, :], conv[:, c, :], PS[:, other + 1, :], SUB), conv_centred)
                E.await_(ring_summed, 4)
                variance(PS[:, other, TT:2 * TT], CONV_T * P, TT)
                E.await_(rstd_ready)
                make_diag(rstd[:, 0:TT])
                E.await_(spread_ready)
                for c in range(CONV_T):
                    E.run(v.tensor_tensor(conv[:, c, :], conv[:, c, :], PS[:, other + 2, :], MUL), conv_scaled)
                for k in range(4, KT):
                    input_lo(k)
            if kind == "xq":
                attention(8, lambda i: MEM, 0.0625, False, x_probs[l % 2],
                          lambda i: input_lo(i - TT - 3) if i >= TT + 3 else None)
                for k in range(2, KT):
                    input_lo(k)
            if ends_sublayer(kind, arg):
                nxt = next(((k2, l2, a2) for k2, l2, a2, _, _ in STAGES[n_stage + 1:]), None)
                close_sublayer(kind, l, arg, first_bank, gain_of(*nxt) if nxt else None)
        E.seen[transposed.name] += 1
        for t in range(TT):
            E.await_(transposed)
            if t % 2:
                E.run(v.tensor_copy(out_rows[:, t, SEQ:], PS[:, 2 * t + 1, :]), odd_out_copied)

    @block.tensor
    def _(pe):
        E = Engine(pe, None)
        mm = nc.tensor.matmul

        def three(out_ap, lh, ll, rh, rl, start, stop, skip_group_check=False):
            mm(out_ap, lh, rl, start=start, stop=False, skip_group_check=skip_group_check)
            mm(out_ap, ll, rh, start=False, stop=False, skip_group_check=skip_group_check)
            return mm(out_ap, lh, rh, start=False, stop=stop, skip_group_check=skip_group_check)

        def kv_piece(l, base, i):
            g, kp = divmod(i, 2)
            weights(base + i)
            if kp == 0:
                if g:
                    E.await_(kv_copied)
                else:
                    E.seen[m_lo_ready.name] += KT
                    pe.wait_ge(m_lo_ready, E.seen[m_lo_ready.name])
            slot = (base + i) % SPLIT_SLOTS
            wh, wl = [t[:, slot].rearrange("p a (b n) -> p (a b) n", n=256) for t in (whi, wlo)]
            for j in range(4):
                k = 4 * kp + j
                for c in range(2):
                    cols = slice(c * P, (c + 1) * P)
                    w_parts = (wh[:, j, cols], wl[:, j, cols]) if g < 4 else (wh[:, j, :], wl[:, j, :])
                    m_parts = (m_hi[l % 2][:, k, :], m_lo[:, k, :]) if g < 4 else \
                        (m_hi[l % 2][:, k, cols], m_lo[:, k, cols])
                    parts = w_parts + m_parts if g < 4 else m_parts + w_parts
                    last = three(PS[:, 7, c * 256:(c + 1) * 256], *parts, k == 0 and c == 0, k == KT - 1 and c == 1,
                                 skip_group_check=True)
            last.then_inc(pieces_used, 1)

        def spread(bank):
            for t in range(TT):
                E.await_(diag_ready)
                last = mm(PS[:, bank, t * P:(t + 1) * P], ones[:], diag[:, t, :], start=True, stop=True)
            E.run(last, spread_ready)

        def column_sums(bank, c0, tile, start, stop):
            for t in range(TT):
                last = mm(PS[:, bank, c0 + t:c0 + t + 1], tile[:, t * P:(t + 1) * P], ones[:, 0:1],
                          start=start and t == 0, stop=stop and t == TT - 1, skip_group_check=True)
            return last

        def square_sums(bank, c0):
            E.await_(ring_squared)
            E.run(column_sums(bank, c0, ring[:, E.made[ring_summed.name] % 4, :], True, True), ring_summed)

        unread = [False, False]

        def wait_banks(group):
            if group >= 2:
                pe.wait_ge(bank_free[group % 2], group // 2)
            if unread[group % 2]:
                E.await_(spread_used)
                unread[group % 2] = False

        def attention(n_steps, qk, blocks, pv, buffers=fox_probs, meanwhile=None, kv_layer=None, first=None):
            probs, _ = buffers
            e0 = E.seen[exp_done.name]

            def scores(i):
                if i >= 2:
                    pe.wait_ge(exp_done, e0 + 2 * (i - 1))
                E.run(qk(i), scores_ready)
            scores(0)
            if first is not None:
                first()
            scores(1)
            if first is not None:
                E.await_(o_copied)
            c0, o0 = E.seen[probsT_copied.name], E.seen[o_copied.name]
            for i in range(n_steps):
                bl = blocks(i)
                E.await_(probs_ready, len({m for m, _ in bl}))
                if i >= 1:
                    pe.wait_ge(probsT_copied, c0 + i)
                for n, (m, kt) in enumerate(bl):
                    last = nc.tensor.transpose(blocks_of(4, 6)[:, n, :], probs[:, i % 2, m, kt * P:(kt + 1) * P],
                                               ident[:])
                E.run(last, probsT_ready)
                if i + 2 < n_steps:
                    scores(i + 2)
                if kv_layer is not None:
                    kv_piece(kv_layer, E.piece, i)
                if meanwhile is not None:
                    meanwhile(i)
                pe.wait_ge(probsT_copied, c0 + i + 1)
                n_banks = 1 if kv_layer is not None else 2
                if i >= n_banks:
                    pe.wait_ge(o_copied, o0 + i + 1 - n_banks)
                E.run(pv(i, PS[:, 6 + i % n_banks, :]), o_ready)
            if kv_layer is not None:
                E.piece += KV_PIECES
                E.await_(kv_copied)
            E.seen[exp_done.name] = e0 + 2 * n_steps
            E.seen[probsT_copied.name] = c0 + n_steps
            E.seen[o_copied.name] = o0 + n_steps
            pe.wait_ge(exp_done, e0 + 2 * n_steps)
            pe.wait_ge(o_copied, o0 + n_steps)

        def weights(base, g=0):
            pe.wait_ge(lo_made, base + 1 + RAW_SLOTS + 4 * g)

        def feature_major(slot, kp, n_kp, bank, src_hi, src_lo, k_of, n=SEQ):
            for i in range(PK):
                k = k_of(kp, i)
                for c in range(4):
                    cols = slice(c * P, (c + 1) * P)
                    last = three(PS[:, bank + c, 0:n], whi[:, slot, i, cols], wlo[:, slot, i, cols],
                                 src_hi[:, k, :], src_lo[:, k, :], kp + i == 0, kp == n_kp - 1 and i == PK - 1)
            return last

        def last_piece(slot, kp, bank, src_hi, src_lo, k_of):
            for c in range(4):
                cols = slice(c * P, (c + 1) * P)
                for i in range(PK):
                    k = k_of(kp, i)
                    last = three(PS[:, bank + c, :], whi[:, slot, i, cols], wlo[:, slot, i, cols],
                                 src_hi[:, k, :], src_lo[:, k, :], False, i == PK - 1)
                if c < 3:
                    E.run(last, y_tile_done)
            return last

        def token_major(slot, kp, n_kp, bank, src_hi, src_lo, tiles):
            for i in range(PK):
                k = 2 * kp + i
                for t in range(tiles):
                    toks = slice(t * P, (t + 1) * P)
                    last = three(PS[:, bank + t, :], src_hi[:, k, toks], src_lo[:, k, toks],
                                 whi[:, slot, i, :], wlo[:, slot, i, :], kp + i == 0,
                                 kp == n_kp - 1 and i == PK - 1)
            return last

        def forget_gates(slot, bank):
            w = [t[:, slot].rearrange("p a (b n) -> p (a b) n", n=P) for t in (whi, wlo)]
            for k in range(KT):
                last = three(PS[:, bank, :], w[0][:, k, :], w[1][:, k, :], xhi[:, k, :], xlo[:, k, :],
                             k == 0, k == KT - 1)
            return last

        T = nc.tensor.transpose
        pe.wait_ge(x_loaded, 16)
        pe.wait_ge(consts_ready, 1).then_inc(pieces_used, SPLIT_SLOTS)
        for k in range(KT):
            for t in range(TT):
                last = T(PS[:, k, t * P:(t + 1) * P], x_in[:, t, k * P:(k + 1) * P], ident[:])
            E.run(last, transposed)
        pe.wait_ge(rows_loaded, 16 * 13)
        pe.wait_ge(h_ready, 1)
        n1 = CONV_TAPS - MEM_G
        n2 = CONV_W * CONV_T
        T(PS[:, 0, 0:P], rows[:, 0, :], ident[:])
        T(PS[:, 0, P:P + n1], rows[0:n1, 1, :], ident[0:n1, 0:n1])
        E.run(T(PS[:, 0, CONV_TAPS:CONV_TAPS + n2], rows[0:n2, 2, :], ident[0:n2, 0:n2]), transposed)
        pe.wait_ge(h_ready, KT)
        E.await_(mem_scaled, MT)
        memo = PS[:, 4:8, :].rearrange("p a (b j) -> p (a b) j", j=MEM)
        for k in range(KT):
            for t in range(MT):
                last = T(memo[:, k, t * P:(t + 1) * P], mem_in[:, t, k * P:(k + 1) * P], ident[:])
        E.run(last, transposed)
        E.await_(memT_ready)

        mids = 0
        for kind, l, arg, ng, np_ in STAGES:
            stats = from_h(kind, arg)
            if kind == "kv":
                continue
            if stats or kind in ("mix_out", "xo"):
                E.seen[xlo_ready.name] += KT
            x_ready = E.seen[xlo_ready.name] - KT

            if kind == "gate_up":
                def body(base, g, group, n, with_stats=False):
                    bank = 4 * (group % 2)
                    for kp in range(4):
                        weights(base + kp, g)
                        if kp == 0:
                            pe.wait_ge(bank_free[group % 2], group // 2 + n)
                        pe.wait_ge(xlo_ready, x_ready + 2 * kp + 2)
                        slot = (base + kp) % SPLIT_SLOTS
                        feature_major(slot, kp, 4, bank, xhi, xlo, lambda a_, b_: 2 * a_ + b_).then_inc(pieces_used, 1)
                        if with_stats and kp == 2:
                            input_sums(group)
                        if with_stats and kp == 3:
                            spread(4 * ((group + 1) % 2) + 1)
                            unread[(group + 1) % 2] = True

                def input_sums(group):
                    wait_banks(group + 1)
                    E.await_(h_added, KT - 1)
                    E.run(column_sums(4 * ((group + 1) % 2), 0, y[:, 0, :], True, True), h_summed)

                first = straight_groups(ng)
                for q in range(first):
                    wait_banks(E.group + q)
                    body(E.piece + 4 * q, 0, E.group + q, 0, stats and q == 0)
                with pe.Fori(0, (ng - first) // 2) as i:
                    for q in range(2):
                        body(E.piece + 4 * (first + q), 2 * i, E.group + first + q, i)
                E.piece += 4 * ng
                E.group += ng
                continue

            if kind == "down":
                m0, mids = mids, mids + np_
            for g in range(straight(kind, ng)):
                wait_banks(E.group)
                if kind == "mix_out" and g == 1:
                    pe.wait_ge(*((head_scaled, KT) if l % 2 == 0 else (conv_scaled, CONV_T)))
                bank = 4 * (E.group % 2)
                other = 4 * ((E.group + 1) % 2)
                name = column_name(kind, g)
                n_kp = group_pieces(kind, g, np_)
                if kind == "mix_out" and l % 2 == 1 and g == 0:
                    E.await_(conv_added, CONV_T - 1)
                    E.run(column_sums(other, 0, ring[:, 0, :], True, True), conv_summed)
                for kp in range(n_kp):
                    weights(E.piece)
                    slot = E.piece % SPLIT_SLOTS
                    by_tile = ends_sublayer(kind, arg) and g == 1 and kp == n_kp - 1
                    if kind == "down":
                        pe.wait_ge(mid_lo_ready, m0 + kp + 1)
                        last = last_piece(slot, kp, bank, mid_hi, mid_lo, lambda a_, b_: 2 * a_ + b_) if by_tile else \
                            feature_major(slot, kp, n_kp, bank, mid_hi, mid_lo, lambda a_, b_: 2 * a_ + b_)
                    else:
                        pe.wait_ge(xlo_ready, x_ready + (KT if name == "c_f" else 2 * kp + 2))
                        last = last_piece(slot, kp, bank, xhi, xlo, lambda a_, b_: 2 * a_ + b_) if by_tile else \
                            forget_gates(slot, bank) if name == "c_f" else \
                            token_major(slot, kp, 4, bank, xhi, xlo, TT) if name in TOKEN_MAJOR else \
                            feature_major(slot, kp, 4, bank, xhi, xlo, lambda a_, b_: 2 * a_ + b_)
                    last.then_inc(pieces_used, 1)
                    E.piece += 1
                    if kind == "mix_out" and l % 2 == 1 and g == 0 and kp == 0:
                        spread(other + 1)
                    if kind == "mix_out" and l % 2 == 1 and g == 0 and kp == 1:
                        for c in range(CONV_T):
                            E.await_(ring_squared)
                            E.run(column_sums(other, TT, ring[:, E.made[ring_summed.name] % 4, :], c == 0,
                                              c == CONV_T - 1), ring_summed)
                        spread(other + 2)
                    if kind == "mix_out" and l % 2 == 0 and g == 0 and kp == 0:
                        for n in range(2):
                            square_sums(other, 4 * n)
                    if kind == "mix_out" and l % 2 == 0 and g == 0 and kp == 1:
                        for n in range(2):
                            spread(other + 1 + n)
                    if stats and g == 0 and kp == 2:
                        wait_banks(E.group + 1)
                        E.await_(h_added, KT - 1)
                        E.run(column_sums(other, 0, y[:, 0, :], True, True), h_summed)
                    if stats and g == 0 and kp == 3:
                        spread(other + 1)
                        unread[(E.group + 1) % 2] = True
                E.group += 1
            if ends_sublayer(kind, arg):
                E.made[ring_summed.name] += ADDED
                pe.wait_ge(ring_summed, E.made[ring_summed.name])
                column_sums(other, 0, square_sum[:], True, False)
                E.seen[ring_squared.name] += ADDED
                for k in range(ADDED, KT):
                    E.await_(ring_squared)
                    E.run(column_sums(other, 0, ring[:, E.made[ring_summed.name] % 4, :], False, k == KT - 1),
                          ring_summed)
                spread(bank + 1)
                unread[bank // 4] = True

            if kind == "even_in":
                base = E.piece
                b_bank = 4 * (E.group % 2)
                level_bank = 4 - b_bank
                wait_banks(E.group)

                def b_piece(p):
                    g, kp = divmod(p, 4)
                    if g and kp == 0:
                        wait_banks(E.group + g + 1)
                    weights(base + p)
                    slot = (base + p) % SPLIT_SLOTS
                    last = token_major(slot, kp, 4, b_bank, xhi, xlo, TT) if g == 2 else \
                        feature_major(slot, kp, 4, b_bank, xhi, xlo, lambda a_, b_: 2 * a_ + b_)
                    last.then_inc(pieces_used, 1)
                done = 0
                for n in range(len(LEVELS) + 1):
                    while done < b_pieces(n):
                        b_piece(done)
                        done += 1
                    if n == 0:
                        wait_banks(E.group + 1)
                    if n < len(LEVELS):
                        E.await_(level_ready)
                    for half in range(2):
                        if n >= 1:
                            pe.wait_ge(level_merged, 2 * n - 1 + half)
                        for b in range(8 * half, 8 * half + 8):
                            tok = slice(b * P, (b + 1) * P)
                            lhs, rhs = (lv[:, n % 2, tok],) * 2 if n < len(LEVELS) else \
                                (flat(a_k[:])[:, tok], flat(a_q[:])[:, tok])
                            last = mm(blocks_of(level_bank, level_bank + 4)[:, b, :], lhs, rhs, start=True, stop=True)
                        E.run(last, level_scores)
                while done < 12:
                    b_piece(done)
                    done += 1
                E.piece += 12
                E.group += 3
                for q in range(2):
                    wait_banks(E.group + q)
                pe.wait_ge(level_merged, 2 * (len(LEVELS) + 1))
                def between_tiles():
                    E.await_(cross_ready)
                    kd = lv[:, 1, :].rearrange("p (h t j) -> p h t j", t=TT, j=P)
                    for hd in range(4):
                        for n, (i, j) in enumerate(CROSS):
                            key = kd[:, hd, j, :] if i - j == 1 else kd2[:, hd, j, :] if i - j == 2 else kd3[:, hd, :]
                            last = mm(blocks_of(2, 8)[:, 6 * hd + n, :], key,
                                      lv[:, 0, hd * SEQ + i * P:hd * SEQ + (i + 1) * P], start=True, stop=True)
                    E.run(last, cross_scores)
                    E.await_(cross_copied)
                    for hd in range(4):
                        for i in range(TT):
                            terms = [(cross[:, 6 * hd + n, :], j) for n, (ii, j) in enumerate(CROSS) if ii == i]
                            terms.append((scoresT[:, 4 * hd + i, :], i))
                            for n, (s, j) in enumerate(terms):
                                last = mm(PS[:, 4 + hd, i * P:(i + 1) * P], a_v[:, j, hd * P:(hd + 1) * P], s,
                                          start=n == 0, stop=n == len(terms) - 1)
                    E.run(last, o_ready)

                def qk(i):
                    hd, qb = i // TT, i % TT
                    nk = (qb + 1) * P
                    for m in range(2):
                        o = PS[:, 2 * (i % 2) + m, :]
                        r = slice(64 * m, 64 * m + 64)
                        mm(o[:, 0:nk], b_q[r, hd, qb * P:nk], b_k[r, hd, 0:nk], start=True, stop=False)
                        mm(o[:, 0:nk], head_sel[0:4, hd, :], alibi[:, 0:nk], start=False, stop=False)
                        last = mm(o[:, qb * P:nk], ident_bf[:], causal_neg[:], start=False, stop=True)
                    return last

                def pv(i, o):
                    hd, qb = i // TT, i % TT
                    for kt in range(qb + 1):
                        last = mm(o[:, 0:P], b_v[:, kt, hd * P:(hd + 1) * P], even_probs[1][:, kt, :],
                                  start=kt == 0, stop=kt == qb)
                    return last

                def meanwhile(i):
                    if i == 0:
                        for t in range(4):
                            square_sums(5, 4 * t)
                    if i in (6, 10):
                        pe.wait_ge(head_scaled, 4 if i == 6 else 5)
                        square_sums(5, 0)
                    if i in SPREAD_AT:
                        k = SPREAD_AT.index(i)
                        if k:
                            pe.wait_ge(head_scaled, k)
                        spread(5)
                attention(16, qk, lambda i: [(0, kt) for kt in range(i % TT + 1)], pv, even_probs, meanwhile, l,
                          between_tiles)
            if kind == "odd_in":
                for q in range(2):
                    wait_banks(E.group + q)
                E.await_(cum_lo_ready)

                def qk(i):
                    pair, qb = i // TT, i % TT
                    nk = (qb + 1) * P
                    for m in range(2):
                        o = PS[:, 2 * (i % 2) + m, :]
                        r = slice(64 * m, 64 * m + 64)
                        sel = head_sel[:, 2 * pair + m, :]
                        mm(o[:, 0:nk], c_q[r, pair, qb * P:nk], c_k[r, pair, 0:nk], start=True, stop=False)
                        mm(o[:, 0:nk], sel, cum_lo[:, 0:nk], start=False, stop=False)
                        mm(o[:, 0:nk], sel, cum_hi[:, 0:nk], start=False, stop=False)
                        last = mm(o[:, qb * P:nk], ident_bf[:], causal_neg[:], start=False, stop=True)
                    return last

                def pv(i, o):
                    pair, qb = i // TT, i % TT
                    for m in range(2):
                        c = (2 * pair + m) * 64
                        for kt in range(qb + 1):
                            last = mm(o[64 * m:64 * m + 64, 0:P], c_v[:, kt, c:c + 64],
                                      fox_probs[1][:, m * (qb + 1) + kt, :], start=kt == 0, stop=kt == qb)
                    return last
                attention(16, qk, lambda i: [(m, kt) for m in range(2) for kt in range(i % TT + 1)], pv,
                          kv_layer=l)
            if kind == "xq":
                for q in range(2):
                    wait_banks(E.group + q)

                def qk(i):
                    pair, qb = i // TT, i % TT
                    for m in range(2):
                        for kt in range(2):
                            ft = 2 * (2 * pair + m) + kt
                            last = mm(PS[:, 2 * (i % 2) + m, 0:MEM], x_q[l % 2][:, ft, qb * P:(qb + 1) * P], x_k[l % 2][:, ft, :],
                                      start=kt == 0, stop=kt == 1)
                    return last

                def pv(i, o):
                    pair = i // TT
                    for m in range(2):
                        for half in range(2):
                            n = 2 * m + half
                            c = (4 * pair + n) * P
                            for kt in range(MT):
                                last = mm(o[:, n * P:(n + 1) * P], x_v[l % 2][:, kt, c:c + P], x_probs[l % 2][1][:, 2 * m + kt, :],
                                          start=kt == 0, stop=kt == MT - 1)
                    return last
                attention(8, qk, lambda i: [(m, kt) for m in range(2) for kt in range(MT)], pv, x_probs[l % 2])
        h0 = KT * 4 * DEPTH
        for k in range(4):
            pe.wait_ge(h_ready, h0 + k + 1)
            for t in range(TT):
                last = T(PS[:, 2 * t, k * P:(k + 1) * P], h[:, k, t * P:(t + 1) * P], ident[:])
        E.run(last, transposed)
        pe.wait_ge(h_ready, h0 + KT)
        E.await_(spread_used)
        for t in range(TT):
            for k in range(4):
                last = T(PS[:, 2 * t + 1, k * P:(k + 1) * P], h[:, 4 + k, t * P:(t + 1) * P], ident[:])
            E.run(last, transposed)

    block_ctx.__exit__(None, None, None)


INPUTS = ["x", "mem", "ffn_norm_pre", "ffn_norm_post", "ffn_w_gate", "ffn_w_up", "ffn_w_down",
          "mix_norm_pre", "mix_norm_post", "even_w_in", "even_w_out", "hgrn_norm_g", "diff_lambda",
          "diff_norm_g", "odd_w_in", "odd_w_out", "fox_f_bias", "conv_w", "conv_b", "conv_ln_g", "conv_ln_b",
          "xattn_norm_pre", "xattn_norm_post", "mem_norm_g", "xattn_w_q", "xattn_w_kv", "xattn_w_o"]


def kernel(**inputs):
    import concourse.bacc as bacc
    from concourse.bass_utils import run_bass_kernel_spmd

    nc = bacc.Bacc("TRN2", target_bir_lowering=False, num_devices=1)
    arrays, tensors = {}, {}
    for name in INPUTS:
        a = np.ascontiguousarray(inputs[name])
        arrays[name + "_dram"] = a
        tensors[name] = nc.dram_tensor(name + "_dram", a.shape, mybir.dt.from_np(a.dtype), kind="ExternalInput").ap()
    out = nc.dram_tensor("out_dram", (1, SEQ, D), mybir.dt.float32, kind="ExternalOutput").ap()
    build(nc, tensors, out)
    r = run_bass_kernel_spmd(nc, [arrays], core_ids=[0])
    return r.results[0]["out_dram"]
```
